# Optimizing a Trainium2 kernel written in Bass

```python
import math
import jax, jax.numpy as jnp
from jax import lax
import numpy as np

D_MODEL = 1024
BATCH = 1
SEQ = 1024
DEPTH = 1
DEC_BATCH = 8
DEC_SEQ = 4
PAST_LEN = 8192
PAGE_SIZE = 128

A_HEADS = 8
A_KV_HEADS = 2
A_GROUP = A_HEADS // A_KV_HEADS
A_HEAD_DIM = 64
A_WIDTH = A_HEADS * A_HEAD_DIM
A_KV_WIDTH = A_KV_HEADS * A_HEAD_DIM
WINDOW = 128
ROT_DIM = A_HEAD_DIM // 4
ROPE_THETA = 500000.0
DN_HEADS = 4
DN_HEAD_DIM = 128
DN_WIDTH = DN_HEADS * DN_HEAD_DIM
DN_CONV = 4
DN_CHUNK = 64
DT_MIN = 1e-3
DT_MAX = 1e-1
X_HEADS = 4
X_HEAD_DIM = 128
X_WIDTH = X_HEADS * X_HEAD_DIM
N_MEM = 256
D_FF = 2816
FFN_CONV = 3
EPS = 1e-6

IN_SPLITS = (A_WIDTH, A_KV_WIDTH, A_KV_WIDTH,
             DN_WIDTH, DN_WIDTH, DN_WIDTH, DN_WIDTH,
             DN_HEADS, DN_HEADS,
             D_MODEL, D_MODEL)
IN_WIDTH = sum(IN_SPLITS)

kernel_name = "hybrid_swa_gdn_xmem_convffn_step"

F32 = jnp.float32

def rmsnorm(x, g):
    xf = x.astype(F32)
    y = xf * lax.rsqrt(jnp.mean(xf * xf, axis=-1, keepdims=True) + EPS)
    return (y * g.astype(F32)).astype(x.dtype)

def l2norm(t):
    tf = t.astype(F32)
    return tf * lax.rsqrt(jnp.sum(tf * tf, axis=-1, keepdims=True) + EPS)

def split_cols(z, sizes):
    idx = [int(i) for i in np.cumsum(sizes)[:-1]]
    return jnp.split(z, idx, axis=-1)

def rope_partial(x, pos):
    half = ROT_DIM // 2
    inv = ROPE_THETA ** (-2.0 * jnp.arange(half, dtype=F32) / ROT_DIM)
    ang = pos.astype(F32)[:, None] * inv[None, :]
    cos = jnp.cos(ang)[None, :, None, :]
    sin = jnp.sin(ang)[None, :, None, :]
    xr = x[..., :ROT_DIM].astype(F32)
    x1, x2 = xr[..., :half], xr[..., half:]
    rot = jnp.concatenate([x1 * cos - x2 * sin, x2 * cos + x1 * sin], axis=-1).astype(x.dtype)
    return jnp.concatenate([rot, x[..., ROT_DIM:]], axis=-1)

def causal_dwconv(x, buf, w):
    width = w.shape[0]
    L = x.shape[1]
    xp = jnp.concatenate([buf.astype(x.dtype), x], axis=1)
    y = sum(xp[:, j:j + L] * w[j] for j in range(width))
    return y, xp[:, L:]

def window_mask(qpos, kpos):
    d = qpos[..., :, None] - kpos[..., None, :]
    return (d >= 0) & (d < WINDOW) & (kpos[..., None, :] >= 0)

def sink_attention(q, k, v, sinks, mask):
    s = jnp.einsum("bnqkgd,bnskd->bnkgqs", q, k, preferred_element_type=F32) * (A_HEAD_DIM ** -0.5)
    s = jnp.where(mask[None, :, None, None], s, -jnp.inf)
    sink = sinks.astype(F32).reshape(A_KV_HEADS, A_GROUP)[None, None, :, :, None, None]
    m = jnp.maximum(jnp.max(s, axis=-1, keepdims=True), sink)
    p = jnp.exp(s - m)
    p = p / (jnp.sum(p, axis=-1, keepdims=True) + jnp.exp(sink - m))
    return jnp.einsum("bnkgqs,bnskd->bnqkgd", p.astype(v.dtype), v)

def swa_prompt(q, k, v, sinks):
    B, L = q.shape[:2]
    nb = L // WINDOW
    qb = q.reshape(B, nb, WINDOW, A_KV_HEADS, A_GROUP, A_HEAD_DIM)

    def band(t):
        tb = t.reshape(B, nb, WINDOW, A_KV_HEADS, A_HEAD_DIM)
        prev = jnp.concatenate([jnp.zeros_like(tb[:, :1]), tb[:, :-1]], axis=1)
        return jnp.concatenate([prev, tb], axis=2)

    blk = jnp.arange(nb, dtype=jnp.int32)[:, None] * WINDOW
    qpos = blk + jnp.arange(WINDOW, dtype=jnp.int32)[None]
    kpos = blk + jnp.arange(-WINDOW, WINDOW, dtype=jnp.int32)[None]
    o = sink_attention(qb, band(k), band(v), sinks, window_mask(qpos, kpos))
    return o.reshape(B, L, A_WIDTH)

def swa_sample(q, k, v, sinks, buf_k, buf_v, pos):
    B, T = q.shape[:2]
    wb = buf_k.shape[1]
    kk = jnp.concatenate([buf_k.astype(k.dtype), k], axis=1)
    vv = jnp.concatenate([buf_v.astype(v.dtype), v], axis=1)
    qpos = pos[None]
    kpos = (pos[0] - wb + jnp.arange(wb + T, dtype=jnp.int32))[None]
    o = sink_attention(q.reshape(B, 1, T, A_KV_HEADS, A_GROUP, A_HEAD_DIM), kk[:, None], vv[:, None],
                       sinks, window_mask(qpos, kpos))
    return o.reshape(B, T, A_WIDTH), kk[:, -wb:], vv[:, -wb:]

def gated_delta(q, k, v, g, beta, S0, chunk):
    B, L, H, _ = q.shape
    dv = v.shape[-1]
    N = L // chunk

    def to_chunks(t):
        t = t.astype(F32).reshape((B, N, chunk) + t.shape[2:])
        return jnp.swapaxes(t, 2, 3)

    qc, kc, vc, gc, bc = [to_chunks(t) for t in (q, k, v, g, beta)]
    gcum = jnp.cumsum(gc, axis=-1)
    tril = jnp.tril(jnp.ones((chunk, chunk), bool))
    strict = jnp.tril(jnp.ones((chunk, chunk), bool), -1)
    decay = jnp.exp(jnp.where(tril, gcum[..., :, None] - gcum[..., None, :], -jnp.inf))
    kb = kc * bc[..., None]
    A = jnp.where(strict, jnp.einsum("bnhid,bnhjd->bnhij", kb, kc) * decay, 0.0)
    eye = jnp.eye(chunk, dtype=F32)
    rhs = jnp.concatenate([vc * bc[..., None], kb * jnp.exp(gcum)[..., None]], axis=-1)
    sol = lax.linalg.triangular_solve(A + eye, rhs, left_side=True, lower=True)
    u, w = sol[..., :dv], sol[..., dv:]
    qk = jnp.where(tril, jnp.einsum("bnhid,bnhjd->bnhij", qc, kc) * decay, 0.0)
    q_dec = qc * jnp.exp(gcum)[..., None]
    k_dec = kc * jnp.exp(gcum[..., -1:] - gcum)[..., None]
    g_last = jnp.exp(gcum[..., -1])

    def step(S, xs):
        u_i, w_i, qd_i, kd_i, qk_i, gl_i = xs
        v_new = u_i - jnp.einsum("bhck,bhkv->bhcv", w_i, S)
        o = jnp.einsum("bhck,bhkv->bhcv", qd_i, S) + jnp.einsum("bhij,bhjv->bhiv", qk_i, v_new)
        S = S * gl_i[..., None, None] + jnp.einsum("bhck,bhcv->bhkv", kd_i, v_new)
        return S, o

    xs = tuple(jnp.moveaxis(t, 1, 0) for t in (u, w, q_dec, k_dec, qk, g_last))
    S, o = lax.scan(step, S0.astype(F32), xs)
    o = jnp.swapaxes(jnp.moveaxis(o, 0, 1), 2, 3).reshape(B, L, H, dv)
    return o, S

def memory_kv(mem, g, w):
    B, M, _ = mem.shape
    mk, mv = jnp.split(rmsnorm(mem, g) @ w, 2, axis=-1)
    return mk.reshape(B, M, X_HEADS, X_HEAD_DIM), mv.reshape(B, M, X_HEADS, X_HEAD_DIM)

def trunk_layer(x, pos, mem_k, mem_v, win, dn_buf, dn_state, ffn_buf, p, chunk):
    B, L, _ = x.shape
    xn = rmsnorm(x, p["norm_mix_g"])
    aq, ak, av, dq, dk, dvv, dz, da, db, ga, gb = split_cols(xn @ p["w_in"], IN_SPLITS)
    aq = rope_partial(aq.reshape(B, L, A_HEADS, A_HEAD_DIM), pos)
    ak = rope_partial(ak.reshape(B, L, A_KV_HEADS, A_HEAD_DIM), pos)
    av = av.reshape(B, L, A_KV_HEADS, A_HEAD_DIM)
    if win is None:
        ya = swa_prompt(aq, ak, av, p["sinks"])
        wb = min(WINDOW, L)
        new_wk, new_wv = ak[:, L - wb:], av[:, L - wb:]
    else:
        ya, new_wk, new_wv = swa_sample(aq, ak, av, p["sinks"], win[0], win[1], pos)
    qkv, new_dn_buf = causal_dwconv(jnp.concatenate([dq, dk, dvv], axis=-1), dn_buf, p["dn_conv_w"])
    dq, dk, dvv = jnp.split(jax.nn.silu(qkv), 3, axis=-1)
    heads = lambda t: t.reshape(B, L, DN_HEADS, DN_HEAD_DIM)
    qh = l2norm(heads(dq)) * (DN_HEAD_DIM ** -0.5)
    kh = l2norm(heads(dk))
    g = -jnp.exp(p["dn_a_log"].astype(F32)) * jax.nn.softplus(da.astype(F32) + p["dn_dt_bias"].astype(F32))
    beta = jax.nn.sigmoid(db.astype(F32))
    o, new_S = gated_delta(qh, kh, heads(dvv), g, beta, dn_state, chunk)
    o = rmsnorm(o.astype(x.dtype), p["dn_norm_g"]) * jax.nn.silu(heads(dz))
    yb = o.reshape(B, L, DN_WIDTH)
    mix = jax.nn.sigmoid(ga) * (ya @ p["w_br_a"]) + jax.nn.sigmoid(gb) * (yb @ p["w_br_b"])
    h = x + mix @ p["w_mix_out"]
    hq = (rmsnorm(h, p["norm_x_g"]) @ p["w_xq"]).reshape(B, L, X_HEADS, X_HEAD_DIM)
    s = jnp.einsum("blhd,bmhd->bhlm", hq, mem_k.astype(hq.dtype), preferred_element_type=F32) * (X_HEAD_DIM ** -0.5)
    pr = jax.nn.softmax(s, axis=-1).astype(hq.dtype)
    xo = jnp.einsum("bhlm,bmhd->blhd", pr, mem_v.astype(hq.dtype)).reshape(B, L, X_WIDTH)
    h = h + xo @ p["w_xo"]
    u, gv = jnp.split(rmsnorm(h, p["norm_ffn_g"]) @ p["w_up"], 2, axis=-1)
    u, new_ffn_buf = causal_dwconv(u, ffn_buf, p["ffn_conv_w"])
    h = h + (jax.nn.silu(u) * gv) @ p["w_down"]
    return h, (new_wk, new_wv, new_dn_buf, new_S.astype(x.dtype), new_ffn_buf)

def setup_inputs(seed: int = 0) -> dict:
    key = jax.random.key(seed)
    ks = iter(jax.random.split(key, 40))
    nrm = lambda shape, scale=1.0: jax.random.normal(next(ks), shape, F32) * scale
    gain = lambda shape: 1.0 + 0.02 * jax.random.normal(next(ks), shape, F32)
    wb = min(WINDOW, PAST_LEN)
    u = jax.random.uniform(next(ks), (DEPTH, DN_HEADS), F32)
    dt = jnp.exp(u * (math.log(DT_MAX) - math.log(DT_MIN)) + math.log(DT_MIN))
    dn_dt_bias = dt + jnp.log(-jnp.expm1(-dt))
    dn_a_log = jnp.log(jax.random.uniform(next(ks), (DEPTH, DN_HEADS), F32, minval=1.0, maxval=16.0))
    return {
        "x_prompt": nrm((BATCH, SEQ, D_MODEL)),
        "x_sample": nrm((DEC_BATCH, DEC_SEQ, D_MODEL)),
        "mem_prompt": nrm((BATCH, N_MEM, D_MODEL)),
        "cache_win_k": nrm((DEPTH, DEC_BATCH, wb, A_KV_HEADS, A_HEAD_DIM)),
        "cache_win_v": nrm((DEPTH, DEC_BATCH, wb, A_KV_HEADS, A_HEAD_DIM)),
        "state_dn_conv": nrm((DEPTH, DEC_BATCH, DN_CONV - 1, 3 * DN_WIDTH)),
        "state_dn": nrm((DEPTH, DEC_BATCH, DN_HEADS, DN_HEAD_DIM, DN_HEAD_DIM), DN_HEAD_DIM ** -0.5),
        "cache_mem_k": nrm((DEPTH, DEC_BATCH, N_MEM, X_HEADS, X_HEAD_DIM)),
        "cache_mem_v": nrm((DEPTH, DEC_BATCH, N_MEM, X_HEADS, X_HEAD_DIM)),
        "state_ffn_conv": nrm((DEPTH, DEC_BATCH, FFN_CONV - 1, D_FF)),
        "norm_mix_g": gain((DEPTH, D_MODEL)),
        "w_in": nrm((DEPTH, D_MODEL, IN_WIDTH), D_MODEL ** -0.5),
        "dn_conv_w": nrm((DEPTH, DN_CONV, 3 * DN_WIDTH), DN_CONV ** -0.5),
        "dn_a_log": dn_a_log,
        "dn_dt_bias": dn_dt_bias,
        "dn_norm_g": gain((DEPTH, DN_HEAD_DIM)),
        "attn_sinks": nrm((DEPTH, A_HEADS), 0.5),
        "w_br_a": nrm((DEPTH, A_WIDTH, D_MODEL), A_WIDTH ** -0.5),
        "w_br_b": nrm((DEPTH, DN_WIDTH, D_MODEL), DN_WIDTH ** -0.5),
        "w_mix_out": nrm((DEPTH, D_MODEL, D_MODEL), D_MODEL ** -0.5),
        "norm_x_g": gain((DEPTH, D_MODEL)),
        "norm_mem_g": gain((DEPTH, D_MODEL)),
        "w_xq": nrm((DEPTH, D_MODEL, X_WIDTH), D_MODEL ** -0.5),
        "w_xkv": nrm((DEPTH, D_MODEL, 2 * X_WIDTH), D_MODEL ** -0.5),
        "w_xo": nrm((DEPTH, X_WIDTH, D_MODEL), X_WIDTH ** -0.5),
        "norm_ffn_g": gain((DEPTH, D_MODEL)),
        "w_up": nrm((DEPTH, D_MODEL, 2 * D_FF), D_MODEL ** -0.5),
        "ffn_conv_w": nrm((DEPTH, FFN_CONV, D_FF), FFN_CONV ** -0.5),
        "w_down": nrm((DEPTH, D_FF, D_MODEL), D_FF ** -0.5),
        "final_norm_g": gain((D_MODEL,)),
    }

def reference(x_prompt, x_sample, mem_prompt, cache_win_k, cache_win_v, state_dn_conv, state_dn,
              cache_mem_k, cache_mem_v, state_ffn_conv, norm_mix_g, w_in, dn_conv_w, dn_a_log,
              dn_dt_bias, dn_norm_g, attn_sinks, w_br_a, w_br_b, w_mix_out, norm_x_g, norm_mem_g,
              w_xq, w_xkv, w_xo, norm_ffn_g, w_up, ffn_conv_w, w_down, final_norm_g):
    Bp, Lp, _ = x_prompt.shape
    Ls = x_sample.shape[1]
    pos_p = jnp.arange(Lp, dtype=jnp.int32)
    pos_s = PAST_LEN + jnp.arange(Ls, dtype=jnp.int32)
    dt = x_prompt.dtype
    hp, hs = x_prompt, x_sample
    new_p = [[] for _ in range(5)]
    new_s = [[] for _ in range(5)]
    mem_k_list, mem_v_list = [], []
    for l in range(DEPTH):
        p = {"norm_mix_g": norm_mix_g[l], "w_in": w_in[l], "dn_conv_w": dn_conv_w[l],
             "dn_a_log": dn_a_log[l], "dn_dt_bias": dn_dt_bias[l], "dn_norm_g": dn_norm_g[l],
             "sinks": attn_sinks[l], "w_br_a": w_br_a[l], "w_br_b": w_br_b[l],
             "w_mix_out": w_mix_out[l], "norm_x_g": norm_x_g[l], "w_xq": w_xq[l], "w_xo": w_xo[l],
             "norm_ffn_g": norm_ffn_g[l], "w_up": w_up[l], "ffn_conv_w": ffn_conv_w[l],
             "w_down": w_down[l]}
        mk, mv = memory_kv(mem_prompt, norm_mem_g[l], w_xkv[l])
        hp, sp = trunk_layer(hp, pos_p, mk, mv, None,
                             jnp.zeros((Bp, DN_CONV - 1, 3 * DN_WIDTH), dt),
                             jnp.zeros((Bp, DN_HEADS, DN_HEAD_DIM, DN_HEAD_DIM), dt),
                             jnp.zeros((Bp, FFN_CONV - 1, D_FF), dt), p, min(DN_CHUNK, Lp))
        hs, ss = trunk_layer(hs, pos_s, cache_mem_k[l], cache_mem_v[l], (cache_win_k[l], cache_win_v[l]),
                             state_dn_conv[l], state_dn[l], state_ffn_conv[l], p, Ls)
        for lst, t in zip(new_p, sp):
            lst.append(t)
        for lst, t in zip(new_s, ss):
            lst.append(t)
        mem_k_list.append(mk)
        mem_v_list.append(mv)
    y_prompt = rmsnorm(hp, final_norm_g)
    y_sample = rmsnorm(hs, final_norm_g)
    p_win_k, p_win_v, p_dn_conv, p_dn_state, p_ffn_conv = [jnp.stack(t) for t in new_p]
    s_win_k, s_win_v, s_dn_conv, s_dn_state, s_ffn_conv = [jnp.stack(t) for t in new_s]
    p_mem_k = jnp.stack(mem_k_list)
    p_mem_v = jnp.stack(mem_v_list)
    return (y_prompt, y_sample, p_win_k, p_win_v, p_dn_conv, p_dn_state, p_mem_k, p_mem_v, p_ffn_conv,
            s_win_k, s_win_v, s_dn_conv, s_dn_state, s_ffn_conv)


_drawn_inputs = setup_inputs


def setup_inputs(seed=0):
    import zlib

    import numpy as np

    out = dict(_drawn_inputs(seed))
    spreads = {}
    factors = {'dn_norm_g': 8.0,
     'attn_sinks': 8.0,
     'norm_x_g': 8.0,
     'norm_mem_g': 2.76,
     'norm_ffn_g': 2.718,
     'final_norm_g': 2.931}
    for name, (base, spread) in spreads.items():
        noise = np.random.default_rng([zlib.crc32(name.encode()), seed]).standard_normal(out[name].shape)
        drawn = base * np.exp(spread * noise) if base else spread * noise
        out[name] = __import__('jax').numpy.asarray(drawn.astype(out[name].dtype))
    for name, factor in factors.items():
        out[name] = (out[name] * factor).astype(out[name].dtype)
    return out
```

```python
from contextlib import ExitStack

import concourse.bass as bass
from concourse import mybir

F32 = mybir.dt.float32
F32R = mybir.dt.float32r
ALU = mybir.AluOpType
ACT = mybir.ActivationFunctionType
AX = mybir.AxisListType

P = 128
D = 1024
KT = D // P
TP, NB, LS = 1024, 8, 4
TS = NB * LS
T = TP + TS
NCH = 3
CW = T // NCH
CH = 128
NBLK = TP // CH
HD = 64
NJ = 4
NH = 4
NM = 256
FT = 22
EPS = 1e-6
NEG = -1e30
PRE = 3 + TP + NB * 7
SLOT = KT * P

SLOTS = {}
_at = 0
for _name, _n in (("attn", 6), ("dn", 12), ("dz", 4), ("gate", 16), ("branch", 8), ("mix", 8),
                  ("xkv", 8), ("xq", 4), ("xo", 4), ("ffn", 66)):
    SLOTS[_name] = (_at, _n)
    _at += _n
NSLOTS = _at

CONST = {}
_at = 0
for _name, _n in (("ident", P), ("ones", P), ("g_mix", KT), ("g_mem", KT), ("g_x", KT), ("g_ffn", KT),
                  ("g_out", KT), ("g_dn", 1), ("sinks", 8), ("sinks_s", 2), ("a_log", NH), ("dt_bias", NH),
                  ("dn_w", 12 * 4), ("ffn_w", FT * 3), ("eps", 1), ("eps_q", 1), ("w_ab", KT * 8)):
    CONST[_name] = (_at, _n)
    _at += _n
NCONST = _at


HALF_BANKS = ((5, 6), (7, 4))
LEVELS = 7


def front_steps():
    return {"dve": ["gu", "t1", "t2", "t3", "a1", "a2", "qk", "qd", "kbe", "kd", "vb"],
            "pe": ["bc", "kk", "kq", "kt", "vt"], "act": ["ks", "vs", "eg", "dt", "dd"]}


def inverse_steps(levels):
    dve, pe = ["x1a", "x1", "p1a", "p1b", "y1a", "y1b"], ["u1a", "u1b"]
    for l in range(2, levels + 1):
        dve += [f"p{l}a", f"p{l}b"]
        pe += [f"lp{l}a", f"lp{l}b"]
        for h in "ab":
            dve += [f"y{l}{h}"] + ([f"x{l}{h}"] if l < levels else [])
            pe += [f"lz{l}{h}"] + ([f"lx{l}{h}"] if l < levels else [])
    return {"dve": dve, "pe": pe, "act": []}


STAGES = {"front": front_steps(), "inverse": inverse_steps(LEVELS),
          "state": {"dve": ["s1", "s2"], "pe": ["wt", "vn", "o", "su"], "act": ["nw", "vn", "o"]}}
SDVE_STEPS, SPE_STEPS, SACT_STEPS = [front_steps()[e] + inverse_steps(2)[e] for e in ("dve", "pe", "act")]
SDVE_STEPS += [f"{x}{h}" for h in range(NH) for x in ("vm", "sa", "sb")]
SPE_STEPS += ["wt", "vnt", "vtok", "o"] + [f"su{h}" for h in range(NH)]
SACT_STEPS += ["nw", "vnt", "vn", "o"]


def at(steps, name, c=0):
    return c * len(steps) + steps.index(name) + 1


def build(nc, d):
    ctx = ExitStack()
    with ctx:
        def sb(name, shape, dt=F32):
            return ctx.enter_context(nc.sbuf_tensor(name, shape, dt))

        def sem(name):
            return ctx.enter_context(nc.semaphore(name))

        def wait(eng, s, v):
            if not (isinstance(v, int) and v <= 0):
                eng.wait_ge(s, v)

        def pairs(eng, n, body):
            body(0, 0)
            body(1, 1)
            if n > 2:
                with eng.Fori(1, n // 2) as i:
                    body(2 * i, 0)
                    body(2 * i + 1, 1)

        def overlay(name, shape):
            with nc.sbuf_tensor(name, shape, F32) as ap:
                return ap

        H = sb("H", [P, KT, T])
        X32 = overlay("X32", [P, 2 * KT, T])
        XH = sb("XH", [P, KT, T], F32R)
        XL = sb("XL", [P, KT, T], F32R)
        RAW = sb("RAW", [P, 2, SLOT])
        WH = sb("WH", [P, 2, SLOT], F32R)
        WL = sb("WL", [P, 2, SLOT], F32R)
        YA = sb("YA", [P, NJ, T])
        DV = sb("DV", [P, NH, T])
        TMP = sb("TMP", [P, 8 * T])
        CST = sb("CST", [P, NCONST])
        A32 = overlay("A32", [P, 4, T])
        AH = sb("AH", [P, 2, T], F32R)
        AL = sb("AL", [P, 2, T], F32R)
        PS = ctx.enter_context(nc.psum_tensor("PS", [P, 8, 512], F32))

        def cst(name):
            a, n = CONST[name]
            return CST[:, a:a + n]

        def acc(g):
            return PS[:, 3 * g:3 * g + 3, 0:CW]

        def wide(ap):
            return ap.rearrange("p (c n) -> p c n", c=NCH)

        ident, ones = cst("ident"), cst("ones")
        perm = TMP[:, 8 * T - P:8 * T]

        n_sq = TMP[:, 0:2 * T].rearrange("p (b n) -> p b n", b=2)
        n_xn = TMP[:, 2 * T:4 * T].rearrange("p (b n) -> p b n", b=2)
        n_rs = TMP[:, 4 * T:5 * T]
        def carve(start):
            at = [start]

            def take(n, pat=None, **kw):
                ap = TMP[:, at[0]:at[0] + n]
                at[0] += n
                assert at[0] <= 8 * T
                return ap.rearrange(pat, **kw) if pat else ap
            return take
        take = carve(0)
        a_mask = take(2 * CH)
        a_q = take(2 * 2 * 512, "p (b g n) -> p b g n", b=2, g=2)
        a_vf = take(2 * CH, "p (b n) -> p b n", b=2)
        a_v = take(2 * CH, "p (b n) -> p b n", b=2)
        a_s = [take(8 * 256, "p (h n) -> p h n", h=8),
               H[:, 6:8, :].rearrange("p a n -> p (a n)")[:, 0:8 * 256].rearrange("p (h n) -> p h n", h=8)]
        a_pt = take(2 * 8 * CH, "p (s h n) -> p s h n", s=2, h=8)
        a_mx, a_nm, a_es, a_den = [take(2 * 8, "p (b n) -> p b n", b=2) for _ in range(4)]
        take = carve(256)
        s_s = take(2 * T, "p (g n) -> p g n", g=2)
        s_pt = take(9 * 256, "p (k g n) -> p k g n", k=9, g=2)
        s_v = take(CH)
        s_mx = take(2)
        s_nm = take(2)
        s_es = take(2)
        s_den = take(2)
        s_ktok = take(2 * CH, "p (b n) -> p b n", b=2)
        s_kc = DV[:, 0, 0:NB * CH].rearrange("p (b n) -> p b n", b=NB)
        s_vc = DV[:, 1, 0:NB * CH].rearrange("p (b n) -> p b n", b=NB)
        s_q = DV[:, 2, 0:CH]
        rope = H[:, 6:8, :]
        s_mask = DV[:, 3, :]

        take = carve(0)
        c_pre = take(2 * PRE, "p (b n) -> p b n", b=2)
        c_acc = take(2 * T, "p (b n) -> p b n", b=2)
        c_hist = take(12 * NB * 3, "p (t b n) -> p t b n", t=12, b=NB)
        c_tail = take(12 * 27, "p (t n) -> p t n", t=12)
        l_sq = c_acc
        l_rs = TMP[:, 0:2 * T].rearrange("p (b n) -> p b n", b=2)
        take = carve(0)
        bufs = [take(NH * P) for _ in range(12)]
        for spare, n_ in ((A32, 8), (RAW, 1)):
            flat = spare[:, :, :].rearrange("p a n -> p (a n)")
            bufs += [flat[:, NH * P * i:NH * P * i + NH * P] for i in range(n_)]
        bufs = [b.rearrange("p (h n) -> p h n", h=NH) for b in bufs]
        b_qd, b_a, b_qk, b_kbe, b_vb, b_kd, b_y = zip(bufs[1:8], bufs[12:19])
        b_p, b_ks, b_vs, b_x, b_s = [bufs[i] for i in (0, 8, 9, 10, 11)]
        b_nw, b_vn = bufs[19:21]
        d_mask = take(11 * P, "p (m n) -> p m n", m=11)
        m_ut, m_u, m_l, m_1l = [d_mask[:, i, :] for i in range(4)]
        m_lev = d_mask[:, 4:11, :]
        ds_mask = take(3 * TS + 3 * TS + NB)
        ms_ut, ms_u, ms_l, ms_blk = [ds_mask[:, TS * i:TS * i + TS] for i in range(4)]
        ms_b = ds_mask[:, 6 * TS:6 * TS + NB]
        S0 = H[:, 4:8, :].rearrange("p a n -> p (a n)")[:, 0:NB * NH * P].rearrange("p (b h v) -> p b h v", b=NB, h=NH)
        s_vm0 = TMP[:, 2 * 512:4 * 512]
        s_vm1 = TMP[:, 4 * 512:6 * 512]
        z_sb = TMP[:, 2 * T:4 * T].rearrange("p (b n) -> p b n", b=2)
        SM = take(640)
        sm_at = [0]

        def small(n, pat=None, **kw):
            ap = SM[:, sm_at[0]:sm_at[0] + n]
            sm_at[0] += n
            return ap.rearrange(pat, **kw) if pat else ap
        WABH, WABL = AH[:, 0, 0:KT * 8], AL[:, 0, 0:KT * 8]
        g_ab = small(9 * 8, "p (c n) -> p c n", c=9)
        g_x, g_ax, g_e, g_l, g_g, g_beta, g_eb, g_c, g_ec, g_be, g_kds, g_t = [
            small(9 * NH, "p (c h) -> p c h", c=9) for _ in range(12)]
        g_gl = small(9 * NH, "p (c h) -> p c h", c=9)
        g_egl = small(NBLK * NH, "p (c h) -> p c h", c=NBLK)
        g_egs = small(NB * NH, "p (b h) -> p b h", b=NB)
        g_bm = small(NB * NH, "p (b h) -> p b h", b=NB)
        g_ea = small(NH)

        def ga(t):
            return H[:, 4 + t, :] if t < 4 else DV[:, t - 4, :]
        gb = lambda t: TMP[:, t * T:t * T + T]
        x_res = TMP[:, :].rearrange("p (k n) -> p k n", k=KT)
        dv_flat = DV[:, :, :].rearrange("p a n -> p (a n)")
        ya_flat = YA[:, :, :].rearrange("p a n -> p (a n)")
        m_x = dv_flat[:, 0:KT * NM].rearrange("p (k n) -> p k n", k=KT)
        m_k, m_v = [dv_flat[:, 2048 + 1024 * i:3072 + 1024 * i].rearrange("p (m n) -> p m n", m=2) for i in range(2)]
        m_kT = dv_flat[:, 0:1024].rearrange("p (h n) -> p h n", h=NH)
        HQ = TMP[:, 0:4 * T].rearrange("p (h n) -> p h n", h=NH)
        take = carve(4 * T)
        x_q = take(2 * 512, "p (b h n) -> p b h n", b=2, h=NH)
        x_s = take(2 * NH * NM, "p (b h n) -> p b h n", b=2, h=NH)
        x_pt = take(2 * NH * CH, "p (m h n) -> p m h n", m=2, h=NH)
        take = carve(4 * T + 4096)
        x_nm = take(4 * NH, "p (b i h) -> p b i h", b=2, i=2)
        x_den = take(4 * NH, "p (b i h) -> p b i h", b=2, i=2)
        x_sm = take(NB)
        X_BANKS = (0, 5)
        x_ps = lambda h, p: PS[:, X_BANKS[p] + h // 2, NM * (h % 2):NM * (h % 2) + NM]
        take = carve(0)
        xs_pt = take(2 * NB * CH, "p (m n) -> p m n", m=2 * NB)
        take = carve(4 * T)
        xs_s = take(NB * NM)
        kc_buf = [ya_flat[:, 0:2048], ya_flat[:, 2048:4096]]
        vc_buf = []
        for bufs_, k in ((kc_buf, 4), (vc_buf, KT + 4)):
            flat = X32[:, k:k + 4, :].rearrange("p a n -> p (a n)")
            bufs_.extend([flat[:, 0:2048], flat[:, 2048:4096]])
        vc_buf += kc_buf[0:2]

        FPRE = 2 + TP + NB * 6
        take = carve(0)
        f_pre = take(2 * FPRE, "p (b n) -> p b n", b=2)
        f_act = take(2 * T, "p (b n) -> p b n", b=2)
        take = carve(5 * T)
        f_hist = take(FT * NB * 2, "p (t b n) -> p t b n", t=FT, b=NB)
        f_one = take(1)
        f_tail = take(FT * 18, "p (t n) -> p t n", t=FT)

        y_hi, y_lo, br_a, br_m, br_s, xres_in = [sem(x) for x in ("y_hi", "y_lo", "branch_a", "branch_mul", "branch_sum", "xres_in")]
        mem_in, kv_ok, kv_sb, mkt_ps, mkt_ok = [sem(x) for x in ("mem_in", "kv_ok", "kv_sb", "mkt_ps", "mkt_ok")]
        hq_ok = sem("hq_ok")
        xa_st, xa_sc, xa_mx, xa_exp, xa_den, xa_p, xa_tp, xa_pt, xa_pv, xa_hi, xa_lo = [
            sem("xattn_" + x) for x in ("stage", "scores", "max", "exp", "den", "probs", "ptr", "pt", "pv", "hi", "lo")]
        xs_in, xk_in, xv_in, xs_sc, xs_dv, xs_exp, xs_tp, xs_ptok, xs_pv = [
            sem("xattns_" + x) for x in ("mask_in", "k_in", "v_in", "scores", "dve", "exp", "ptr", "pt", "pv")]
        xo_a, xo_free = sem("xo_a"), sem("xo_free")
        f_in, f_z, fp_ok, fu_free, f_his, f_cv, f_silu, f_gate, f_hi, f_lo, f_down, fd_free = [
            sem("mlp_" + x) for x in ("in", "zero", "pre", "u_free", "hist", "cv", "silu", "gate", "hi", "lo", "down", "d_free")]
        y_fin = sem("y_final")
        dn_in, dm_in, s0_in = map(sem, ("dn_in", "dm_in", "s0_in"))
        c_pre_ok, c_his, c_cv, c_act = [sem("conv_" + x) for x in ("pre", "hist", "cv", "act")]
        l_sq_ok, l_ps, l_sd, l_iv, l_ok = [sem("l2_" + x) for x in ("sq", "ps", "std", "inv", "ok")]
        gt_dve, gt_act, gt_pe = [sem("gates_" + x) for x in ("dve", "act", "pe")]
        delta_sem = {(stage, e): sem(f"delta_{stage}_{e}") for stage in STAGES for e in ("dve", "act", "pe")
                     if STAGES[stage][e]}

        def delta_wait(eng, e, name, c):
            stage = [x for x in STAGES if name in STAGES[x][e]][0]
            wait(eng, delta_sem[stage, e], at(STAGES[stage][e], name, c))

        sd_dve, sd_act, sd_pe = [sem("sdelta_" + x) for x in ("dve", "act", "pe")]
        gt_dve2, s_zero = sem("gt_dve2"), sem("state_zero")
        n_attn = 16 * (2 + 1 + 1 + 16)
        n_dn_state = n_attn + 48
        n_mem = n_dn_state + 32
        z_ok, z_y = sem("z_ok"), sem("z_y")
        const_in, x_in, rope_in, smask_in, kc_in = map(sem, ("const_in", "x_in", "rope_in", "smask_in", "kc_in"))
        raw_in = [sem("raw_in0"), sem("raw_in1")]
        w_hi, w_split, w_used = sem("w_hi"), sem("w_split"), sem("w_used")
        acc_free = sem("acc_free")
        nsq, nss, nln, nrs, nxn, nhi, nlo = [sem("norm_" + x) for x in ("sq", "ss", "ln", "rs", "xn", "hi", "lo")]
        rot_ps, rot_t, rot_c, rot_x = [sem("rot_" + x) for x in ("ps", "t", "c", "x")]
        at_stage, at_sc, at_msk, at_mx, at_exp, at_es, at_den, at_p = [
            sem("swa_" + x) for x in ("stage", "scores", "masked", "max", "exp", "sinkexp", "den", "probs")]
        at_vt, at_tp, at_pt, at_pv, at_y, at_v = [sem("swa_" + x) for x in ("vtr", "ptr", "pt", "pv", "y", "v")]
        at_zero, pwv_out = sem("swa_zero"), sem("pwv_out")
        ss_q = sem("swas_q")
        ss_tr, ss_tok, ss_sc, ss_msk, ss_mx, ss_exp, ss_den, ss_p, ss_tp, ss_pt, ss_pv, ss_y = [
            sem("swas_" + x) for x in ("tr", "tok", "scores", "masked", "max", "exp", "den", "probs", "ptr", "pt",
                                       "pv", "y")]
        out_done = sem("out_done")
        n_out = [0]

        acc0 = {}
        n = 0
        for name in ("attn", "dn", "dz", "gate"):
            acc0[name] = n
            n += SLOTS[name][1]

        def norm_act(act, i, src, hi, w, src_ready):
            for k in range(KT):
                src_ready(act, k)
                wait(act, nss, 8 * i + k - 1)
                nc.scalar.activation(n_sq[:, k % 2, 0:w], src[:, k, :], ACT.Square).then_inc(nsq, 1)
            act.wait_ge(nss, 8 * i + 8)
            ps = acc(0) if w == T else PS[:, 0:1, 0:w]
            rs = wide(n_rs) if w == T else n_rs[:, 0:w].unsqueeze(1)
            nc.scalar.activation(rs, ps, ACT.Ln, scale=1.0 / D, bias=cst("eps")).then_inc(nln, 1)
            act.wait_ge(nln, i + 1)
            nc.scalar.activation(rs, rs, ACT.Exp, scale=-0.5).then_inc(nrs, 1)
            if hi is None:
                return
            for k in range(KT):
                act.wait_ge(nxn, 8 * i + k + 1)
                nc.scalar.activation(hi[:, k, 0:w], n_xn[:, k % 2, 0:w], ACT.Copy).then_inc(nhi, 1)

        def norm_pe(pe, i, w):
            for k in range(KT):
                pe.wait_ge(nsq, 8 * i + k + 1)
                for c in range(NCH if w == T else 1):
                    cw = CW if w == T else w
                    mm = nc.tensor.matmul(PS[:, c, 0:cw], ones, n_sq[:, k % 2, c * cw:(c + 1) * cw],
                                          start=(k == 0), stop=(k == KT - 1))
                mm.then_inc(nss, 1)

        def norm_dve(dve, i, src, gain, hi, lo, w):
            dve.wait_ge(nrs, i + 1)

            def rest(k):
                dve.wait_ge(nhi, 8 * i + k + 1)
                nc.vector.tensor_tensor(lo[:, k, 0:w], n_xn[:, k % 2, 0:w], hi[:, k, 0:w].bitcast(F32),
                                        ALU.subtract).then_inc(nlo, 1)
            for k in range(KT):
                if k >= 2:
                    rest(k - 2)
                    dve.wait_ge(nlo, 8 * i + k - 1)
                nc.vector.scalar_tensor_tensor(n_xn[:, k % 2, 0:w], src[:, k, :], gain[:, k:k + 1], n_rs[:, 0:w],
                                               ALU.mult, ALU.mult).then_inc(nxn, 1)
            rest(KT - 2)
            rest(KT - 1)

        def gemm_tile(mm_g, p, k0, kn, off, xk0=0, ready=None):
            for k in range(kn):
                if ready is not None:
                    nc.tensor.wait_ge(ready[0], ready[1] + xk0 + k + 1)
                for w_, x_ in ((WH, XH), (WH, XL), (WL, XH)):
                    for c in range(NCH):
                        first = k == 0 and w_ is WH and x_ is XH
                        last = k == kn - 1 and w_ is WL
                        mm = nc.tensor.matmul(PS[:, 3 * mm_g + c, 0:CW], w_[:, p, off + k * P:off + (k + 1) * P],
                                              x_[:, xk0 + k, c * CW:(c + 1) * CW], start=first, stop=last)
            return mm

        def gemm_pe(pe, name, ready=None):
            s0, n = SLOTS[name]

            def body(t, p):
                pe.wait_ge(w_split, s0 + t + 1)
                wait(pe, acc_free, acc0[name] + (t - 1 if not (isinstance(t, int) and t < 2) else 0))
                gemm_tile(p, p, 0, KT, 0, ready=ready if isinstance(t, int) and t == 0 else None).then_inc(w_used, 1)
            pairs(pe, n, body)

        def FFN0(f):
            return SLOTS["ffn"][0] + 6 * f - (0 if isinstance(f, int) and f == 0 else 2)

        acc_free2 = sem("mix_free")
        def pipelined(eng, n, front, back):
            front(0, 0)
            back(0, 0, 2)
            back(1, 1, 2)
            with eng.Fori(1, n // 2 - 1) as i:
                back(2 * i, 0, 2)
                back(2 * i + 1, 1, 2)
            back(n - 2, 0, 1)
            back(n - 1, 1, 0)

        def delta_blocks(eng, body):
            body(0, 0, False, True)
            body(1, 1, True, True)
            with eng.Fori(1, NBLK // 2 - 1) as i:
                body(2 * i, 0, True, True)
                body(2 * i + 1, 1, True, True)
            body(NBLK - 2, 0, True, True)
            body(NBLK - 1, 1, True, False)

        block = ctx.enter_context(nc.Block())


        @block.sync
        def _(sp):
            def store(dst, src):
                n_out[0] += 16
                sp.dma_start(dst, src).then_inc(out_done, 16)

            sp.dma_start(CST[:, :], d["cst"]).then_inc(const_in, 16)
            sp.dma_start(H[:, :, :], d["xT"].rearrange("k p t -> p k t")).then_inc(x_in, 16)

            def loads(a, b):
                def load(n, p):
                    wait(sp, w_split, n - 1)
                    sp.dma_start(RAW[:, p, :], d["w"][n, :, :]).then_inc(raw_in[p], 16)
                if a == 0:
                    pairs(sp, b, load)
                else:
                    with sp.Fori(a // 2, b // 2) as i:
                        load(2 * i, 0)
                        load(2 * i + 1, 1)
            loads(0, 4)
            sp.dma_start(s_kc, d["kcT"]).then_inc(kc_in, 16)
            sp.dma_start(s_vc, d["cwv"].rearrange("b s c -> s b c")).then_inc(kc_in, 16)
            sp.dma_start(s_mask, d["swas_mask"]).then_inc(smask_in, 16)
            store(d["s_win_k"][:, 0:CH - LS, :], d["cwk"][:, LS:CH, :])
            store(d["s_win_v"][:, 0:CH - LS, :], d["cwv"][:, LS:CH, :])
            sp.wait_ge(nlo, 8)
            sp.dma_start(rope, d["rope"]).then_inc(rope_in, 16)
            sp.dma_start(a_mask, d["swa_mask"]).then_inc(rope_in, 16)
            sp.dma_start(perm, d["perm"]).then_inc(rope_in, 16)
            loads(4, 8)
            sp.wait_ge(at_v, 8)
            store(d["p_win_v"], a_v[:, 1, :])
            sp.wait_ge(out_done, n_out[0])
            sp.nop().then_inc(pwv_out, 1)
            sp.wait_ge(ss_tok, 3)
            store(d["p_win_k"], s_ktok[:, 0, :])
            for b in range(NB):
                store(d["s_win_k"][b, CH - LS:CH, :], s_ktok[LS * b:LS * b + LS, 1, :])
                store(d["s_win_v"][b, CH - LS:CH, :], s_v[LS * b:LS * b + LS, :])
            sp.wait_ge(ss_y, 1)
            sp.dma_start(c_hist, d["dn_hist"]).then_inc(dn_in, 16)
            loads(8, 20)
            sp.wait_ge(c_act, 12)
            store(d["dn_tail"], c_tail)
            sp.wait_ge(out_done, n_out[0])
            sp.wait_ge(l_ok, 8)
            sp.dma_start(d_mask, d["d_mask"]).then_inc(dm_in, 16)
            sp.dma_start(ds_mask, d["ds_mask"]).then_inc(dm_in, 16)
            sp.wait_ge(sd_act, at(SACT_STEPS, "ks"))
            delta_wait(sp, "pe", "su", NBLK - 1)
            sp.dma_start(S0, d["s0"].rearrange("b h k v -> k b h v")).then_inc(s0_in, 16)
            loads(20, 22)
            delta_wait(sp, "dve", "s2", NBLK - 1)
            store(d["p_dn_state"].rearrange("h k v -> k h v"), b_s)
            sp.wait_ge(sd_dve, at(SDVE_STEPS, "sb3"))
            store(d["s_dn_state"].rearrange("b h k v -> k b h v"), S0)
            loads(22, 48)
            sp.wait_ge(br_s, 8)
            sp.dma_start(x_res, d["xT"].rearrange("k p t -> p k t")).then_inc(xres_in, 16)
            sp.wait_ge(y_lo, 16)
            sp.dma_start(m_x, d["memT"].rearrange("k p t -> p k t")).then_inc(mem_in, 16)
            loads(48, 56)
            for h in range(2):
                sp.dma_start(kc_buf[h], d["mkT"][h, :, :]).then_inc(xk_in, 16)
            loads(56, 64)
            sp.wait_ge(kv_sb, 4)
            store(d["p_mem_k"].rearrange("(m p) n -> p m n", p=P), m_k)
            store(d["p_mem_v"].rearrange("(m p) n -> p m n", p=P), m_v)
            loads(64, 68)
            sp.wait_ge(w_used, SLOTS["xq"][0] + SLOTS["xq"][1])
            sp.dma_start(x_sm, d["xs_mask"]).then_inc(xs_in, 16)
            for h in range(2, 4):
                sp.dma_start(kc_buf[h], d["mkT"][h, :, :]).then_inc(xk_in, 16)
            for h in range(4):
                if h >= 2:
                    sp.wait_ge(xs_sc, h - 1)
                sp.dma_start(vc_buf[h].rearrange("p (m n) -> p m n", n=P), d["mv"][h]).then_inc(xv_in, 16)
            loads(68, 72)
            sp.wait_ge(xa_lo, NBLK + 1)
            sp.dma_start(f_hist, d["ffn_hist"]).then_inc(f_in, 16)
            loads(72, NSLOTS)
            sp.wait_ge(fu_free, FT)
            store(d["ffn_tail"], f_tail)
            for k in range(KT):
                sp.wait_ge(y_fin, k + 1)
                store(d["yT"][k, :, :], H[:, k, :])
            sp.wait_ge(out_done, n_out[0])

        @block.gpsimd
        def _(pool):
            one = cst("ones")[:, 0:1].to_broadcast([P, SLOT])

            def split(n, p):
                pool.wait_ge(raw_in[p], 8 * (n - p) + 16)
                wait(pool, w_used, n - 1)
                nc.gpsimd.tensor_tensor(WH[:, p, :], RAW[:, p, :], one, ALU.mult).then_inc(w_hi, 1)
                pool.wait_ge(w_hi, n + 1)
                nc.gpsimd.tensor_tensor(WL[:, p, :], RAW[:, p, :], WH[:, p, :].bitcast(F32),
                                        ALU.subtract).then_inc(w_split, 1)
            pool.wait_ge(const_in, 16)
            pairs(pool, NSLOTS, split)

        @block.scalar
        def _(act):
            act.wait_ge(const_in, 16)
            norm_act(act, 0, H, XH, T, lambda e, k: e.wait_ge(x_in, 16))

            def attn_tile(t, p):
                act.wait_ge(w_used, t + 1)
                if isinstance(t, int) and t == 0:
                    act.wait_ge(nlo, 8)
                nc.scalar.activation(wide(H[:, t, :]), acc(p), ACT.Copy).then_inc(acc_free, 1)
            pairs(act, 6, attn_tile)

            def swa_front(c, p):
                wait(act, at_sc, 4 * c - 4)
                wait(act, at_vt, c - 1)
                if isinstance(c, int) and c == 0:
                    act.wait_ge(rot_x, 15)
                    act.wait_ge(at_zero, 4)
                for g in range(2):
                    rows = slice(HD * g, HD * g + HD)
                    nc.scalar.activation(a_q[rows, p, g, :].rearrange("p (j n) -> p j n", j=NJ),
                                         H[rows, 0:NJ, bass.ts(c, CH)], ACT.Copy).then_inc(at_stage, 1)
                nc.scalar.activation(a_vf[:, p, :], H[:, 5, bass.ts(c, CH)], ACT.Copy).then_inc(at_stage, 1)

            def swa_out(c):
                act.wait_ge(at_pv, c + 1)
                nc.scalar.activation(YA[:, :, bass.ts(c, CH)], PS[:, 6, :].rearrange("p (j n) -> p j n", j=NJ),
                                     ACT.Copy).then_inc(at_y, 1)

            def swa_back(c, p, left):
                act.wait_ge(at_mx, 4 * c + 4)
                for h in range(8):
                    nc.scalar.activation(a_s[p][:, h, :], a_s[p][:, h, :], ACT.Exp, bias=a_nm[:, p, h:h + 1],
                                         accum_out=a_den[:, p, h:h + 1]).then_inc(at_exp, 1)
                nc.scalar.activation(a_es[:, p, :], a_es[:, p, :], ACT.Exp).then_inc(at_exp, 1)
                if not (isinstance(c, int) and c == 0):
                    swa_out(c - 1)
                act.wait_ge(at_vt, c + 1)
                nc.scalar.activation(a_v[:, p, :], PS[:, 7, 0:CH], ACT.Copy).then_inc(at_v, 1)
                if left == 2:
                    swa_front(c + 2, p)
                for b in range(4):
                    act.wait_ge(at_tp, 4 * c + b + 1)
                    nc.scalar.activation(a_pt[:, b // 2, 4 * (b % 2):4 * (b % 2) + 4, :],
                                         PS[:, 4 + b % 2, :].rearrange("p (h n) -> p h n", h=4),
                                         ACT.Copy).then_inc(at_pt, 1)
            swa_front(0, 0)
            pipelined(act, NBLK, lambda c, p: swa_front(1, 1), swa_back)
            swa_out(NBLK - 1)

            nc.scalar.activation(s_q.rearrange("p (j n) -> p j n", j=NJ), H[:, 0:NJ, TP:T], ACT.Copy).then_inc(ss_q, 1)
            act.wait_ge(ss_tr, 1)
            act.wait_ge(pwv_out, 1)
            nc.scalar.activation(s_ktok[:, 0, :], PS[:, 6, 0:CH], ACT.Copy).then_inc(ss_tok, 1)
            nc.scalar.activation(s_ktok[0:TS, 1, :], PS[0:TS, 6, CH:2 * CH], ACT.Copy).then_inc(ss_tok, 1)
            nc.scalar.activation(s_v[0:TS, :], PS[0:TS, 6, 2 * CH:3 * CH], ACT.Copy).then_inc(ss_tok, 1)
            act.wait_ge(ss_mx, 4)
            for g in range(2):
                nc.scalar.activation(s_s[:, g, :], s_s[:, g, :], ACT.Exp, bias=s_nm[:, g:g + 1],
                                     accum_out=s_den[:, g:g + 1]).then_inc(ss_exp, 1)
            nc.scalar.activation(s_es, s_es, ACT.Exp).then_inc(ss_exp, 1)
            for b in range(4):
                act.wait_ge(ss_tp, b + 1)
                nc.scalar.activation(s_pt[:, 2 * b:2 * b + 2, :, :],
                                     PS[:, b, :].rearrange("p (k g n) -> p k g n", k=2, g=2),
                                     ACT.Copy).then_inc(ss_pt, 1)
            act.wait_ge(ss_tp, 5)
            nc.scalar.activation(s_pt[0:TS, 8, :, :], PS[0:TS, 4, 0:256].rearrange("p (g n) -> p g n", g=2),
                                 ACT.Copy).then_inc(ss_pt, 1)
            act.wait_ge(ss_pv, 1)
            nc.scalar.activation(YA[:, :, TP:T], PS[:, 5, 0:CH].rearrange("p (j n) -> p j n", j=NJ),
                                 ACT.Copy).then_inc(ss_y, 1)

            def pre(t, p):
                act.wait_ge(w_used, SLOTS["dn"][0] + t + 1)
                wait(act, c_cv, 8 * (t - 1))
                if isinstance(t, int) and t == 0:
                    act.wait_ge(ss_pv, 1)
                a = acc(p)
                nc.scalar.activation(c_tail[:, t, 0:3], a[:, 2, TP - 2 * CW - 3:TP - 2 * CW], ACT.Copy).then_inc(c_pre_ok, 1)
                new = a[:, 2, TP - 2 * CW:CW].rearrange("p (b n) -> p b n", b=NB)
                nc.scalar.activation(c_tail[:, t, 3:27].rearrange("p (b n) -> p b n", b=NB), new[:, :, 1:4],
                                     ACT.Copy).then_inc(c_pre_ok, 1)
                nc.scalar.activation(c_pre[:, p, 3:3 + 2 * CW].rearrange("p (c n) -> p c n", c=2), a[:, 0:2, :],
                                     ACT.Copy).then_inc(c_pre_ok, 1)
                nc.scalar.activation(c_pre[:, p, 3 + 2 * CW:3 + TP], a[:, 2, 0:TP - 2 * CW], ACT.Copy).then_inc(c_pre_ok, 1)
                nc.scalar.activation(c_pre[:, p, 3 + TP:PRE].rearrange("p (b n) -> p b n", b=NB)[:, :, 3:7], new,
                                     ACT.Copy).then_inc(acc_free, 1)

            def silu(dst, t, p):
                act.wait_ge(c_cv, 8 * t + 8)
                nc.scalar.activation(dst, c_acc[:, p, :], ACT.Silu).then_inc(c_act, 1)
            pre(0, 0)
            pre(1, 1)
            with act.Fori(0, 3) as i:
                silu(H[:, 2 * i, :], 2 * i, 0)
                pre(2 * i + 2, 0)
                silu(H[:, 2 * i + 1, :], 2 * i + 1, 1)
                pre(2 * i + 3, 1)
            for t in range(6, 12):
                silu(H[:, t, :] if t < 8 else DV[:, t - 8, :], t, t % 2)
                if t + 2 < 12:
                    pre(t + 2, t % 2)

            def rows_norm(i0, n, src, scale, bias):
                def sq(t):
                    wait(act, l_ps, i0 + t - 1)
                    nc.scalar.activation(l_sq[:, t % 2, :], src(t), ACT.Square).then_inc(l_sq_ok, 1)
                sq(0)
                for t in range(n):
                    if t + 1 < n:
                        sq(t + 1)
                    act.wait_ge(l_ps, i0 + t + 1)
                    wait(act, l_ok, i0 + t - 1)
                    nc.scalar.activation(wide(l_rs[:, t % 2, :]), acc(t % 2), ACT.Ln, scale=scale(t),
                                         bias=bias(t)).then_inc(l_sd, 1)
                    act.wait_ge(l_sd, i0 + t + 1)
                    nc.scalar.activation(l_rs[:, t % 2, :], l_rs[:, t % 2, :], ACT.Exp, scale=-0.5).then_inc(l_iv, 1)
            act.wait_ge(c_act, 12)
            act.wait_ge(out_done, n_attn + 16)
            rows_norm(0, 8, lambda t: H[:, t, :], lambda t: float(P) if t < 4 else 1.0,
                      lambda t: cst("eps_q") if t < 4 else cst("eps"))

            act.wait_ge(gt_pe, 1)
            act.wait_ge(gt_dve, 1)
            nc.scalar.activation(g_ab[:, 0:NBLK, :], PS[:, 6, 0:64].rearrange("p (c n) -> p c n", c=NBLK), ACT.Copy).then_inc(gt_act, 1)
            nc.scalar.activation(g_ab[0:TS, NBLK, :], PS[0:TS, 6, 64:72], ACT.Copy).then_inc(gt_act, 1)
            act.wait_ge(gt_dve, 6)
            nc.scalar.activation(g_e, g_ax, ACT.Exp, scale=-1.0).then_inc(gt_act, 1)
            nc.scalar.activation(g_eb, g_ab[:, :, 4:8], ACT.Exp, scale=-1.0).then_inc(gt_act, 1)
            nc.scalar.activation(g_ea, cst("a_log"), ACT.Exp).then_inc(gt_act, 1)
            act.wait_ge(gt_act, 3)
            nc.scalar.activation(g_l, g_e, ACT.Ln, bias=1.0).then_inc(gt_act, 1)
            act.wait_ge(gt_pe, 2)
            nc.scalar.activation(g_c[:, 0:NBLK, :], PS[:, 6, 128:160].rearrange("p (c h) -> p c h", c=NBLK), ACT.Copy).then_inc(gt_act, 1)
            nc.scalar.activation(g_c[0:TS, NBLK, :], PS[0:TS, 6, 160:164], ACT.Copy).then_inc(gt_act, 1)
            nc.scalar.activation(g_gl[:, 0:NBLK, :], PS[:, 6, 192:224].rearrange("p (c h) -> p c h", c=NBLK), ACT.Copy).then_inc(gt_act, 1)
            nc.scalar.activation(g_gl[0:TS, NBLK, :], PS[0:TS, 6, 224:228], ACT.Copy).then_inc(gt_act, 1)
            nc.scalar.activation(g_egl, PS[:, 6, 192:224].rearrange("p (c h) -> p c h", c=NBLK), ACT.Exp).then_inc(gt_act, 1)
            nc.scalar.activation(g_egs, PS[:, 6, 256:288].rearrange("p (b h) -> p b h", b=NB), ACT.Exp).then_inc(gt_act, 1)
            act.wait_ge(gt_dve, 13)
            act.wait_ge(gt_act, 12)
            nc.scalar.activation(g_ec, g_c, ACT.Exp).then_inc(gt_act, 1)
            nc.scalar.activation(g_kds, g_kds, ACT.Exp).then_inc(gt_act, 1)

            def dv(name, c): delta_wait(act, "dve", name, c)
            def pw(name, c): delta_wait(act, "pe", name, c)
            def done(stage, i): i.then_inc(delta_sem[stage, "act"], 1)
            heads = lambda bank: PS[:, bank, :].rearrange("p (h n) -> p h n", h=NH)

            def front_stage(c):
                first = isinstance(c, int) and c == 0
                if not first:
                    pw("kt", c - 1)
                    pw("vt", c - 1)
                done("front", nc.scalar.activation(b_ks, H[:, 4:8, bass.ts(c, CH)], ACT.Copy))
                done("front", nc.scalar.activation(b_vs, DV[:, :, bass.ts(c, CH)], ACT.Copy))

            def front_decays(c, p):
                pw("bc", c)
                dv("t1", c)
                done("front", nc.scalar.activation(b_qd[p], heads(0), ACT.Exp))
                dv("t2", c)
                done("front", nc.scalar.activation(b_qk[p], b_qk[p], ACT.Exp))
                dv("t3", c)
                done("front", nc.scalar.activation(b_a[p], b_a[p], ACT.Exp))

            def state(c):
                pw("wt", c)
                done("state", nc.scalar.activation(b_nw, heads(0), ACT.Copy, scale=-1.0))
                pw("vn", c)
                done("state", nc.scalar.activation(b_vn, heads(1), ACT.Copy))
                pw("o", c)
                done("state", nc.scalar.activation(H[:, 0:4, bass.ts(c, CH)], heads(2), ACT.Copy))

            def delta(c, p, before, after):
                if after:
                    front_stage(c + 1)
                if before:
                    state(c - 1)
                if after:
                    front_decays(c + 1, 1 - p)
            act.wait_ge(l_ok, 8)
            act.wait_ge(gt_dve, 15)
            act.wait_ge(w_split, SLOTS["dz"][0] + 2)
            front_stage(0)
            front_decays(0, 0)
            delta_blocks(act, delta)
            state(NBLK - 1)

            def sdone(i): i.then_inc(sd_act, 1)
            r, tn = slice(0, TS), slice(TP, T)
            sb4 = lambda b: b[:, :, 0:TS]
            pw("su", NBLK - 1)
            act.wait_ge(gt_dve, 15)
            sdone(nc.scalar.activation(sb4(b_ks), H[:, 4:8, tn], ACT.Copy))
            sdone(nc.scalar.activation(sb4(b_vs), DV[:, :, tn], ACT.Copy))
            act.wait_ge(sd_dve, at(SDVE_STEPS, "t1"))
            sdone(nc.scalar.activation(sb4(b_qd[0]), PS[:, 0, 0:P].rearrange("p (h n) -> p h n", h=NH), ACT.Exp))
            act.wait_ge(sd_dve, at(SDVE_STEPS, "t3"))
            sdone(nc.scalar.activation(b_qk[0][r, :, r], b_qk[0][r, :, r], ACT.Exp))
            sdone(nc.scalar.activation(b_a[0][r, :, r], b_a[0][r, :, r], ACT.Exp))
            act.wait_ge(sd_pe, at(SPE_STEPS, "wt"))
            sdone(nc.scalar.activation(sb4(b_ks), PS[:, 0, 0:P].rearrange("p (h n) -> p h n", h=NH), ACT.Copy, scale=-1.0))
            act.wait_ge(sd_pe, at(SPE_STEPS, "vnt"))
            sdone(nc.scalar.activation(sb4(b_vs), PS[:, 1, 0:P].rearrange("p (h n) -> p h n", h=NH), ACT.Copy))
            act.wait_ge(sd_pe, at(SPE_STEPS, "vtok"))
            sdone(nc.scalar.activation(b_x[r, :, :], PS[r, 4, :].rearrange("p (h n) -> p h n", h=NH), ACT.Copy))
            act.wait_ge(sd_pe, at(SPE_STEPS, "o"))
            sdone(nc.scalar.activation(H[:, 0:4, tn], PS[:, 2, 0:P].rearrange("p (h n) -> p h n", h=NH), ACT.Copy))

            act.wait_ge(sd_act, len(SACT_STEPS))
            act.wait_ge(sd_pe, len(SPE_STEPS))
            act.wait_ge(sd_dve, len(SDVE_STEPS))
            act.wait_ge(out_done, n_dn_state)
            rows_norm(8, 4, lambda t: H[:, t, :], lambda t: 1.0 / P, lambda t: cst("eps"))
            for t in range(4):
                act.wait_ge(w_used, SLOTS["dz"][0] + t + 1)
                wait(act, z_y, t - 1)
                nc.scalar.activation(wide(z_sb[:, t % 2, :]), acc(t % 2), ACT.Silu).then_inc(acc_free, 1)

            def gates(t0, n, dst):
                def gate(t, p):
                    act.wait_ge(w_used, SLOTS["gate"][0] + t0 + t + 1)
                    nc.scalar.activation(wide(dst(t)), acc(p), ACT.Sigmoid).then_inc(acc_free, 1)
                pairs(act, n, gate)
            act.wait_ge(z_y, 4)
            act.wait_ge(out_done, n_dn_state)
            gates(0, 4, lambda t: H[:, 4 + t, :])
            gates(4, 4, lambda t: DV[:, t, :])
            gates(8, 8, lambda t: x_res[:, t, :])

            def split_heads(src, base):
                for k in range(KT):
                    nc.scalar.activation(XH[:, k, :], src(k), ACT.Copy).then_inc(y_hi, 1)
            split_heads(lambda k: YA[:, k, :] if k < 4 else H[:, k - 4, :], 0)
            act.wait_ge(w_used, SLOTS["branch"][0] + 8)
            act.wait_ge(br_s, 8)
            split_heads(ga, 8)

            act.wait_ge(y_lo, 16)
            act.wait_ge(acc_free2, 8)
            norm_act(act, 1, m_x, XH, NM, lambda e, k: e.wait_ge(mem_in, 16))
            for n, m in enumerate((m_k, m_v)):
                act.wait_ge(w_used, SLOTS["xkv"][0] + 4 * n + 4)
                for i in range(2):
                    nc.scalar.activation(m[:, i, :], PS[:, 2 * n + i, :], ACT.Copy).then_inc(kv_sb, 1)
            act.wait_ge(mkt_ps, 1)
            act.wait_ge(nlo, 16)
            for i in range(2):
                nc.scalar.activation(m_kT[:, :, CH * i:CH * i + CH], PS[:, 4 + i, :].rearrange("p (h n) -> p h n", h=NH),
                                     ACT.Copy).then_inc(mkt_ok, 1)
            act.wait_ge(mkt_ok, 2)
            norm_act(act, 2, H, XH, T, lambda e, k: None)
            for t in range(4):
                act.wait_ge(w_used, SLOTS["xq"][0] + t + 1)
                if t == 0:
                    act.wait_ge(nlo, 24)
                nc.scalar.activation(wide(HQ[:, t, :]), acc(t % 2), ACT.Copy).then_inc(hq_ok, 1)
            act.wait_ge(hq_ok, 4)
            xscale = float(P) ** -0.5

            def xattn_stage(c, p):
                nc.scalar.activation(x_q[:, p, :, :], HQ[:, :, bass.ts(c, CH)], ACT.Copy).then_inc(xa_st, 1)

            def xattn_out(c):
                act.wait_ge(xa_pv, c + 1)
                nc.scalar.activation(XH[:, 0:4, bass.ts(c, CH)], PS[:, 4, :].rearrange("p (h n) -> p h n", h=NH),
                                     ACT.Copy).then_inc(xa_hi, 1)

            def xattn_back(c, p, left):
                act.wait_ge(xa_mx, 4 * c + 4)
                wait(act, xa_tp, 2 * (c - 1))
                wait(act, xa_den, c - 1)
                for h in range(NH):
                    nc.scalar.activation(x_s[:, p, h, :], x_ps(h, p), ACT.Exp, scale=xscale,
                                         bias=x_nm[:, p, 1, h:h + 1], accum_out=x_den[:, p, 0, h:h + 1]).then_inc(xa_exp, 1)
                if not (isinstance(c, int) and c == 0):
                    xattn_out(c - 1)
                if left == 2:
                    xattn_stage(c + 2, p)
                for i in range(2):
                    act.wait_ge(xa_tp, 2 * c + i + 1)
                    nc.scalar.activation(x_pt[:, i, :, :], PS[:, 2 + i, :].rearrange("p (h n) -> p h n", h=NH), ACT.Copy).then_inc(xa_pt, 1)
            xattn_stage(0, 0)
            pipelined(act, NBLK, lambda c, p: xattn_stage(1, 1), xattn_back)
            xattn_out(NBLK - 1)
            act.wait_ge(xs_dv, 3)
            nc.scalar.activation(xs_s, xs_s, ACT.Exp, scale=xscale, bias=x_nm[:, 0, 1, 0:1],
                                 accum_out=x_den[:, 0, 0, 0:1]).then_inc(xs_exp, 1)
            for q in range(4):
                act.wait_ge(xs_tp, q + 1)
                if q == 0:
                    act.wait_ge(xs_sc, 4)
                nc.scalar.activation(xs_pt[:, 4 * q:4 * q + 4, :], PS[:, 4 + q % 2, :].rearrange("p (m n) -> p m n", m=4),
                                     ACT.Copy).then_inc(xs_ptok, 1)
            act.wait_ge(xs_pv, 1)
            nc.scalar.activation(XH[:, 0:4, TP:T], PS[:, 6, 0:P].rearrange("p (h n) -> p h n", h=NH), ACT.Copy).then_inc(xa_hi, 1)

            act.wait_ge(xo_free, 8)
            norm_act(act, 3, H, XH, T, lambda e, k: None)
            act.wait_ge(nlo, 32)
            act.wait_ge(f_z, 1)

            def mlp_u(f, i):
                t = 2 * f + i
                act.wait_ge(w_used, FFN0(f) + i + 1)
                wait(act, f_cv, 6 * t - 6)
                a = acc(i)
                k = TP - 2 * CW
                new = a[:, 2, k:CW].rearrange("p (b n) -> p b n", b=NB)
                nc.scalar.activation(f_tail[:, t, 0:2], a[:, 2, k - 2:k], ACT.Copy).then_inc(fp_ok, 1)
                nc.scalar.activation(f_tail[:, t, 2:18].rearrange("p (b n) -> p b n", b=NB), new[:, :, 2:4], ACT.Copy).then_inc(fp_ok, 1)
                nc.scalar.activation(f_pre[:, i, 2:2 + 2 * CW].rearrange("p (c n) -> p c n", c=2), a[:, 0:2, :], ACT.Copy).then_inc(fp_ok, 1)
                nc.scalar.activation(f_pre[:, i, 2 + 2 * CW:2 + TP], a[:, 2, 0:k], ACT.Copy).then_inc(fp_ok, 1)
                nc.scalar.activation(f_pre[:, i, 2 + TP:FPRE].rearrange("p (b n) -> p b n", b=NB)[:, :, 2:6], new,
                                     ACT.Copy).then_inc(fu_free, 1)

            def mlp_act(f):
                for i in range(2):
                    mlp_u(f, i)
                for i in range(2):
                    act.wait_ge(f_cv, 12 * f + 6 * i + 6)
                    nc.scalar.activation(f_act[:, i, :], f_act[:, i, :], ACT.Silu).then_inc(f_silu, 1)
                for i in range(2):
                    act.wait_ge(f_gate, 2 * f + i + 1)
                    if i == 0 and not (isinstance(f, int) and f == 0):
                        act.wait_ge(w_used, FFN0(f) + 6)
                    nc.scalar.activation(AH[:, i, :], f_act[:, i, :], ACT.Copy).then_inc(f_hi, 1)
            mlp_act(0)
            with act.Fori(1, FT // 2) as f:
                mlp_act(f)
            act.wait_ge(fd_free, 4 * FT + 1)
            norm_act(act, 4, H, None, T, lambda e, k: None)

        @block.tensor
        def _(pe):
            pe.wait_ge(const_in, 16)
            norm_pe(pe, 0, T)
            pe.wait_ge(nln, 1)
            gemm_pe(pe, "attn", (nlo, 0))
            pe.wait_ge(acc_free, 6)
            pe.wait_ge(rope_in, 48)
            for t in range(5):
                wait(pe, rot_t, t - 1)
                for c in range(NCH):
                    mm = nc.tensor.matmul(PS[:, 3 * (t % 2) + c, 0:CW], perm, H[:, t, bass.ts(c, CW)],
                                          start=True, stop=True)
                mm.then_inc(rot_ps, 1)

            def swa_front(c, p):
                pe.wait_ge(at_stage, 3 * c + 3)
                if isinstance(c, int) and c == 0:
                    pe.wait_ge(rot_t, 5)
                for b in range(4):
                    wait(pe, at_msk, 4 * (c - 1) + b + 1)
                    for h in (2 * b, 2 * b + 1):
                        q = a_q[:, p, h // 4, (h % 4) * CH:(h % 4) * CH + CH]
                        o = (h % 2) * 2 * CH
                        if isinstance(c, int) and c == 0:
                            mm = nc.tensor.matmul(PS[:, b, o + CH:o + 2 * CH], q, H[:, 4, 0:CH], start=True, stop=True)
                        else:
                            mm = nc.tensor.matmul(PS[:, b, o:o + 2 * CH], q, H[:, 4, bass.ds((c - 1) * CH, 2 * CH)],
                                                  start=True, stop=True)
                    mm.then_inc(at_sc, 1)
                wait(pe, at_v, c)
                nc.tensor.transpose(PS[:, 7, 0:CH], a_vf[:, p, :], ident).then_inc(at_vt, 1)

            def swa_back(c, p, left):
                if left:
                    swa_front(c + 1, 1 - p)
                pe.wait_ge(at_p, c + 1)
                for b in range(4):
                    wait(pe, at_pt, 4 * c + b - 1)
                    for i in range(4):
                        s, h = (4 * b + i) // 8, (4 * b + i) % 8
                        mm = nc.tensor.transpose(PS[:, 4 + b % 2, i * CH:i * CH + CH], a_s[p][:, h, s * CH:s * CH + CH], ident)
                    mm.then_inc(at_tp, 1)
                pe.wait_ge(at_pt, 4 * c + 4)
                pe.wait_ge(at_v, c + 1)
                wait(pe, at_y, c)
                for g in range(2):
                    for s in range(2):
                        mm = nc.tensor.matmul(PS[HD * g:HD * g + HD, 6, :], a_v[:, (1 - p, p)[s], HD * g:HD * g + HD],
                                              a_pt[:, s, 4 * g:4 * g + 4, :], start=(s == 0), stop=(s == 1))
                mm.then_inc(at_pv, 1)
            pipelined(pe, NBLK, swa_front, swa_back)

            pe.wait_ge(at_y, NBLK)
            nc.tensor.transpose(PS[:, 6, 0:CH], H[:, 4, TP - CH:TP], ident)
            nc.tensor.transpose(PS[0:TS, 6, CH:2 * CH], H[:, 4, TP:T], ident)
            nc.tensor.transpose(PS[0:TS, 6, 2 * CH:3 * CH], H[:, 5, TP:T], ident).then_inc(ss_tr, 1)
            pe.wait_ge(kc_in, 32)
            pe.wait_ge(ss_q, 1)
            for g in range(2):
                rows = slice(HD * g, HD * g + HD)
                q = s_q[rows, :]
                nc.tensor.matmul(PS[:, 3 * g, :], q, s_kc[rows, 0:4, :], start=True, stop=True)
                nc.tensor.matmul(PS[:, 3 * g + 1, :], q, s_kc[rows, 4:8, :], start=True, stop=True)
                nc.tensor.matmul(PS[:, 3 * g + 2, 0:TS], q, H[rows, 4, TP:T], start=True, stop=True).then_inc(ss_sc, 1)
            pe.wait_ge(ss_p, 1)
            for k in range(NB + 1):
                rows = CH if k < NB else TS
                for g in range(2):
                    i = 2 * k + g
                    mm = nc.tensor.transpose(PS[0:rows, i // 4, (i % 4) * CH:(i % 4) * CH + CH],
                                             s_s[:, g, k * CH:k * CH + rows], ident)
                if k % 2 or k == NB:
                    mm.then_inc(ss_tp, 1)
            pe.wait_ge(ss_pt, 5)
            for g in range(2):
                for k in range(NB):
                    nc.tensor.matmul(PS[HD * g:HD * g + HD, 5, 0:CH], s_vc[:, k, HD * g:HD * g + HD], s_pt[:, k, g, :],
                                     start=(k == 0), stop=False)
                mm = nc.tensor.matmul(PS[HD * g:HD * g + HD, 5, 0:CH], s_v[0:TS, HD * g:HD * g + HD],
                                      s_pt[0:TS, NB, g, :], start=False, stop=True)
            mm.then_inc(ss_pv, 1)

            pe.wait_ge(ss_y, 1)
            pe.wait_ge(ss_pt, 5)
            gemm_pe(pe, "dn")
            pe.wait_ge(gt_dve, 3)
            for c in range(NBLK):
                for k in range(KT):
                    for n, (x_, w_) in enumerate(((XH, WABH), (XL, WABH), (XH, WABL))):
                        nc.tensor.matmul(PS[:, 6, 8 * c:8 * c + 8], x_[:, k, bass.ts(c, CH)], w_[:, 8 * k:8 * k + 8],
                                         start=(k == 0 and n == 0), stop=(k == KT - 1 and n == 2))
            for k in range(KT):
                for n, (x_, w_) in enumerate(((XH, WABH), (XL, WABH), (XH, WABL))):
                    mm = nc.tensor.matmul(PS[0:TS, 6, 64:72], x_[:, k, TP:T].bitcast(F32), w_[:, 8 * k:8 * k + 8].bitcast(F32),
                                          start=(k == 0 and n == 0), stop=(k == KT - 1 and n == 2))
            mm.then_inc(gt_pe, 1)

            def rows_norm(i0, n):
                for t in range(n):
                    pe.wait_ge(l_sq_ok, i0 + t + 1)
                    wait(pe, l_sd, i0 + t - 1)
                    for c in range(NCH):
                        mm = nc.tensor.matmul(PS[:, 3 * (t % 2) + c, 0:CW], ones, l_sq[:, t % 2, bass.ts(c, CW)],
                                              start=True, stop=True)
                    mm.then_inc(l_ps, 1)
            rows_norm(0, 8)
            pe.wait_ge(dm_in, 32)
            pe.wait_ge(gt_dve, 12)
            gp = g_g[:, 0:NBLK, :].rearrange("p c h -> p (c h)")
            nc.tensor.matmul(PS[:, 6, 128:160], m_ut, gp, start=True, stop=True)
            nc.tensor.matmul(PS[0:TS, 6, 160:164], ms_ut[0:TS, :], g_g[0:TS, NBLK, :], start=True, stop=True)
            nc.tensor.matmul(PS[:, 6, 192:224], ones, gp, start=True, stop=True)
            nc.tensor.matmul(PS[0:TS, 6, 224:228], ms_blk[0:TS, :], g_g[0:TS, NBLK, :], start=True, stop=True)
            nc.tensor.matmul(PS[:, 6, 256:288], ones[0:TS, :], g_bm[0:TS, :, :].rearrange("p b h -> p (b h)"),
                             start=True, stop=True).then_inc(gt_pe, 1)

            def invert(levels, r, n, dv, done, p, side):
                def part(i, bank, lhs, rhs):
                    for j in range(2):
                        h = 2 * i + j
                        mm = nc.tensor.matmul(PS[r, bank, n * j:n * j + n], lhs(h), rhs(h), start=True, stop=True)
                    done(mm)
                A_, P_ = (lambda h: b_a[p][r, h, r]), (lambda h: b_p[r, h, r])
                X_, Y_ = (lambda h: b_x[r, h, r]), (lambda h: b_y[p][r, h, r])
                halves = [(i, "ab"[i], HALF_BANKS[i]) for i in range(2)]
                dv("a2")
                for i, nm, (b0, b1) in halves:
                    part(i, b0, A_, lambda h: ident[r, r])
                side(1)
                for l in range(2, levels + 1):
                    for i, nm, (b0, b1) in halves:
                        dv(f"y{l - 1}{nm}")
                        part(i, b0, A_, Y_)
                    side(l)
                    for i, nm, (b0, b1) in halves:
                        dv(f"p{l}{nm}")
                        part(i, b0, X_, P_)
                        if l < levels:
                            part(i, b1, P_, X_)
                dv(f"y{levels}b")

            def dv(name, c): delta_wait(pe, "dve", name, c)
            def aw(name, c): delta_wait(pe, "act", name, c)
            def done(stage, i): i.then_inc(delta_sem[stage, "pe"], 1)

            def each(stage, bank, lhs, rhs):
                for h in range(NH):
                    mm = nc.tensor.matmul(PS[:, bank, P * h:P * h + P], lhs(h), rhs(h), start=True, stop=True)
                done(stage, mm)

            def front(part, c, p):
                first = isinstance(c, int) and c == 0
                if part == "bc":
                    dv("gu", c)
                    if not first:
                        dv("vb", c - 1)
                    done("front", nc.tensor.matmul(PS[:, 0, :], ones, b_kbe[p].rearrange("p h n -> p (h n)"), start=True, stop=True))
                elif part == "kk":
                    aw("ks", c)
                    each("front", 1, lambda h: b_ks[:, h, :], lambda h: b_ks[:, h, :])
                elif part == "kq":
                    each("front", 2, lambda h: b_ks[:, h, :], lambda h: H[:, h, bass.ts(c, CH)])
                elif part == "kt":
                    for h in range(NH):
                        mm = nc.tensor.transpose(PS[:, 3, P * h:P * h + P], b_ks[:, h, :], ident)
                    done("front", mm)
                elif part == "vt":
                    aw("vs", c)
                    dv("t1", c)
                    aw("eg", c)
                    for h in range(NH):
                        mm = nc.tensor.transpose(PS[:, 0, P * h:P * h + P], b_vs[:, h, :], ident)
                    done("front", mm)

            def state(part, c, p):
                if part == "wt":
                    dv("y7b", c)
                    if not (isinstance(c, int) and c == NBLK - 1):
                        dv("vb", c + 1)
                    each("state", 0, lambda h: b_kbe[p][:, h, :], lambda h: b_y[p][:, h, :])
                elif part == "vn":
                    aw("nw", c)
                    if not (isinstance(c, int) and c == 0):
                        dv("s2", c - 1)
                    for h in range(NH):
                        o = PS[:, 1, P * h:P * h + P]
                        nc.tensor.matmul(o, b_y[p][:, h, :], b_vb[p][:, h, :], start=True, stop=False)
                        mm = nc.tensor.matmul(o, b_nw[:, h, :], b_s[:, h, :], start=False, stop=True)
                    done("state", mm)
                elif part == "o":
                    aw("vn", c)
                    for h in range(NH):
                        o = PS[:, 2, P * h:P * h + P]
                        nc.tensor.matmul(o, b_s[:, h, :], b_qd[p][:, h, :], start=True, stop=False)
                        mm = nc.tensor.matmul(o, b_vn[:, h, :], b_qk[p][:, h, :], start=False, stop=True)
                    done("state", mm)
                elif part == "su":
                    each("state", 3, lambda h: b_kd[p][:, h, :], lambda h: b_vn[:, h, :])

            def delta(c, p, before, after):
                def side(l):
                    if before and l == 1:
                        state("wt", c - 1, 1 - p)
                    if before and l == 2:
                        state("vn", c - 1, 1 - p)
                    if after and l == 3:
                        front("bc", c + 1, 1 - p)
                    if before and l == 3:
                        state("o", c - 1, 1 - p)
                    if before and l == 4:
                        state("su", c - 1, 1 - p)
                    if after and l == 4:
                        front("kk", c + 1, 1 - p)
                    if after and l == 5:
                        if before:
                            aw("o", c - 1)
                        front("kq", c + 1, 1 - p)
                    if after and l == 6:
                        if before:
                            dv("s2", c - 1)
                        front("kt", c + 1, 1 - p)
                    if after and l == 7:
                        front("vt", c + 1, 1 - p)
                invert(LEVELS, slice(0, P), P, lambda name: dv(name, c), lambda mm: done("inverse", mm), p, side)
            pe.wait_ge(l_sd, 8)
            pe.wait_ge(gt_act, 14)
            for part in ("bc", "kk", "kq", "kt", "vt"):
                front(part, 0, 0)
            delta_blocks(pe, delta)
            for part in ("wt", "vn", "o", "su"):
                state(part, NBLK - 1, 1)

            r, tn = slice(0, TS), slice(TP, T)
            def sdv(name): pe.wait_ge(sd_dve, at(SDVE_STEPS, name))
            def saw(name): pe.wait_ge(sd_act, at(SACT_STEPS, name))
            def seach(bank, rows, width, lhs, rhs):
                for h in range(NH):
                    mm = nc.tensor.matmul(PS[rows, bank, width * h:width * h + width], lhs(h), rhs(h), start=True, stop=True)
                mm.then_inc(sd_pe, 1)
            sdv("gu")
            aw("o", NBLK - 1)
            dv("s2", NBLK - 1)
            nc.tensor.matmul(PS[:, 0, 0:P].rearrange("p (h n) -> p h n", h=NH), ones[r, :], b_kbe[0][r, :, r], start=True, stop=True).then_inc(sd_pe, 1)
            saw("ks")
            seach(1, r, TS, lambda h: b_ks[:, h, r], lambda h: b_ks[:, h, r])
            seach(2, r, TS, lambda h: b_ks[:, h, r], lambda h: H[:, h, tn])
            for h in range(NH):
                mm = nc.tensor.transpose(PS[r, 3, P * h:P * h + P], b_ks[:, h, r], ident)
            mm.then_inc(sd_pe, 1)
            saw("vs")
            sdv("t1")
            saw("eg")
            for h in range(NH):
                mm = nc.tensor.transpose(PS[r, 0, P * h:P * h + P], b_vs[:, h, r], ident)
            mm.then_inc(sd_pe, 1)
            invert(2, r, TS, sdv, lambda mm: mm.then_inc(sd_pe, 1), 0, lambda l: None)
            sdv("vb")
            seach(0, slice(0, P), TS, lambda h: b_kbe[0][r, h, :], lambda h: b_y[0][r, h, r])
            saw("nw")
            pe.wait_ge(s0_in, 16)
            for h in range(NH):
                nc.tensor.matmul(PS[:, 1, TS * h:TS * h + TS], b_vb[0][r, h, :], b_y[0][r, h, r], start=True, stop=False)
                for b in range(NB):
                    o = slice(LS * b, LS * b + LS)
                    mm = nc.tensor.matmul(PS[:, 1, TS * h + LS * b:TS * h + LS * b + LS], S0[:, b, h, :], b_ks[:, h, o],
                                          start=False, stop=(b == NB - 1))
            mm.then_inc(sd_pe, 1)
            saw("vnt")
            for h in range(NH):
                mm = nc.tensor.transpose(PS[r, 4, P * h:P * h + P], b_vs[:, h, r], ident)
            mm.then_inc(sd_pe, 1)
            saw("vn")
            for h in range(NH):
                nc.tensor.matmul(PS[:, 2, TS * h:TS * h + TS], b_x[r, h, :], b_qk[0][r, h, r], start=True, stop=False)
                for b in range(NB):
                    o = slice(LS * b, LS * b + LS)
                    mm = nc.tensor.matmul(PS[:, 2, TS * h + LS * b:TS * h + LS * b + LS], S0[:, b, h, :], b_qd[0][:, h, o],
                                          start=False, stop=(b == NB - 1))
            mm.then_inc(sd_pe, 1)
            for h in range(NH):
                sdv(f"vm{h}")
                vm = (s_vm0, s_vm1)[h % 2]
                if h >= 2:
                    sdv(f"sb{h - 2}")
                for q in range(2):
                    mm = nc.tensor.matmul(PS[:, 4 + 2 * (h % 2) + q, :], b_kd[0][r, h, :], vm[r, 512 * q:512 * q + 512],
                                          start=True, stop=True)
                mm.then_inc(sd_pe, 1)

            rows_norm(8, 4)
            pe.wait_ge(l_sd, 12)
            gemm_pe(pe, "dz")

            gemm_pe(pe, "gate")
            pe.wait_ge(acc_free, acc0["gate"] + 16)

            def branch(t, p):
                pe.wait_ge(w_split, SLOTS["branch"][0] + t + 1)
                wait(pe, br_m, 2 * t - 1)
                ready = (y_lo, 0) if isinstance(t, int) and t == 0 else None
                gemm_tile(0, p, 0, 4, 0, ready=ready).then_inc(br_a, 1)
                wait(pe, br_m, 2 * t)
                gemm_tile(1, p, 4, 4, 4 * P, 4, ready=ready).then_inc(w_used, 1)
            pairs(pe, 8, branch)
            pe.wait_ge(br_m, 16)

            def simple(name, free, ready):
                def body(t, p):
                    pe.wait_ge(w_split, SLOTS[name][0] + t + 1)
                    wait(pe, free, t - 1)
                    gemm_tile(p, p, 0, KT, 0, ready=ready if isinstance(t, int) and t == 0 else None).then_inc(w_used, 1)
                pairs(pe, SLOTS[name][1], body)
            simple("mix", acc_free2, (y_lo, 8))

            pe.wait_ge(acc_free2, 8)
            norm_pe(pe, 1, NM)
            pe.wait_ge(nlo, 16)
            for n in range(2):
                for s in range(4):
                    pe.wait_ge(w_split, SLOTS["xkv"][0] + 4 * n + s + 1)
                    p = s % 2
                    for kk in range(2):
                        k = 2 * s + kk
                        for m in range(2):
                            for j, (x_, w_) in enumerate(((XH, WH), (XL, WH), (XH, WL))):
                                mm = nc.tensor.matmul(PS[:, 2 * n + m, :], x_[:, k, CH * m:CH * m + CH],
                                                      w_[:, p, 512 * kk:512 * kk + 512],
                                                      start=(k == 0 and j == 0), stop=(k == KT - 1 and j == 2))
                    mm.then_inc(w_used, 1)
            pe.wait_ge(kv_sb, 2)
            for m in range(2):
                for h in range(NH):
                    mm = nc.tensor.transpose(PS[:, 4 + m, P * h:P * h + P], m_k[:, m, P * h:P * h + P], ident)
            mm.then_inc(mkt_ps, 1)
            pe.wait_ge(kv_sb, 4)
            norm_pe(pe, 2, T)
            simple("xq", hq_ok, (nlo, 16))

            def xattn_front(c, p):
                pe.wait_ge(xa_st, c + 1)
                if isinstance(c, int) and c == 0:
                    pe.wait_ge(hq_ok, 4)
                wait(pe, xa_exp, 4 * (c - 1))
                for h in range(NH):
                    mm = nc.tensor.matmul(x_ps(h, p), x_q[:, p, h, :], m_kT[:, h, :], start=True, stop=True)
                    if h % 2:
                        mm.then_inc(xa_sc, 1)

            def xattn_back(c, p, left):
                if left:
                    xattn_front(c + 1, 1 - p)
                pe.wait_ge(xa_p, c + 1)
                wait(pe, xa_pt, 2 * c)
                for i in range(2):
                    for h in range(NH):
                        mm = nc.tensor.transpose(PS[:, 2 + i, CH * h:CH * h + CH], x_s[:, p, h, CH * i:CH * i + CH], ident)
                    mm.then_inc(xa_tp, 1)
                pe.wait_ge(xa_pt, 2 * c + 2)
                wait(pe, xa_lo, c)
                for h in range(NH):
                    for i in range(2):
                        mm = nc.tensor.matmul(PS[:, 4, CH * h:CH * h + CH], m_v[:, i, P * h:P * h + P], x_pt[:, i, h, :],
                                              start=(i == 0), stop=(i == 1))
                mm.then_inc(xa_pv, 1)
            pipelined(pe, NBLK, xattn_front, xattn_back)
            pe.wait_ge(xa_lo, NBLK)
            pe.wait_ge(xk_in, 64)
            for h in range(NH):
                for q in range(4):
                    mm = nc.tensor.matmul(PS[TS * h:TS * h + TS, q, :], HQ[:, h, TP:T], kc_buf[h][:, 512 * q:512 * q + 512],
                                          start=True, stop=True)
                mm.then_inc(xs_sc, 1)
            pe.wait_ge(xs_dv, 5)
            for q in range(4):
                wait(pe, xs_ptok, q - 1)
                for i in range(4):
                    k = 4 * q + i
                    mm = nc.tensor.transpose(PS[:, 4 + q % 2, CH * i:CH * i + CH], xs_s[:, CH * k:CH * k + CH], ident)
                mm.then_inc(xs_tp, 1)
            pe.wait_ge(xs_ptok, 4)
            pe.wait_ge(xv_in, 64)
            for h in range(NH):
                v = vc_buf[h].rearrange("p (m n) -> p m n", n=P)
                for k in range(2 * NB):
                    mm = nc.tensor.matmul(PS[:, 6, TS * h:TS * h + TS], v[:, k, :], xs_pt[:, k, TS * h:TS * h + TS],
                                          start=(k == 0), stop=(k == 2 * NB - 1))
            mm.then_inc(xs_pv, 1)

            pe.wait_ge(xa_lo, NBLK + 1)
            for s in range(4):
                pe.wait_ge(w_split, SLOTS["xo"][0] + s + 1)
                wait(pe, xo_free, 2 * s - 1)
                gemm_tile(0, s % 2, 0, 4, 0).then_inc(xo_a, 1)
                wait(pe, xo_free, 2 * s)
                gemm_tile(1, s % 2, 0, 4, 4 * P).then_inc(w_used, 1)

            pe.wait_ge(xo_free, 8)
            norm_pe(pe, 3, T)

            def down(f, n0):
                pe.wait_ge(f_lo, 2 * f + 2)
                for m in range(KT):
                    if m % 4 == 0:
                        pe.wait_ge(w_split, n0 + m // 4 + 1)
                    pe.wait_ge(fd_free, 8 * f + (m if m >= 2 else 1))
                    p = m // 4
                    for k in range(2):
                        for w_, x_ in ((WH, AH), (WH, AL), (WL, AH)):
                            for c in range(NCH):
                                mm = nc.tensor.matmul(PS[:, 3 * (m % 2) + c, 0:CW],
                                                      w_[:, p, (m % 4) * 256 + k * P:(m % 4) * 256 + k * P + P],
                                                      x_[:, k, bass.ts(c, CW)], start=(k == 0 and w_ is WH and x_ is AH),
                                                      stop=(k == 1 and w_ is WL))
                    mm.then_inc(w_used if m % 4 == 3 else f_down, 1)

            def mlp_pe(f):
                first = isinstance(f, int) and f == 0
                for j in range(4):
                    pe.wait_ge(w_split, FFN0(f) + j + 1)
                    if j < 2:
                        if not first:
                            pe.wait_ge(fd_free, 8 * (f - 1) + 1)
                            pe.wait_ge(f_gate, 2 * f - 1 + j)
                    else:
                        pe.wait_ge(fu_free, 2 * f + j - 1)
                    gemm_tile(j % 2, j % 2, 0, KT, 0, ready=(nlo, 24) if first and j == 0 else None).then_inc(w_used, 1)
                if not first:
                    pe.wait_ge(f_gate, 2 * f + 2)
                    down(f - 1, FFN0(f) + 4)
            mlp_pe(0)
            with pe.Fori(1, FT // 2) as f:
                mlp_pe(f)
            pe.wait_ge(f_gate, FT)
            down(FT // 2 - 1, NSLOTS - 2)
            pe.wait_ge(fd_free, 4 * FT + 1)
            norm_pe(pe, 4, T)

        @block.vector
        def _(dve):
            dve.wait_ge(const_in, 16)
            norm_dve(dve, 0, H, cst("g_mix"), XH, XL, T)
            dve.wait_ge(rope_in, 48)
            for t in range(5):
                dve.wait_ge(rot_ps, t + 1)
                wait(dve, rot_x, 3 * t)
                nc.vector.tensor_tensor(wide(n_sq[:, 1, :]), acc(t % 2), wide(rope[:, 1, :]), ALU.mult).then_inc(rot_t, 1)
                nc.vector.tensor_tensor(H[:, t, :], H[:, t, :], rope[:, 0, :], ALU.mult).then_inc(rot_x, 1)
                dve.wait_ge(rot_t, t + 1)
                dve.wait_ge(rot_x, 3 * t + 1)
                nc.vector.tensor_tensor(H[:, t, :], H[:, t, :], n_sq[:, 1, :], ALU.add).then_inc(rot_x, 2)
            dve.wait_ge(rot_x, 15)
            nc.vector.memset(a_q, 0.0).then_inc(at_zero, 1)
            nc.vector.memset(a_v[:, 1, :], 0.0).then_inc(at_zero, 1)
            nc.vector.memset(a_s[0][:, :, 0:CH], NEG).then_inc(at_zero, 1)
            nc.vector.memset(a_s[1][:, :, 0:CH], NEG).then_inc(at_zero, 1)
            dve.wait_ge(at_zero, 4)
            scale = float(HD) ** -0.5

            def row_max(mx, nm, es, sinks, s, done, n0):
                nc.vector.reduce_max(mx, s, AX.X).then_inc(done, 1)
                dve.wait_ge(done, n0 + 1)
                nc.vector.tensor_tensor(nm, mx, sinks, ALU.max).then_inc(done, 1)
                dve.wait_ge(done, n0 + 2)
                nc.vector.tensor_tensor(es, sinks, nm, ALU.subtract).then_inc(done, 1)
                dve.wait_ge(done, n0 + 3)
                nc.vector.tensor_scalar(nm, nm, -1.0, None, ALU.mult).then_inc(done, 1)

            def row_divide(s, den_t, es, den, n0, probs):
                nc.vector.tensor_tensor(den_t, den_t, es, ALU.add).then_inc(den, 1)
                dve.wait_ge(den, n0 + 1)
                nc.vector.reciprocal(den_t, den_t).then_inc(den, 1)
                dve.wait_ge(den, n0 + 2)
                nc.vector.tensor_tensor(s, s, den_t.unsqueeze(2).to_broadcast(list(s.shape)), ALU.mult).then_inc(probs, 1)

            def swa_front(c, p):
                wait(dve, at_tp, 4 * (c - 1))
                for b in range(4):
                    dve.wait_ge(at_sc, 4 * c + b + 1)
                    ps = PS[:, b, :].rearrange("p (h n) -> p h n", h=2)
                    k0 = CH if isinstance(c, int) and c == 0 else 0
                    mask = a_mask[:, k0:2 * CH].unsqueeze(1).to_broadcast([P, 2, 2 * CH - k0])
                    nc.vector.scalar_tensor_tensor(a_s[p][:, 2 * b:2 * b + 2, k0:2 * CH], ps[:, :, k0:2 * CH], scale, mask,
                                                   ALU.mult, ALU.add).then_inc(at_msk, 1)
                dve.wait_ge(at_msk, 4 * c + 4)
                row_max(a_mx[:, p, :], a_nm[:, p, :], a_es[:, p, :], cst("sinks"), a_s[p], at_mx, 4 * c)

            def swa_back(c, p, left):
                dve.wait_ge(at_exp, 9 * c + 9)
                row_divide(a_s[p], a_den[:, p, :], a_es[:, p, :], at_den, 2 * c, at_p)
                if left:
                    swa_front(c + 1, 1 - p)
            pipelined(dve, NBLK, swa_front, swa_back)

            dve.wait_ge(smask_in, 16)
            dve.wait_ge(pwv_out, 1)
            for g in range(2):
                dve.wait_ge(ss_sc, g + 1)
                nc.vector.scalar_tensor_tensor(s_s[:, g, 0:TP].rearrange("p (b n) -> p b n", b=2), PS[:, 3 * g:3 * g + 2, :],
                                               scale, s_mask[:, 0:TP].rearrange("p (b n) -> p b n", b=2),
                                               ALU.mult, ALU.add).then_inc(ss_msk, 1)
                nc.vector.scalar_tensor_tensor(s_s[:, g, TP:T], PS[:, 3 * g + 2, 0:TS], scale, s_mask[:, TP:T],
                                               ALU.mult, ALU.add).then_inc(ss_msk, 1)
            dve.wait_ge(ss_msk, 4)
            row_max(s_mx, s_nm, s_es, cst("sinks_s"), s_s, ss_mx, 0)
            dve.wait_ge(ss_exp, 3)
            row_divide(s_s, s_den, s_es, ss_den, 0, ss_p)

            nc.vector.memset(SM, 0.0).then_inc(gt_dve, 1)
            nc.vector.tensor_copy(WABH, cst("w_ab")).then_inc(gt_dve, 1)
            dve.wait_ge(gt_dve, 2)
            nc.vector.tensor_tensor(WABL, cst("w_ab"), WABH.bitcast(F32), ALU.subtract).then_inc(gt_dve, 1)
            dve.wait_ge(ss_pv, 1)
            dve.wait_ge(out_done, n_attn)
            for p in range(2):
                nc.vector.memset(c_pre[:, p, 0:3], 0.0).then_inc(c_his, 1)
            dve.wait_ge(dn_in, 16)

            def conv(t, p):
                x = c_pre[:, p, :]
                xs = x[:, 3 + TP:PRE].rearrange("p (b n) -> p b n", b=NB)
                y = c_acc[:, p, :]
                ys = y[:, TP:T].rearrange("p (b n) -> p b n", b=NB)
                wait(dve, c_cv, 8 * (t - 1))
                nc.vector.tensor_copy(xs[:, :, 0:3], c_hist[:, t, :, :]).then_inc(c_his, 1)
                dve.wait_ge(c_pre_ok, 4 * t + 4)
                dve.wait_ge(acc_free, acc0["dn"] + t + 1)
                dve.wait_ge(c_his, t + 3)
                wait(dve, c_act, t - 1)
                for j in range(4):
                    w_ = CST[:, bass.ds(CONST["dn_w"][0] + 4 * t + j, 1)]
                    if j == 0:
                        nc.vector.tensor_scalar(y[:, 0:TP], x[:, 0:TP], w_, None, ALU.mult).then_inc(c_cv, 1)
                        nc.vector.tensor_scalar(ys, xs[:, :, 0:4], w_, None, ALU.mult).then_inc(c_cv, 1)
                    else:
                        dve.wait_ge(c_cv, 8 * t + 2 * j - 1)
                        nc.vector.scalar_tensor_tensor(y[:, 0:TP], x[:, j:j + TP], w_, y[:, 0:TP], ALU.mult, ALU.add).then_inc(c_cv, 1)
                        dve.wait_ge(c_cv, 8 * t + 2 * j)
                        nc.vector.scalar_tensor_tensor(ys, xs[:, :, j:j + 4], w_, ys, ALU.mult, ALU.add).then_inc(c_cv, 1)
            pairs(dve, 12, conv)

            def rows_norm(i0, n, src, gain):
                for t in range(n):
                    dve.wait_ge(l_iv, i0 + t + 1)
                    if gain is None:
                        i = nc.vector.tensor_tensor(src(t), src(t), l_rs[:, t % 2, :], ALU.mult)
                    else:
                        i = nc.vector.scalar_tensor_tensor(src(t), src(t), gain, l_rs[:, t % 2, :], ALU.mult, ALU.mult)
                    i.then_inc(l_ok, 1)
            rows_norm(0, 8, lambda t: H[:, t, :], None)

            n = [3]

            def g(i, after=None):
                i.then_inc(gt_dve, 1)
                n[0] += 1
                dve.wait_ge(gt_dve, n[0])
            bc4 = lambda ap: ap.unsqueeze(1).to_broadcast([P, 9, NH])
            dve.wait_ge(gt_act, 2)
            g(nc.vector.tensor_tensor(g_x, g_ab[:, :, 0:4], bc4(cst("dt_bias")), ALU.add))
            g(nc.vector.tensor_scalar(g_t, g_x, -1.0, None, ALU.mult))
            g(nc.vector.tensor_tensor(g_ax, g_x, g_t, ALU.max))
            g(nc.vector.tensor_scalar(g_x, g_x, 0.0, None, ALU.max))
            dve.wait_ge(gt_act, 6)
            g(nc.vector.tensor_tensor(g_x, g_x, g_l, ALU.add))
            g(nc.vector.tensor_tensor(g_g, g_x, bc4(g_ea), ALU.mult))
            g(nc.vector.tensor_scalar(g_g, g_g, -1.0, None, ALU.mult))
            g(nc.vector.tensor_scalar(g_eb, g_eb, 1.0, None, ALU.add))
            dve.wait_ge(dm_in, 32)
            g(nc.vector.tensor_tensor(g_bm[0:TS], g_g[0:TS, NBLK, :].unsqueeze(1).to_broadcast([TS, NB, NH]),
                                      ms_b[0:TS, :].unsqueeze(2).to_broadcast([TS, NB, NH]), ALU.mult))
            assert n[0] == 12
            dve.wait_ge(gt_act, 12)
            for c0, c1, rows in ((0, NBLK, P), (NBLK, 9, TS)):
                i = nc.vector.tensor_tensor(g_kds[0:rows, c0:c1, :], g_gl[0:rows, c0:c1, :], g_c[0:rows, c0:c1, :], ALU.subtract)
                if c0 == 0:
                    i.then_inc(gt_dve2, 1)
            i.then_inc(gt_dve, 1)
            n[0] += 1
            nc.vector.reciprocal(g_beta, g_eb).then_inc(gt_dve, 1)
            n[0] += 1
            dve.wait_ge(gt_act, 14)
            dve.wait_ge(gt_dve, n[0])
            nc.vector.tensor_tensor(g_be, g_beta, g_ec, ALU.mult).then_inc(gt_dve, 1)
            n[0] += 1
            dve.wait_ge(gt_dve, n[0])
            nc.vector.memset(b_s, 0.0).then_inc(s_zero, 1)
            dve.wait_ge(s_zero, 1)

            def front(part, p, done, dv, pw, aw, rows, q, c, ut, mu, ml):
                r = slice(0, rows)
                hb = lambda ap: ap.unsqueeze(1).to_broadcast([rows, NH, rows])
                tb = lambda ap, w=rows: ap[r, c, :].unsqueeze(2).to_broadcast([rows, NH, w])
                ps = lambda bank, w=rows: PS[r, bank, 0:NH * w].rearrange("p (h n) -> p h n", h=NH)
                ba, bqk = b_a[p][r, :, r], b_qk[p][r, :, r]
                if part == "gu":
                    done(nc.vector.tensor_tensor(b_kbe[p][r, :, r], hb(ut), tb(g_g), ALU.mult))
                elif part == "t":
                    pw("bc")
                    done(nc.vector.tensor_tensor(ba, ps(0), tb(g_c), ALU.subtract))
                    dv("t1")
                    done(nc.vector.tensor_tensor(bqk, ba, hb(mu), ALU.add))
                    dv("t2")
                    done(nc.vector.tensor_tensor(ba, hb(ml), ba, ALU.subtract))
                elif part == "a":
                    pw("kk")
                    aw("dd")
                    done(nc.vector.tensor_tensor(ba, ps(1), ba, ALU.mult))
                    dv("a1")
                    done(nc.vector.tensor_tensor(ba, ba, tb(g_beta), ALU.mult))
                elif part == "q":
                    pw("kq")
                    done(nc.vector.tensor_tensor(bqk, ps(2), bqk, ALU.mult))
                    done(nc.vector.tensor_tensor(b_qd[p][:, :, r], q, b_qd[p][:, :, r], ALU.mult))
                elif part == "k":
                    pw("kt")
                    done(nc.vector.tensor_tensor(b_kbe[p][r, :, :], ps(3, w=P), tb(g_be, P), ALU.mult))
                    done(nc.vector.tensor_tensor(b_kd[p][r, :, :], ps(3, w=P), tb(g_kds, P), ALU.mult))
                elif part == "v":
                    pw("vt")
                    done(nc.vector.tensor_tensor(b_vb[p][r, :, :], ps(0, w=P), tb(g_beta, P), ALU.mult))

            def invert(levels, rows, p, done, dv, pw, side):
                r = slice(0, rows)
                hb = lambda ap: ap.unsqueeze(1).to_broadcast([rows, NH, rows])
                bp, ba, by, bx = (b[r, :, r] for b in (b_p, b_a[p], b_y[p], b_x))
                halves = [(n, slice(2 * i, 2 * i + 2), HALF_BANKS[i]) for i, n in enumerate("ab")]
                h2 = lambda ap: ap.unsqueeze(1).to_broadcast([rows, 2, rows])
                p2 = lambda bank: PS[r, bank, 0:2 * rows].rearrange("p (h n) -> p h n", h=2)
                dv("a2")
                done(nc.vector.tensor_tensor(bx, ba, hb(m_1l[r, r]), ALU.mult))
                dv("x1a")
                done(nc.vector.tensor_tensor(bx, hb(ident[r, r]), bx, ALU.subtract))
                for n, hh, (b0, b1) in halves:
                    pw("u1" + n)
                    done(nc.vector.tensor_tensor(bp[:, hh, :], p2(b0), h2(m_lev[r, 0, r]), ALU.mult))
                for n, hh, (b0, b1) in halves:
                    dv("p1" + n)
                    done(nc.vector.tensor_tensor(by[:, hh, :], h2(ident[r, r]), bp[:, hh, :], ALU.subtract))
                for l in range(2, levels + 1):
                    for n, hh, (b0, b1) in halves:
                        pw(f"lp{l}{n}")
                        dv(f"y{l - 1}{n}")
                        done(nc.vector.tensor_tensor(bp[:, hh, :], p2(b0), h2(m_lev[r, l - 1, r]), ALU.mult))
                    side(l)
                    for n, hh, (b0, b1) in halves:
                        pw(f"lz{l}{n}")
                        done(nc.vector.tensor_tensor(by[:, hh, :], by[:, hh, :], p2(b0), ALU.subtract))
                        if l < levels:
                            pw(f"lx{l}{n}")
                            done(nc.vector.tensor_tensor(bx[:, hh, :], bx[:, hh, :], p2(b1), ALU.subtract))

            def dv(name, c): delta_wait(dve, "dve", name, c)
            def pw(name, c): delta_wait(dve, "pe", name, c)
            def aw(name, c): delta_wait(dve, "act", name, c)

            def prompt_front(part, c, p):
                front(part, p, lambda i: i.then_inc(delta_sem["front", "dve"], 1), lambda name: dv(name, c),
                      lambda name: pw(name, c), lambda name: aw(name, c), P, H[:, 0:4, bass.ts(c, CH)], c,
                      m_ut[:, :], m_u[:, :], m_l[:, :])

            def state(c):
                def done(i): i.then_inc(delta_sem["state", "dve"], 1)
                pw("su", c)
                done(nc.vector.tensor_tensor(b_s, b_s, g_egl[:, c, :].unsqueeze(2).to_broadcast([P, NH, P]), ALU.mult))
                dv("s1", c)
                done(nc.vector.tensor_tensor(b_s, b_s, PS[:, 3, :].rearrange("p (h n) -> p h n", h=NH), ALU.add))

            def delta(c, p, before, after):
                def side(l):
                    if after and l == 2:
                        if before:
                            pw("wt", c - 1)
                        prompt_front("gu", c + 1, 1 - p)
                    if after and l == 4:
                        if before:
                            pw("o", c - 1)
                        prompt_front("t", c + 1, 1 - p)
                    if before and l == 5:
                        state(c - 1)
                    if after and l == 6:
                        prompt_front("a", c + 1, 1 - p)
                        prompt_front("q", c + 1, 1 - p)
                    if after and l == 7:
                        prompt_front("k", c + 1, 1 - p)
                invert(LEVELS, P, p, lambda i: i.then_inc(delta_sem["inverse", "dve"], 1), lambda name: dv(name, c),
                       lambda name: pw(name, c), side)
                if after:
                    prompt_front("v", c + 1, 1 - p)
            for part in ("gu", "t", "a", "q", "k", "v"):
                prompt_front(part, 0, 0)
            delta_blocks(dve, delta)
            state(NBLK - 1)

            def sdone(i): i.then_inc(sd_dve, 1)
            def sdv(name): dve.wait_ge(sd_dve, at(SDVE_STEPS, name))
            def spw(name): dve.wait_ge(sd_pe, at(SPE_STEPS, name))
            def saw(name): dve.wait_ge(sd_act, at(SACT_STEPS, name))
            for part in ("gu", "t", "a", "q", "k", "v"):
                front(part, 0, sdone, sdv, spw, saw, TS, H[:, 0:4, TP:T], NBLK, ms_ut[0:TS, :], ms_u[0:TS, :], ms_l[0:TS, :])
            invert(2, TS, 0, sdone, sdv, spw, lambda l: None)
            dve.wait_ge(s0_in, 16)
            spw("o")
            saw("vn")
            for h in range(NH):
                vm = (s_vm0, s_vm1)[h % 2]
                if h >= 2:
                    spw(f"su{h - 2}")
                sdone(nc.vector.tensor_tensor(vm[0:TS, :].rearrange("p (b n) -> p b n", b=NB),
                                              b_x[0:TS, h, :].unsqueeze(1).to_broadcast([TS, NB, P]),
                                              ms_b[0:TS, :].unsqueeze(2).to_broadcast([TS, NB, P]), ALU.mult))
                s0 = S0[:, :, h, :]
                sdone(nc.vector.tensor_tensor(s0, s0, g_egs[:, :, h].unsqueeze(2).to_broadcast([P, NB, P]), ALU.mult))
                sdv(f"sa{h}")
                spw(f"su{h}")
                k = 4 + 2 * (h % 2)
                sdone(nc.vector.tensor_tensor(s0, s0, PS[:, k:k + 2, :].rearrange("p a (b n) -> p (a b) n", n=P), ALU.add))

            rows_norm(8, 4, lambda t: H[:, t, :], cst("g_dn"))
            for t in range(4):
                dve.wait_ge(l_ok, 9 + t)
                dve.wait_ge(acc_free, acc0["dz"] + t + 1)
                nc.vector.tensor_tensor(H[:, t, :], H[:, t, :], z_sb[:, t % 2, :], ALU.mult).then_inc(z_y, 1)

            def split_rests(src, base):
                for k in range(KT):
                    dve.wait_ge(y_hi, base + k + 1)
                    nc.vector.tensor_tensor(XL[:, k, :], src(k), XH[:, k, :].bitcast(F32), ALU.subtract).then_inc(y_lo, 1)
            split_rests(lambda k: YA[:, k, :] if k < 4 else H[:, k - 4, :], 0)
            dve.wait_ge(acc_free, acc0["gate"] + 16)
            for t in range(8):
                dve.wait_ge(br_a, t + 1)
                nc.vector.tensor_tensor(wide(ga(t)), wide(ga(t)), acc(0), ALU.mult).then_inc(br_m, 1)
                dve.wait_ge(w_used, SLOTS["branch"][0] + t + 1)
                nc.vector.tensor_tensor(wide(gb(t)), wide(gb(t)), acc(1), ALU.mult).then_inc(br_m, 1)
                dve.wait_ge(br_m, 2 * t + 2)
                nc.vector.tensor_tensor(ga(t), ga(t), gb(t), ALU.add).then_inc(br_s, 1)
            split_rests(ga, 8)
            dve.wait_ge(y_lo, 16)
            dve.wait_ge(xres_in, 16)

            def residual(t, p):
                dve.wait_ge(w_used, SLOTS["mix"][0] + t + 1)
                nc.vector.tensor_tensor(wide(H[:, t, :]), wide(x_res[:, t, :]), acc(p), ALU.add).then_inc(acc_free2, 1)
            pairs(dve, 8, residual)

            dve.wait_ge(acc_free2, 8)
            norm_dve(dve, 1, m_x, cst("g_mem"), XH, XL, NM)
            dve.wait_ge(w_used, SLOTS["xkv"][0] + 8)
            norm_dve(dve, 2, H, cst("g_x"), XH, XL, T)
            xscale = float(P) ** -0.5

            def xattn_front(c, p):
                for b in range(2):
                    dve.wait_ge(xa_sc, 2 * c + b + 1)
                    nc.vector.reduce_max(x_nm[:, p, 0, 2 * b:2 * b + 2],
                                         PS[:, X_BANKS[p] + b, :].rearrange("p (h n) -> p h n", h=2), AX.X).then_inc(xa_mx, 1)
                dve.wait_ge(xa_mx, 4 * c + 2)
                nc.vector.tensor_scalar(x_nm[:, p, 1, :], x_nm[:, p, 0, :], -xscale, None, ALU.mult).then_inc(xa_mx, 2)

            def xattn_rest(c):
                dve.wait_ge(xa_hi, c + 1)
                cs = bass.ts(c, CH)
                nc.vector.tensor_tensor(XL[:, 0:4, cs], PS[:, 4, :].rearrange("p (h n) -> p h n", h=NH),
                                        XH[:, 0:4, cs].bitcast(F32), ALU.subtract).then_inc(xa_lo, 1)

            def xattn_back(c, p, left):
                dve.wait_ge(xa_exp, 4 * c + 4)
                nc.vector.reciprocal(x_den[:, p, 1, :], x_den[:, p, 0, :]).then_inc(xa_den, 1)
                dve.wait_ge(xa_den, c + 1)
                nc.vector.tensor_tensor(x_s[:, p, :, :], x_s[:, p, :, :],
                                        x_den[:, p, 1, :].unsqueeze(2).to_broadcast([P, NH, NM]), ALU.mult).then_inc(xa_p, 1)
                if not (isinstance(c, int) and c == 0):
                    xattn_rest(c - 1)
                if left:
                    xattn_front(c + 1, 1 - p)
            pipelined(dve, NBLK, xattn_front, xattn_back)
            xattn_rest(NBLK - 1)
            dve.wait_ge(xs_in, 16)
            dve.wait_ge(xs_sc, 4)
            nc.vector.tensor_tensor(xs_s.rearrange("p (q b n) -> p q b n", q=4, b=2),
                                    PS[:, 0:4, :].rearrange("p q (b n) -> p q b n", b=2),
                                    x_sm.rearrange("p (q b) -> p q b", q=4).unsqueeze(3).to_broadcast([P, 4, 2, NM]),
                                    ALU.add).then_inc(xs_dv, 1)
            dve.wait_ge(xs_dv, 1)
            nc.vector.reduce_max(x_nm[:, 0, 0, 0:1], xs_s, AX.X).then_inc(xs_dv, 1)
            dve.wait_ge(xs_dv, 2)
            nc.vector.tensor_scalar(x_nm[:, 0, 1, 0:1], x_nm[:, 0, 0, 0:1], -xscale, None, ALU.mult).then_inc(xs_dv, 1)
            dve.wait_ge(xs_exp, 1)
            nc.vector.reciprocal(x_den[:, 0, 1, 0:1], x_den[:, 0, 0, 0:1]).then_inc(xs_dv, 1)
            dve.wait_ge(xs_dv, 4)
            nc.vector.tensor_scalar(xs_s, xs_s, x_den[:, 0, 1, 0:1], None, ALU.mult).then_inc(xs_dv, 1)
            dve.wait_ge(xa_hi, NBLK + 1)
            nc.vector.tensor_tensor(XL[:, 0:4, TP:T], PS[:, 6, 0:P].rearrange("p (h n) -> p h n", h=NH),
                                    XH[:, 0:4, TP:T].bitcast(F32), ALU.subtract).then_inc(xa_lo, 1)

            for t in range(8):
                if t % 2 == 0:
                    dve.wait_ge(xo_a, t // 2 + 1)
                else:
                    dve.wait_ge(w_used, SLOTS["xo"][0] + t // 2 + 1)
                nc.vector.tensor_tensor(wide(H[:, t, :]), wide(H[:, t, :]), acc(t % 2), ALU.add).then_inc(xo_free, 1)
            dve.wait_ge(xo_free, 8)
            norm_dve(dve, 3, H, cst("g_ffn"), XH, XL, T)

            dve.wait_ge(nlo, 32)
            nc.vector.memset(f_pre[:, :, 0:2], 0.0).then_inc(f_z, 1)
            nc.vector.memset(f_one, 1.0).then_inc(fd_free, 1)
            dve.wait_ge(f_in, 16)

            def mlp_conv(f, i):
                t = 2 * f + i
                x, y = f_pre[:, i, :], f_act[:, i, :]
                xs = x[:, 2 + TP:FPRE].rearrange("p (b n) -> p b n", b=NB)
                ys = y[:, TP:T].rearrange("p (b n) -> p b n", b=NB)
                wait(dve, f_cv, 6 * t - 6)
                nc.vector.tensor_copy(xs[:, :, 0:2], f_hist[:, t, :, :]).then_inc(f_his, 1)
                dve.wait_ge(fp_ok, 4 * t + 4)
                dve.wait_ge(fu_free, t + 1)
                dve.wait_ge(f_his, t + 1)
                wait(dve, f_lo, t - 1)
                for j in range(3):
                    w_ = CST[:, bass.ds(CONST["ffn_w"][0] + 3 * t + j, 1)]
                    if j == 0:
                        nc.vector.tensor_scalar(y[:, 0:TP], x[:, 0:TP], w_, None, ALU.mult).then_inc(f_cv, 1)
                        nc.vector.tensor_scalar(ys, xs[:, :, 0:4], w_, None, ALU.mult).then_inc(f_cv, 1)
                    else:
                        dve.wait_ge(f_cv, 6 * t + 2 * j - 1)
                        nc.vector.scalar_tensor_tensor(y[:, 0:TP], x[:, j:j + TP], w_, y[:, 0:TP], ALU.mult, ALU.add).then_inc(f_cv, 1)
                        dve.wait_ge(f_cv, 6 * t + 2 * j)
                        nc.vector.scalar_tensor_tensor(ys, xs[:, :, j:j + 4], w_, ys, ALU.mult, ALU.add).then_inc(f_cv, 1)

            def mlp_down(f, n0):
                for m in range(KT):
                    if m % 4 == 3:
                        dve.wait_ge(w_used, n0 + m // 4 + 1)
                    else:
                        dve.wait_ge(f_down, 6 * f + m - m // 4 + 1)
                    dve.wait_ge(fd_free, 8 * f + 1)
                    nc.vector.tensor_tensor(wide(H[:, m, :]), wide(H[:, m, :]), acc(m % 2), ALU.add).then_inc(fd_free, 1)

            def mlp_dve(f):
                for i in range(2):
                    mlp_conv(f, i)
                for i in range(2):
                    dve.wait_ge(w_used, FFN0(f) + 2 + i + 1)
                    dve.wait_ge(f_silu, 2 * f + i + 1)
                    nc.vector.tensor_tensor(wide(f_act[:, i, :]), wide(f_act[:, i, :]), acc(i), ALU.mult).then_inc(f_gate, 1)
                if not (isinstance(f, int) and f == 0):
                    mlp_down(f - 1, FFN0(f) + 4)
                for i in range(2):
                    dve.wait_ge(f_hi, 2 * f + i + 1)
                    nc.vector.tensor_tensor(AL[:, i, :], f_act[:, i, :], AH[:, i, :].bitcast(F32), ALU.subtract).then_inc(f_lo, 1)
            mlp_dve(0)
            with dve.Fori(1, FT // 2) as f:
                mlp_dve(f)
            mlp_down(FT // 2 - 1, NSLOTS - 2)
            dve.wait_ge(nrs, 5)
            for k in range(KT):
                nc.vector.scalar_tensor_tensor(H[:, k, :], H[:, k, :], cst("g_out")[:, k:k + 1], n_rs,
                                               ALU.mult, ALU.mult).then_inc(y_fin, 1)


def layouts(inputs):
    import numpy as np
    f = {k: np.asarray(v) for k, v in inputs.items()}
    A = np.ascontiguousarray
    gk = lambda g: g.reshape(-1, P).T
    o = {}
    x = np.concatenate([f["x_prompt"][0], f["x_sample"].reshape(TS, D)], 0)
    o["xT"] = A(x.T.reshape(KT, P, T))
    w_in = f["w_in"][0]
    out_tile = lambda w: w.reshape(KT, P, -1, P).transpose(2, 1, 0, 3).reshape(-1, P, SLOT)
    qcols = np.concatenate([np.r_[64 * j:64 * j + 64, 64 * (j + 4):64 * (j + 4) + 64] for j in range(NJ)])
    st = [out_tile(w_in[:, qcols]), out_tile(w_in[:, 512:768]), out_tile(w_in[:, 768:768 + 1536]),
          out_tile(w_in[:, 2304:2816]), out_tile(w_in[:, 2824:4872])]
    bra = f["w_br_a"][0][qcols].reshape(4, P, 8, P)
    brb = f["w_br_b"][0].reshape(4, P, 8, P)
    st.append(np.concatenate([bra, brb], 0).transpose(2, 1, 0, 3).reshape(8, P, SLOT))
    st.append(out_tile(f["w_mix_out"][0]))
    st.append(f["w_xkv"][0].reshape(4, 2, P, 2, 512).transpose(3, 0, 2, 1, 4).reshape(8, P, SLOT))
    st.append(out_tile(f["w_xq"][0]))
    st.append(f["w_xo"][0].reshape(4, P, 4, 2, P).transpose(2, 1, 3, 0, 4).reshape(4, P, SLOT))
    up = out_tile(f["w_up"][0]).reshape(2, FT // 2, 2, P, SLOT).transpose(1, 0, 2, 3, 4).reshape(FT // 2, 4, P, SLOT)
    dn = f["w_down"][0].reshape(FT // 2, 2, P, 2, 4, P).transpose(0, 3, 2, 4, 1, 5).reshape(FT // 2, 2, P, SLOT)
    for g in range(FT // 2 + 1):
        st += [up[g]] if g < FT // 2 else []
        st += [dn[g - 1]] if g > 0 else []
    o["w"] = A(np.concatenate(st, 0))
    assert o["w"].shape[0] == NSLOTS
    rep = lambda v: np.broadcast_to(v, (P, v.shape[-1]))
    sk = f["attn_sinks"][0]
    parts = {"ident": np.eye(P), "ones": np.ones((P, P)), "g_mix": gk(f["norm_mix_g"][0]), "g_mem": gk(f["norm_mem_g"][0]),
             "g_x": gk(f["norm_x_g"][0]), "g_ffn": gk(f["norm_ffn_g"][0]), "g_out": gk(f["final_norm_g"]),
             "g_dn": f["dn_norm_g"][0][:, None], "sinks": rep(sk), "sinks_s": np.stack([np.repeat(sk[:4], 32), np.repeat(sk[4:], 32)], 1),
             "a_log": rep(f["dn_a_log"][0]), "dt_bias": rep(f["dn_dt_bias"][0]),
             "dn_w": f["dn_conv_w"][0].reshape(4, 12, P).transpose(2, 1, 0).reshape(P, 48),
             "ffn_w": f["ffn_conv_w"][0].reshape(3, FT, P).transpose(2, 1, 0).reshape(P, FT * 3),
             "eps": np.full((P, 1), EPS), "eps_q": np.full((P, 1), P * EPS),
             "w_ab": w_in[:, 2816:2824].reshape(KT, P, 8).transpose(1, 0, 2).reshape(P, 64)}
    o["cst"] = A(np.concatenate([parts[k].astype(np.float32) for k in CONST], 1))
    assert o["cst"].shape[1] == NCONST
    pos = np.concatenate([np.arange(TP), np.tile(8192 + np.arange(LS), NB)]).astype(np.float32)
    inv = np.float32(500000.0) ** (np.float32(-2.0) * np.arange(8, dtype=np.float32) / np.float32(16))
    ang = pos[None, :] * inv.astype(np.float32)[:, None]
    cs, sn = np.ones((P, T), np.float32), np.zeros((P, T), np.float32)
    for g in range(2):
        for half in range(2):
            r = 64 * g + 8 * half
            cs[r:r + 8], sn[r:r + 8] = np.cos(ang), np.sin(ang)
    o["rope"] = A(np.stack([cs, sn], 1))
    pm = np.zeros((P, P), np.float32)
    for g in range(2):
        for i in range(8):
            pm[64 * g + 8 + i, 64 * g + i] = -1.0
            pm[64 * g + i, 64 * g + 8 + i] = 1.0
    o["perm"] = pm
    q, k = np.arange(CH)[:, None], np.arange(CH)[None]
    o["swa_mask"] = A(np.where(np.concatenate([k > q, k <= q], 1), 0.0, NEG).astype(np.float32))
    tok = np.tile(np.arange(TS), NJ)
    tb, tt = (tok // LS)[:, None], (tok % LS)[:, None]
    kb, ks = np.arange(TP)[None] // CH, np.arange(TP)[None] % CH
    nb_, nt = np.arange(TS)[None] // LS, np.arange(TS)[None] % LS
    o["swas_mask"] = A(np.where(np.concatenate([(kb == tb) & (ks > tt), (nb_ == tb) & (nt <= tt)], 1), 0.0, NEG).astype(np.float32))
    o["kcT"] = A(f["cache_win_k"][0].reshape(NB, CH, P).transpose(2, 0, 1))
    o["cwk"] = A(f["cache_win_k"][0].reshape(NB, CH, P))
    o["cwv"] = A(f["cache_win_v"][0].reshape(NB, CH, P))
    o["dn_hist"] = A(f["state_dn_conv"][0].reshape(NB, 3, 12, P).transpose(3, 2, 0, 1))
    o["ffn_hist"] = A(f["state_ffn_conv"][0].reshape(NB, 2, FT, P).transpose(3, 2, 0, 1))
    o["memT"] = A(f["mem_prompt"][0].T.reshape(KT, P, NM))
    o["mkT"] = A(f["cache_mem_k"][0].transpose(2, 3, 0, 1).reshape(NH, P, NB * NM))
    o["mv"] = A(f["cache_mem_v"][0].reshape(NB, 2, P, NH, P).transpose(3, 2, 0, 1, 4).reshape(NH, P, 2 * NB, P))
    rb = (np.arange(P) % TS) // LS
    o["xs_mask"] = np.where(rb[:, None] == np.arange(NB)[None], 0.0, NEG).astype(np.float32)
    o["s0"] = A(f["state_dn"][0])
    a_, b_ = np.arange(P)[:, None], np.arange(P)[None]
    lev = [((a_ >> l) == (b_ >> l)) & ((a_ >> (l - 1)) < (b_ >> (l - 1))) for l in range(1, LEVELS + 1)]
    o["d_mask"] = A(np.stack([(a_ <= b_) * 1.0, np.where(a_ <= b_, 0.0, NEG), np.where(b_ < a_, 0.0, NEG), lev[0].T * 1.0]
                             + [m * 1.0 for m in lev], 1).astype(np.float32))
    same = (a_ // LS) == (b_ // LS)
    sm = np.zeros((P, 6 * TS + NB), np.float32)
    for i, m in enumerate((same & (a_ <= b_), np.where(same & (a_ <= b_), 0.0, NEG), np.where(same & (b_ < a_), 0.0, NEG), same)):
        sm[:TS, TS * i:TS * i + TS] = m[:TS, :TS]
    sm[:TS, 6 * TS:] = (np.arange(TS)[:, None] // LS) == np.arange(NB)[None]
    o["ds_mask"] = sm
    return o


OUTS = {"yT": (KT, P, T), "p_mem_k": (NM, 512), "p_mem_v": (NM, 512), "ffn_tail": (P, FT, 18), "dn_tail": (P, 12, 27), "p_dn_state": (NH, P, P), "s_dn_state": (NB, NH, P, P), "p_win_k": (CH, P), "p_win_v": (CH, P), "s_win_k": (NB, CH, P), "s_win_v": (NB, CH, P)}


def kernel(**inputs):
    import numpy as np
    import concourse.bacc as bacc
    from concourse.bass_utils import run_bass_kernel_spmd

    nc = bacc.Bacc("TRN2", target_bir_lowering=False, num_devices=1)
    arrays, d = {}, {}
    for name, a in layouts(inputs).items():
        arrays["in_" + name] = a
        d[name] = nc.dram_tensor("in_" + name, a.shape, F32, kind="ExternalInput").ap()
    for name, shape in OUTS.items():
        d[name] = nc.dram_tensor("out_" + name, shape, F32, kind="ExternalOutput").ap()
    build(nc, d)
    r = run_bass_kernel_spmd(nc, [arrays], core_ids=[0]).results[0]
    o = {name: r["out_" + name] for name in OUTS}
    y = o["yT"].reshape(D, T).T
    dn, fn = o["dn_tail"], o["ffn_tail"]
    A = np.ascontiguousarray
    return (A(y[None, :TP]), A(y[TP:].reshape(NB, LS, D)),
            o["p_win_k"].reshape(1, 1, CH, 2, HD), o["p_win_v"].reshape(1, 1, CH, 2, HD),
            A(dn[:, :, 0:3].transpose(2, 1, 0).reshape(1, 1, 3, 12 * P)), o["p_dn_state"].reshape(1, 1, NH, P, P),
            o["p_mem_k"].reshape(1, 1, NM, NH, P), o["p_mem_v"].reshape(1, 1, NM, NH, P),
            A(fn[:, :, 0:2].transpose(2, 1, 0).reshape(1, 1, 2, FT * P)),
            o["s_win_k"].reshape(1, NB, CH, 2, HD), o["s_win_v"].reshape(1, NB, CH, 2, HD),
            A(dn[:, :, 3:].reshape(P, 12, NB, 3).transpose(2, 3, 1, 0).reshape(1, NB, 3, 12 * P)),
            o["s_dn_state"].reshape(1, NB, NH, P, P),
            A(fn[:, :, 2:].reshape(P, FT, NB, 2).transpose(2, 3, 1, 0).reshape(1, NB, 2, FT * P)))
```

```python
from contextlib import ExitStack

import concourse.bass as bass
from concourse import mybir

F32 = mybir.dt.float32
F32R = mybir.dt.float32r
ALU = mybir.AluOpType
ACT = mybir.ActivationFunctionType
AX = mybir.AxisListType

P = 128
D = 1024
KT = D // P
TP, NB, LS = 1024, 8, 4
TS = NB * LS
T = TP + TS
NCH = 3
CW = T // NCH
CH = 128
NBLK = TP // CH
HD = 64
NJ = 4
NH = 4
NM = 256
FT = 22
EPS = 1e-6
NEG = -1e30
PRE = 3 + TP + NB * 7
SLOT = KT * P

SLOTS = {}
_at = 0
for _name, _n in (("attn", 6), ("dn", 12), ("dz", 4), ("gate", 16), ("branch", 8), ("mix", 8),
                  ("xkv", 8), ("xq", 4), ("xo", 4), ("ffn", 66)):
    SLOTS[_name] = (_at, _n)
    _at += _n
NSLOTS = _at

CONST = {}
_at = 0
for _name, _n in (("w_ab", KT * 8), ("ident", P), ("ones", P), ("g_mix", KT), ("g_mem", KT), ("g_x", KT), ("g_ffn", KT),
                  ("g_out", KT), ("g_dn", 1), ("sinks", 8), ("sinks_s", 2), ("a_log", NH), ("dt_bias", NH),
                  ("dn_w", 12 * 4), ("ffn_w", FT * 3), ("eps", 1), ("l2_gain", 8)):
    CONST[_name] = (_at, _n)
    _at += _n
NCONST = _at


HALF_BANKS = ((5, 6), (7, 4))
SHALF_BANKS = ((7, None), (1, None))
LEVELS = 7


def front_steps():
    return {"dve": ["gu", "t1", "t2", "t3", "a1", "a2", "qk", "qd", "kbe", "kd", "vb"],
            "pe": ["bc", "kk", "kq", "kt", "vt"], "act": ["ks", "vs", "eg", "dt", "dd"]}


def inverse_steps(levels):
    dve, pe = ["x1a", "x1", "p1a", "p1b", "y1a", "y1b"], ["u1a", "u1b"]
    for l in range(2, levels + 1):
        dve += [f"p{l}a", f"p{l}b"]
        pe += [f"lp{l}a", f"lp{l}b"]
        for h in "ab":
            dve += [f"y{l}{h}"] + ([f"x{l}{h}"] if l < levels else [])
            pe += [f"lz{l}{h}"] + ([f"lx{l}{h}"] if l < levels else [])
    return {"dve": dve, "pe": pe, "act": []}


STAGES = {"front": front_steps(), "inverse": inverse_steps(LEVELS),
          "state": {"dve": ["s1", "s2"], "pe": ["wt", "vn", "o", "su"], "act": ["nw", "vn", "o"]}}
SDVE_STEPS, SPE_STEPS, SACT_STEPS = [front_steps()[e] + inverse_steps(2)[e] for e in ("dve", "pe", "act")]
SDVE_STEPS += [f"{x}{h}" for h in range(NH) for x in ("vm", "sa", "sb")]
SPE_STEPS += ["wt", "vnt", "vtok", "o"] + [f"su{h}" for h in range(NH)]
SACT_STEPS += ["nw", "vnt", "vn", "o"]


def at(steps, name, c=0):
    return c * len(steps) + steps.index(name) + 1


def build(nc, d):
    ctx = ExitStack()
    with ctx:
        def sb(name, shape, dt=F32):
            return ctx.enter_context(nc.sbuf_tensor(name, shape, dt))

        def sem(name):
            return ctx.enter_context(nc.semaphore(name))

        def wait(eng, s, v):
            if not (isinstance(v, int) and v <= 0):
                eng.wait_ge(s, v)

        def pairs(eng, n, body):
            body(0, 0)
            body(1, 1)
            if n > 2:
                with eng.Fori(1, n // 2) as i:
                    body(2 * i, 0)
                    body(2 * i + 1, 1)

        def overlay(name, shape):
            with nc.sbuf_tensor(name, shape, F32) as ap:
                return ap

        H = sb("H", [P, KT, T])
        X32 = overlay("X32", [P, 2 * KT, T])
        XH = sb("XH", [P, KT, T], F32R)
        XL = sb("XL", [P, KT, T], F32R)
        RAW = sb("RAW", [P, 2, SLOT])
        WH = sb("WH", [P, 2, SLOT], F32R)
        WL = sb("WL", [P, 2, SLOT], F32R)
        YA = sb("YA", [P, NJ, T])
        DV = sb("DV", [P, NH, T])
        TMP = sb("TMP", [P, 8 * T])
        CST = sb("CST", [P, NCONST])
        A32 = overlay("A32", [P, 4, T])
        AH = sb("AH", [P, 2, T], F32R)
        AL = sb("AL", [P, 2, T], F32R)
        PS = ctx.enter_context(nc.psum_tensor("PS", [P, 8, 512], F32))

        def cst(name):
            a, n = CONST[name]
            return CST[:, a:a + n]

        def acc(g):
            return PS[:, 3 * g:3 * g + 3, 0:CW]

        def wide(ap):
            return ap.rearrange("p (c n) -> p c n", c=NCH)

        ident, ones = cst("ident"), cst("ones")
        perm = TMP[:, 8 * T - P:8 * T]

        def norm_space(i):
            w_ = YA[:, :, :].rearrange("p a n -> p (a n)") if i in (1, 2) else TMP
            return w_[:, 0:2 * T].rearrange("p (b n) -> p b n", b=2), w_[:, 2 * T:3 * T], w_[:, 3 * T:4 * T]
        r_sin = TMP[:, 5 * T:5 * T + TP]
        r_sins = TMP[:, 6 * T:6 * T + 5 * TS].rearrange("p (t n) -> p t n", t=5)
        def carve(start):
            at = [start]

            def take(n, pat=None, **kw):
                ap = TMP[:, at[0]:at[0] + n]
                at[0] += n
                assert at[0] <= 8 * T
                return ap.rearrange(pat, **kw) if pat else ap
            return take
        take = carve(0)
        a_mask = take(2 * CH)
        a_q = take(2 * 2 * 512, "p (b g n) -> p b g n", b=2, g=2)
        a_vf = take(2 * CH, "p (b n) -> p b n", b=2)
        a_v = take(2 * CH, "p (b n) -> p b n", b=2)
        a_s = [take(8 * 256, "p (h n) -> p h n", h=8),
               H[:, 6:8, :].rearrange("p a n -> p (a n)")[:, 0:8 * 256].rearrange("p (h n) -> p h n", h=8)]
        a_pt = take(2 * 8 * CH, "p (s h n) -> p s h n", s=2, h=8)
        a_mx, a_nm, a_es, a_den = [take(2 * 8, "p (b n) -> p b n", b=2) for _ in range(4)]
        take = carve(256)
        s_s = take(2 * T, "p (g n) -> p g n", g=2)
        s_pt = take(9 * 256, "p (k g n) -> p k g n", k=9, g=2)
        s_v = take(CH)
        s_mx = take(2)
        s_nm = take(2)
        s_es = take(2)
        s_den = take(2)
        s_ktok = take(2 * CH, "p (b n) -> p b n", b=2)
        s_kc = DV[:, 0, 0:NB * CH].rearrange("p (b n) -> p b n", b=NB)
        s_vc = DV[:, 1, 0:NB * CH].rearrange("p (b n) -> p b n", b=NB)
        s_q = DV[:, 2, 0:CH]
        rope = H[:, 6:8, :]
        s_mask = DV[:, 3, :]

        take = carve(0)
        c_pre = take(2 * PRE, "p (b n) -> p b n", b=2)
        c_acc = take(2 * T, "p (b n) -> p b n", b=2)
        c_hist = take(12 * NB * 3, "p (t b n) -> p t b n", t=12, b=NB)
        c_tail = take(12 * 27, "p (t n) -> p t n", t=12)
        l_sq = [A32[:, i, 0:TP] for i in range(2)]
        l_sqs = TMP[:, 5 * T:5 * T + KT * TS].rearrange("p (t n) -> p t n", t=KT)
        o_sq = [c_acc[:, i % 2, :] for i in range(4)]
        o_rs = [TMP[:, 0:T], TMP[:, T:2 * T], TMP[:, 5 * T:6 * T], TMP[:, 6 * T:7 * T]]
        take = carve(0)
        bufs = [take(NH * P) for _ in range(12)]
        for spare, n_ in ((A32, 8), (RAW, 1)):
            flat = spare[:, :, :].rearrange("p a n -> p (a n)")
            bufs += [flat[:, NH * P * i:NH * P * i + NH * P] for i in range(n_)]
        bufs = [b.rearrange("p (h n) -> p h n", h=NH) for b in bufs]
        b_qd, b_a, b_qk, b_kbe, b_vb, b_kd, b_y = zip(bufs[1:8], bufs[12:19])
        b_p, b_ks, b_vs, b_x, b_s = [bufs[i] for i in (0, 8, 9, 10, 11)]
        b_nw, b_vn = bufs[19:21]
        d_mask = take(11 * P, "p (m n) -> p m n", m=11)
        m_ut, m_u, m_l, m_1l = [d_mask[:, i, :] for i in range(4)]
        m_lev = d_mask[:, 4:11, :]
        ds_mask = take(3 * TS + 3 * TS + NB)
        ms_ut, ms_u, ms_l, ms_blk = [ds_mask[:, TS * i:TS * i + TS] for i in range(4)]
        ms_b = ds_mask[:, 6 * TS:6 * TS + NB]
        S0 = H[:, 4:8, :].rearrange("p a n -> p (a n)")[:, 0:NB * NH * P].rearrange("p (b h v) -> p b h v", b=NB, h=NH)
        s_vm0 = TMP[:, 2 * 512:4 * 512]
        s_vm1 = TMP[:, 4 * 512:6 * 512]
        z_sb = A32
        s_ks = RAW[:, 1, 0:NH * TS].rearrange("p (h n) -> p h n", h=NH)
        SM = take(640)
        sm_at = [0]

        def small(n, pat=None, **kw):
            ap = SM[:, sm_at[0]:sm_at[0] + n]
            sm_at[0] += n
            return ap.rearrange(pat, **kw) if pat else ap
        NAB = 7 * 8 + P
        WABH, WABL = AH[:, 0, 0:NAB], AL[:, 0, 0:NAB]
        g_rows = A32[0:8, 3, :]
        g_ab = small(9 * 8, "p (c n) -> p c n", c=9)
        g_x, g_ax, g_e, g_l, g_g, g_beta, g_eb, g_c, g_ec, g_be, g_kds, g_t = [
            small(9 * NH, "p (c h) -> p c h", c=9) for _ in range(12)]
        g_gl = small(9 * NH, "p (c h) -> p c h", c=9)
        g_egl = small(NBLK * NH, "p (c h) -> p c h", c=NBLK)
        g_egs = small(NB * NH, "p (b h) -> p b h", b=NB)
        g_bm = small(NB * NH, "p (b h) -> p b h", b=NB)
        g_ea = small(NH)

        def ga(t):
            return H[:, 4 + t, :] if t < 4 else DV[:, t - 4, :]
        gb = lambda t: TMP[:, t * T:t * T + T]
        x_res = TMP[:, :].rearrange("p (k n) -> p k n", k=KT)
        dv_flat = DV[:, :, :].rearrange("p a n -> p (a n)")
        ya_flat = YA[:, :, :].rearrange("p a n -> p (a n)")
        m_x = dv_flat[:, 0:KT * NM].rearrange("p (k n) -> p k n", k=KT)
        MH, ML = [a_[:, :, :].rearrange("p a n -> p (a n)")[:, 0:KT * NM].rearrange("p (k n) -> p k n", k=KT)
                  for a_ in (AH, AL)]
        m_k, m_v = [dv_flat[:, 2048 + 1024 * i:3072 + 1024 * i].rearrange("p (m n) -> p m n", m=2) for i in range(2)]
        m_kT = dv_flat[:, 0:1024].rearrange("p (h n) -> p h n", h=NH)
        HQ = TMP[:, 0:4 * T].rearrange("p (h n) -> p h n", h=NH)
        take = carve(4 * T)
        x_q = take(2 * 512, "p (b h n) -> p b h n", b=2, h=NH)
        x_s = take(2 * NH * NM, "p (b h n) -> p b h n", b=2, h=NH)
        x_pt = take(2 * NH * CH, "p (m h n) -> p m h n", m=2, h=NH)
        take = carve(4 * T + 4096)
        x_nm = take(4 * NH, "p (b i h) -> p b i h", b=2, i=2)
        x_den = take(4 * NH, "p (b i h) -> p b i h", b=2, i=2)
        x_sm = take(NB)
        X_BANKS = (0, 5)
        x_ps = lambda h, p: PS[:, X_BANKS[p] + h // 2, NM * (h % 2):NM * (h % 2) + NM]
        take = carve(0)
        xs_pt = take(2 * NB * CH, "p (m n) -> p m n", m=2 * NB)
        take = carve(4 * T)
        xs_s = take(NB * NM)
        kc_buf = [ya_flat[:, 0:2048], ya_flat[:, 2048:4096]]
        vc_buf = []
        for bufs_, k in ((kc_buf, 4), (vc_buf, KT + 4)):
            flat = X32[:, k:k + 4, :].rearrange("p a n -> p (a n)")
            bufs_.extend([flat[:, 0:2048], flat[:, 2048:4096]])
        vc_buf += kc_buf[0:2]

        FPRE = 2 + TP + NB * 6
        take = carve(0)
        f_pre = take(2 * FPRE, "p (b n) -> p b n", b=2)
        f_act = take(2 * T, "p (b n) -> p b n", b=2)
        take = carve(5 * T)
        f_hist = take(FT * NB * 2, "p (t b n) -> p t b n", t=FT, b=NB)
        f_one = take(1)
        f_tail = take(FT * 18, "p (t n) -> p t n", t=FT)

        y_hi, y_lo, br_a, br_m, br_s, xres_in = [sem(x) for x in ("y_hi", "y_lo", "branch_a", "branch_mul", "branch_sum", "xres_in")]
        mem_in, kv_ok, kv_sb, mkt_ps, mkt_ok = [sem(x) for x in ("mem_in", "kv_ok", "kv_sb", "mkt_ps", "mkt_ok")]
        hq_ok = sem("hq_ok")
        xa_st, xa_sc, xa_mx, xa_exp, xa_den, xa_p, xa_tp, xa_pt, xa_pv, xa_hi, xa_lo = [
            sem("xattn_" + x) for x in ("stage", "scores", "max", "exp", "den", "probs", "ptr", "pt", "pv", "hi", "lo")]
        xs_in, xk_in, xv_in, xs_sc, xs_dv, xs_exp, xs_tp, xs_ptok, xs_pv = [
            sem("xattns_" + x) for x in ("mask_in", "k_in", "v_in", "scores", "dve", "exp", "ptr", "pt", "pv")]
        xo_a, xo_free = sem("xo_a"), sem("xo_free")
        f_in, f_z, fp_ok, fu_free, f_his, f_cv, f_silu, f_gate, f_hi, f_lo, f_down, fd_free = [
            sem("mlp_" + x) for x in ("in", "zero", "pre", "u_free", "hist", "cv", "silu", "gate", "hi", "lo", "down", "d_free")]
        y_fin = sem("y_final")
        dn_in, dm_in, s0_in = map(sem, ("dn_in", "dm_in", "s0_in"))
        c_pre_ok, c_his, c_cv, c_act = [sem("conv_" + x) for x in ("pre", "hist", "cv", "act")]
        l_sq_ok, l_ps, l_sd, l_iv, l_ok = [sem("l2_" + x) for x in ("sq", "ps", "std", "inv", "ok")]
        ab_w, ab_mm, ab_row = [sem("ab_" + x) for x in ("weights", "products", "rows")]
        gt_dve, gt_act, gt_pe = [sem("gates_" + x) for x in ("dve", "act", "pe")]
        delta_sem = {(stage, e): sem(f"delta_{stage}_{e}") for stage in STAGES for e in ("dve", "act", "pe")
                     if STAGES[stage][e]}

        def delta_wait(eng, e, name, c):
            stage = [x for x in STAGES if name in STAGES[x][e]][0]
            wait(eng, delta_sem[stage, e], at(STAGES[stage][e], name, c))

        sd_dve, sd_act, sd_pe = [sem("sdelta_" + x) for x in ("dve", "act", "pe")]
        gt_dve2, s_zero = sem("gt_dve2"), sem("state_zero")
        n_attn = 16 * (2 + 1 + 1 + 16)
        n_dn_state = n_attn + 48
        n_mem = n_dn_state + 32
        z_ok, z_y = sem("z_ok"), sem("z_y")
        const_in, rope_in, smask_in, kc_in = map(sem, ("const_in", "rope_in", "smask_in", "kc_in"))
        x_in = [sem(f"x_in{i}") for i in range(4)]
        raw_in = [sem("raw_in0"), sem("raw_in1")]
        w_hi, w_split, w_used = sem("w_hi"), sem("w_split"), sem("w_used")
        acc_free = sem("acc_free")
        nsq, nadd, nss, nln, nrs, nxn, nhi, nlo = [sem("norm_" + x) for x in ("sq", "add", "ss", "ln", "rs", "xn", "hi", "lo")]
        rot_ps, rot_t, rot_c, rot_x = [sem("rot_" + x) for x in ("ps", "t", "c", "x")]
        at_stage, at_sc, at_msk, at_mx, at_exp, at_es, at_den, at_p = [
            sem("swa_" + x) for x in ("stage", "scores", "masked", "max", "exp", "sinkexp", "den", "probs")]
        at_vt, at_tp, at_pt, at_pv, at_y, at_v = [sem("swa_" + x) for x in ("vtr", "ptr", "pt", "pv", "y", "v")]
        at_zero, pwv_out = sem("swa_zero"), sem("pwv_out")
        ss_q = sem("swas_q")
        ss_tr, ss_tok, ss_sc, ss_msk, ss_mx, ss_exp, ss_den, ss_p, ss_tp, ss_pt, ss_pv, ss_y = [
            sem("swas_" + x) for x in ("tr", "tok", "scores", "masked", "max", "exp", "den", "probs", "ptr", "pt",
                                       "pv", "y")]
        out_done = sem("out_done")
        n_out = [0]

        acc0 = {}
        n = 0
        for name in ("attn", "dn", "dz", "gate"):
            acc0[name] = n
            n += SLOTS[name][1]

        def norm_square(act, i, k, src, w):
            sq, ss, rs = norm_space(i)
            if k < 2:
                wait(act, nlo, 8 * i)
            else:
                act.wait_ge(nadd, 7 * i + max(1, k - 2))
            nc.scalar.activation(sq[:, k % 2, 0:w], src[:, k, :], ACT.Square).then_inc(nsq, 1)

        def norm_add(dve, i, k, w):
            sq, ss, rs = norm_space(i)
            dve.wait_ge(nsq, 8 * i + k + 1)
            if k == 1:
                wait(dve, nss, i)
                nc.vector.tensor_tensor(ss[:, 0:w], sq[:, 0, 0:w], sq[:, 1, 0:w], ALU.add).then_inc(nadd, 1)
            else:
                dve.wait_ge(nadd, 7 * i + k - 1)
                nc.vector.tensor_tensor(ss[:, 0:w], ss[:, 0:w], sq[:, k % 2, 0:w], ALU.add).then_inc(nadd, 1)

        def norm_acc(i):
            return PS[:, 6:7, 0:NM] if i == 1 else acc(1 if i == 2 else 0)

        def norm_sum(pe, i):
            sq, ss, rs = norm_space(i)
            pe.wait_ge(nadd, 7 * i + 7)
            ps = norm_acc(i)
            for c in range(ps.shape[1]):
                n = ps.shape[2]
                mm = nc.tensor.matmul(ps[:, c, :], ones, ss[:, c * n:c * n + n], start=True, stop=True)
            mm.then_inc(nss, 1)

        def norm_root(act, i, w):
            rs = norm_space(i)[2][:, 0:w]
            act.wait_ge(nss, i + 1)
            nc.scalar.activation(wide(rs) if w == T else rs.unsqueeze(1), norm_acc(i), ACT.Ln, scale=1.0 / D,
                                 bias=cst("eps")).then_inc(nln, 1)
            act.wait_ge(nln, i + 1)
            nc.scalar.activation(rs, rs, ACT.Exp, scale=-0.5).then_inc(nrs, 1)

        def norm_heads(act, i, hi, w):
            sq, ss, rs = norm_space(i)
            for k in range(KT):
                act.wait_ge(nxn, 8 * i + k + 1)
                nc.scalar.activation(hi[:, k, 0:w], sq[:, k % 2, 0:w], ACT.Copy).then_inc(nhi, 1)

        def norm_dve(dve, i, src, gain, hi, lo, w):
            xn, ss, rs = norm_space(i)
            dve.wait_ge(nrs, i + 1)

            def rest(k):
                dve.wait_ge(nhi, 8 * i + k + 1)
                nc.vector.tensor_tensor(lo[:, k, 0:w], xn[:, k % 2, 0:w], hi[:, k, 0:w].bitcast(F32),
                                        ALU.subtract).then_inc(nlo, 1)
            for k in range(KT):
                if k >= 2:
                    rest(k - 2)
                    dve.wait_ge(nlo, 8 * i + k - 1)
                nc.vector.scalar_tensor_tensor(xn[:, k % 2, 0:w], src[:, k, :], gain[:, k:k + 1], rs[:, 0:w],
                                               ALU.mult, ALU.mult).then_inc(nxn, 1)
            rest(KT - 2)
            rest(KT - 1)

        def gemm_tile(mm_g, p, k0, kn, off, xk0=0, ready=None):
            for k in range(kn):
                if ready is not None:
                    nc.tensor.wait_ge(ready[0], ready[1] + xk0 + k + 1)
                mm = gemm_part(mm_g, p, k, kn, off, xk0)
            return mm

        def gemm_part(mm_g, p, k, kn, off=0, xk0=0):
            for w_, x_ in ((WH, XH), (WH, XL), (WL, XH)):
                for c in range(NCH):
                    first = k == 0 and w_ is WH and x_ is XH
                    last = k == kn - 1 and w_ is WL
                    mm = nc.tensor.matmul(PS[:, 3 * mm_g + c, 0:CW], w_[:, p, off + k * P:off + (k + 1) * P],
                                          x_[:, xk0 + k, c * CW:(c + 1) * CW], start=first, stop=last)
            return mm

        def gemm_pe(pe, name, ready=None):
            s0, n = SLOTS[name]

            def body(t, p):
                pe.wait_ge(w_split, s0 + t + 1)
                wait(pe, acc_free, acc0[name] + (t - 1 if not (isinstance(t, int) and t < 2) else 0))
                gemm_tile(p, p, 0, KT, 0, ready=ready if isinstance(t, int) and t == 0 else None).then_inc(w_used, 1)
            pairs(pe, n, body)

        def FFN0(f):
            return SLOTS["ffn"][0] + 6 * f - (0 if isinstance(f, int) and f == 0 else 2)

        acc_free2 = sem("mix_free")
        def pipelined(eng, n, front, back):
            front(0, 0)
            back(0, 0, 2)
            back(1, 1, 2)
            with eng.Fori(1, n // 2 - 1) as i:
                back(2 * i, 0, 2)
                back(2 * i + 1, 1, 2)
            back(n - 2, 0, 1)
            back(n - 1, 1, 0)

        def delta_blocks(eng, body):
            body(0, 0, False, True)
            body(1, 1, True, True)
            with eng.Fori(1, NBLK // 2 - 1) as i:
                body(2 * i, 0, True, True)
                body(2 * i + 1, 1, True, True)
            body(NBLK - 2, 0, True, True)
            body(NBLK - 1, 1, True, False)

        block = ctx.enter_context(nc.Block())


        @block.sync
        def _(sp):
            def store(dst, src):
                n_out[0] += 16
                sp.dma_start(dst, src).then_inc(out_done, 16)

            sp.dma_start(CST[:, :], d["cst"]).then_inc(const_in, 16)
            for i in range(4):
                sp.dma_start(H[:, 2 * i:2 * i + 2, :], d["xT"][2 * i:2 * i + 2].rearrange("k p t -> p k t")).then_inc(x_in[i], 16)

            def loads(a, b):
                def load(n, p):
                    wait(sp, w_split, n - 1)
                    sp.dma_start(RAW[:, p, :], d["w"][n, :, :]).then_inc(raw_in[p], 16)
                if a == 0:
                    pairs(sp, b, load)
                else:
                    with sp.Fori(a // 2, b // 2) as i:
                        load(2 * i, 0)
                        load(2 * i + 1, 1)
            loads(0, 4)
            sp.dma_start(s_kc, d["kcT"]).then_inc(kc_in, 16)
            sp.dma_start(s_vc, d["cwv"].rearrange("b s c -> s b c")).then_inc(kc_in, 16)
            sp.dma_start(s_mask, d["swas_mask"]).then_inc(smask_in, 16)
            store(d["s_win_k"][:, 0:CH - LS, :], d["cwk"][:, LS:CH, :])
            store(d["s_win_v"][:, 0:CH - LS, :], d["cwv"][:, LS:CH, :])
            sp.wait_ge(nlo, 8)
            sp.dma_start(rope, d["rope"]).then_inc(rope_in, 16)
            sp.dma_start(a_mask, d["swa_mask"]).then_inc(rope_in, 16)
            sp.dma_start(perm, d["perm"]).then_inc(rope_in, 16)
            loads(4, 8)
            sp.wait_ge(at_v, 8)
            store(d["p_win_v"], a_v[:, 1, :])
            sp.wait_ge(out_done, n_out[0])
            sp.nop().then_inc(pwv_out, 1)
            sp.wait_ge(ss_tok, 3)
            store(d["p_win_k"], s_ktok[:, 0, :])
            for b in range(NB):
                store(d["s_win_k"][b, CH - LS:CH, :], s_ktok[LS * b:LS * b + LS, 1, :])
                store(d["s_win_v"][b, CH - LS:CH, :], s_v[LS * b:LS * b + LS, :])
            sp.wait_ge(ss_y, 1)
            sp.dma_start(ds_mask, d["ds_mask"]).then_inc(dm_in, 16)
            sp.dma_start(d_mask, d["d_mask"]).then_inc(dm_in, 16)
            sp.dma_start(c_hist, d["dn_hist"]).then_inc(dn_in, 16)
            loads(8, 20)
            sp.wait_ge(acc_free, acc0["dn"] + 12)
            store(d["dn_tail"], c_tail)
            sp.wait_ge(out_done, n_out[0])
            sp.wait_ge(sd_act, at(SACT_STEPS, "ks"))
            delta_wait(sp, "act", "ks", NBLK - 1)
            sp.dma_start(S0, d["s0"].rearrange("b h k v -> k b h v")).then_inc(s0_in, 16)
            delta_wait(sp, "dve", "s2", NBLK - 1)
            store(d["p_dn_state"].rearrange("h k v -> k h v"), b_s)
            sp.wait_ge(sd_pe, at(SPE_STEPS, "kt"))
            loads(20, 24)
            sp.wait_ge(sd_dve, at(SDVE_STEPS, "sb3"))
            store(d["s_dn_state"].rearrange("b h k v -> k b h v"), S0)
            loads(24, 48)
            sp.wait_ge(br_s, 8)
            sp.dma_start(x_res, d["xT"].rearrange("k p t -> p k t")).then_inc(xres_in, 16)
            sp.wait_ge(y_lo, 16)
            sp.dma_start(m_x, d["memT"].rearrange("k p t -> p k t")).then_inc(mem_in, 16)
            loads(48, 56)
            loads(56, 64)
            sp.wait_ge(kv_sb, 4)
            store(d["p_mem_k"].rearrange("(m p) n -> p m n", p=P), m_k)
            store(d["p_mem_v"].rearrange("(m p) n -> p m n", p=P), m_v)
            loads(64, 68)
            sp.wait_ge(w_used, SLOTS["xq"][0] + SLOTS["xq"][1])
            sp.dma_start(x_sm, d["xs_mask"]).then_inc(xs_in, 16)
            for h in range(4):
                sp.dma_start(kc_buf[h], d["mkT"][h, :, :]).then_inc(xk_in, 16)
            for h in range(4):
                if h >= 2:
                    sp.wait_ge(xs_sc, h - 1)
                sp.dma_start(vc_buf[h].rearrange("p (m n) -> p m n", n=P), d["mv"][h]).then_inc(xv_in, 16)
            loads(68, 72)
            sp.wait_ge(xa_lo, NBLK + 1)
            sp.dma_start(f_hist, d["ffn_hist"]).then_inc(f_in, 16)
            loads(72, NSLOTS)
            sp.wait_ge(fu_free, FT)
            store(d["ffn_tail"], f_tail)
            for k in range(KT):
                sp.wait_ge(y_fin, k + 1)
                store(d["yT"][k, :, :], H[:, k, :])
            sp.wait_ge(out_done, n_out[0])

        @block.gpsimd
        def _(pool):
            one = cst("ones")[:, 0:1].to_broadcast([P, SLOT])

            def split(n, p):
                pool.wait_ge(raw_in[p], 8 * (n - p) + 16)
                wait(pool, w_used, n - 1)
                nc.gpsimd.tensor_tensor(WH[:, p, :], RAW[:, p, :], one, ALU.mult).then_inc(w_hi, 1)
                pool.wait_ge(w_hi, n + 1)
                nc.gpsimd.tensor_tensor(WL[:, p, :], RAW[:, p, :], WH[:, p, :].bitcast(F32),
                                        ALU.subtract).then_inc(w_split, 1)
            pool.wait_ge(const_in, 16)
            pairs(pool, NSLOTS, split)

        @block.scalar
        def _(act):
            act.wait_ge(const_in, 16)
            for k in range(KT):
                if k % 2 == 0:
                    act.wait_ge(x_in[k // 2], 16)
                norm_square(act, 0, k, H, T)
            norm_root(act, 0, T)
            norm_heads(act, 0, XH, T)

            def attn_tile(t, p):
                act.wait_ge(w_used, t + 1)
                if isinstance(t, int) and t == 0:
                    act.wait_ge(nlo, 8)
                nc.scalar.activation(wide(H[:, t, :]), acc(p), ACT.Copy).then_inc(acc_free, 1)
            pairs(act, 6, attn_tile)

            def swa_front(c, p):
                wait(act, at_sc, 4 * c - 4)
                wait(act, at_vt, c - 1)
                if isinstance(c, int) and c == 0:
                    act.wait_ge(acc_free, 6)
                    act.wait_ge(rot_x, 6)
                    act.wait_ge(at_zero, 4)
                for g in range(2):
                    rows = slice(HD * g, HD * g + HD)
                    nc.scalar.activation(a_q[rows, p, g, :].rearrange("p (j n) -> p j n", j=NJ),
                                         H[rows, 0:NJ, bass.ts(c, CH)], ACT.Copy).then_inc(at_stage, 1)
                nc.scalar.activation(a_vf[:, p, :], H[:, 5, bass.ts(c, CH)], ACT.Copy).then_inc(at_stage, 1)

            def swa_out(c):
                act.wait_ge(at_pv, c + 1)
                nc.scalar.activation(YA[:, :, bass.ts(c, CH)], PS[:, 6, :].rearrange("p (j n) -> p j n", j=NJ),
                                     ACT.Copy).then_inc(at_y, 1)

            def swa_back(c, p, left):
                act.wait_ge(at_mx, 4 * c + 4)
                for h in range(8):
                    nc.scalar.activation(a_s[p][:, h, :], a_s[p][:, h, :], ACT.Exp, bias=a_nm[:, p, h:h + 1],
                                         accum_out=a_den[:, p, h:h + 1]).then_inc(at_exp, 1)
                nc.scalar.activation(a_es[:, p, :], a_es[:, p, :], ACT.Exp).then_inc(at_exp, 1)
                if not (isinstance(c, int) and c == 0):
                    swa_out(c - 1)
                act.wait_ge(at_vt, c + 1)
                nc.scalar.activation(a_v[:, p, :], PS[:, 7, 0:CH], ACT.Copy).then_inc(at_v, 1)
                if left == 2:
                    swa_front(c + 2, p)
                for b in range(4):
                    act.wait_ge(at_tp, 4 * c + b + 1)
                    nc.scalar.activation(a_pt[:, b // 2, 4 * (b % 2):4 * (b % 2) + 4, :],
                                         PS[:, 4 + b % 2, :].rearrange("p (h n) -> p h n", h=4),
                                         ACT.Copy).then_inc(at_pt, 1)
            swa_front(0, 0)
            pipelined(act, NBLK, lambda c, p: swa_front(1, 1), swa_back)
            swa_out(NBLK - 1)

            nc.scalar.activation(s_q.rearrange("p (j n) -> p j n", j=NJ), H[:, 0:NJ, TP:T], ACT.Copy).then_inc(ss_q, 1)
            act.wait_ge(ss_tr, 1)
            act.wait_ge(pwv_out, 1)
            nc.scalar.activation(s_ktok[:, 0, :], PS[:, 6, 0:CH], ACT.Copy).then_inc(ss_tok, 1)
            nc.scalar.activation(s_ktok[0:TS, 1, :], PS[0:TS, 6, CH:2 * CH], ACT.Copy).then_inc(ss_tok, 1)
            nc.scalar.activation(s_v[0:TS, :], PS[0:TS, 6, 2 * CH:3 * CH], ACT.Copy).then_inc(ss_tok, 1)
            def gate_rows(c):
                act.wait_ge(ab_mm, c + 1)
                nc.scalar.activation(g_rows[:, bass.ts(c, CW)], PS[0:8, (7, 6, 7)[c], 0:CW], ACT.Copy).then_inc(ab_row, 1)
            gate_rows(0)
            act.wait_ge(ss_mx, 4)
            for g in range(2):
                nc.scalar.activation(s_s[:, g, :], s_s[:, g, :], ACT.Exp, bias=s_nm[:, g:g + 1],
                                     accum_out=s_den[:, g:g + 1]).then_inc(ss_exp, 1)
            nc.scalar.activation(s_es, s_es, ACT.Exp).then_inc(ss_exp, 1)
            gate_rows(1)
            for b in range(4):
                act.wait_ge(ss_tp, b + 1)
                nc.scalar.activation(s_pt[:, 2 * b:2 * b + 2, :, :],
                                     PS[:, b, :].rearrange("p (k g n) -> p k g n", k=2, g=2),
                                     ACT.Copy).then_inc(ss_pt, 1)
            act.wait_ge(ss_tp, 5)
            nc.scalar.activation(s_pt[0:TS, 8, :, :], PS[0:TS, 4, 0:256].rearrange("p (g n) -> p g n", g=2),
                                 ACT.Copy).then_inc(ss_pt, 1)
            gate_rows(2)
            act.wait_ge(ss_pv, 1)
            nc.scalar.activation(YA[:, :, TP:T], PS[:, 5, 0:CH].rearrange("p (j n) -> p j n", j=NJ),
                                 ACT.Copy).then_inc(ss_y, 1)

            act.wait_ge(gt_pe, 1)
            act.wait_ge(gt_dve, 1)
            nc.scalar.activation(g_ab[:, 0:NBLK, :], PS[:, 6, 0:64].rearrange("p (c n) -> p c n", c=NBLK), ACT.Copy).then_inc(gt_act, 1)
            nc.scalar.activation(g_ab[0:TS, NBLK, :], PS[0:TS, 6, 64:72], ACT.Copy).then_inc(gt_act, 1)
            act.wait_ge(gt_dve, 4)
            nc.scalar.activation(g_e, g_ax, ACT.Exp, scale=-1.0).then_inc(gt_act, 1)
            nc.scalar.activation(g_eb, g_ab[:, :, 4:8], ACT.Exp, scale=-1.0).then_inc(gt_act, 1)
            nc.scalar.activation(g_ea, cst("a_log"), ACT.Exp).then_inc(gt_act, 1)
            act.wait_ge(gt_act, 3)
            nc.scalar.activation(g_l, g_e, ACT.Ln, bias=1.0).then_inc(gt_act, 1)
            def pre(t, p):
                act.wait_ge(w_used, SLOTS["dn"][0] + t + 1)
                wait(act, c_cv, 8 * (t - 1))
                if isinstance(t, int) and t == 0:
                    act.wait_ge(ss_pv, 1)
                a = acc(p)
                nc.scalar.activation(c_tail[:, t, 0:3], a[:, 2, TP - 2 * CW - 3:TP - 2 * CW], ACT.Copy).then_inc(c_pre_ok, 1)
                new = a[:, 2, TP - 2 * CW:CW].rearrange("p (b n) -> p b n", b=NB)
                nc.scalar.activation(c_tail[:, t, 3:27].rearrange("p (b n) -> p b n", b=NB), new[:, :, 1:4],
                                     ACT.Copy).then_inc(c_pre_ok, 1)
                nc.scalar.activation(c_pre[:, p, 3:3 + 2 * CW].rearrange("p (c n) -> p c n", c=2), a[:, 0:2, :],
                                     ACT.Copy).then_inc(c_pre_ok, 1)
                nc.scalar.activation(c_pre[:, p, 3 + 2 * CW:3 + TP], a[:, 2, 0:TP - 2 * CW], ACT.Copy).then_inc(c_pre_ok, 1)
                nc.scalar.activation(c_pre[:, p, 3 + TP:PRE].rearrange("p (b n) -> p b n", b=NB)[:, :, 3:7], new,
                                     ACT.Copy).then_inc(acc_free, 1)

            def silu(dst, t, p):
                act.wait_ge(c_cv, 8 * t + 8)
                nc.scalar.activation(dst, c_acc[:, p, :], ACT.Silu).then_inc(c_act, 1)
            def root(j, sums, rs):
                act.wait_ge(l_ps, j + 1)
                nc.scalar.activation(rs, sums, ACT.Ln, bias=cst("eps")).then_inc(l_sd, 1)
                act.wait_ge(l_sd, j + 1)
                nc.scalar.activation(rs, rs, ACT.Exp, scale=-0.5).then_inc(l_iv, 1)

            def tile_root(j, p):
                root(j, PS[:, 6:8, :], l_sq[p].rearrange("p (b n) -> p b n", b=2))
            pre(0, 0)
            pre(1, 1)
            act.wait_ge(gt_pe, 2)
            nc.scalar.activation(g_c[:, 0:NBLK, :], PS[:, 6, 128:160].rearrange("p (c h) -> p c h", c=NBLK), ACT.Copy).then_inc(gt_act, 1)
            nc.scalar.activation(g_c[0:TS, NBLK, :], PS[0:TS, 6, 160:164], ACT.Copy).then_inc(gt_act, 1)
            nc.scalar.activation(g_gl[:, 0:NBLK, :], PS[:, 6, 192:224].rearrange("p (c h) -> p c h", c=NBLK), ACT.Copy).then_inc(gt_act, 1)
            nc.scalar.activation(g_gl[0:TS, NBLK, :], PS[0:TS, 6, 224:228], ACT.Copy).then_inc(gt_act, 1)
            nc.scalar.activation(g_egl, PS[:, 6, 192:224].rearrange("p (c h) -> p c h", c=NBLK), ACT.Exp).then_inc(gt_act, 1)
            nc.scalar.activation(g_egs, PS[:, 6, 256:288].rearrange("p (b h) -> p b h", b=NB), ACT.Exp).then_inc(gt_act, 1)
            act.wait_ge(gt_dve, 11)
            act.wait_ge(gt_act, 12)
            nc.scalar.activation(g_ec, g_c, ACT.Exp).then_inc(gt_act, 1)
            nc.scalar.activation(g_kds, g_kds, ACT.Exp).then_inc(gt_act, 1)
            silu(H[:, 0, :], 0, 0)
            pre(2, 0)
            silu(H[:, 1, :], 1, 1)
            pre(3, 1)
            with act.Fori(1, 4) as i:
                for p in range(2):
                    silu(H[:, 2 * i + p, :], 2 * i + p, p)
                    pre(2 * i + p + 2, p)
                    tile_root(2 * i + p - 2, p)
            for t in range(8, 10):
                silu(DV[:, t - 8, :], t, t % 2)
                pre(t + 2, t % 2)
                tile_root(t - 2, t % 2)
            root(8, PS[:, 6, 0:KT * TS].rearrange("p (t n) -> p t n", t=KT), l_sqs)
            for t in range(10, 12):
                silu(DV[:, t - 8, :], t, t % 2)

            def rows_ln(i0, tiles, rs, scale, bias):
                for t in tiles:
                    act.wait_ge(l_ps, i0 + t + 1)
                    nc.scalar.activation(wide(rs[t]), acc(0), ACT.Ln, scale=scale(t),
                                         bias=bias(t)).then_inc(l_sd, 1)

            def rows_exp(i0, tiles, rs):
                for t in tiles:
                    act.wait_ge(l_sd, i0 + t + 1)
                    nc.scalar.activation(rs[t], rs[t], ACT.Exp, scale=-0.5).then_inc(l_iv, 1)

            act.wait_ge(out_done, n_attn + 16)
            act.wait_ge(c_act, 12)

            def dv(name, c): delta_wait(act, "dve", name, c)
            def pw(name, c): delta_wait(act, "pe", name, c)
            def done(stage, i): i.then_inc(delta_sem[stage, "act"], 1)
            heads = lambda bank: PS[:, bank, :].rearrange("p (h n) -> p h n", h=NH)

            def front_stage(c):
                first = isinstance(c, int) and c == 0
                if not first:
                    pw("kt", c - 1)
                    pw("vt", c - 1)
                done("front", nc.scalar.activation(b_ks, H[:, 4:8, bass.ts(c, CH)], ACT.Copy))
                done("front", nc.scalar.activation(b_vs, DV[:, :, bass.ts(c, CH)], ACT.Copy))

            def front_decays(c, p):
                pw("bc", c)
                dv("t1", c)
                done("front", nc.scalar.activation(b_qd[p], heads(0), ACT.Exp))
                dv("t2", c)
                done("front", nc.scalar.activation(b_qk[p], b_qk[p], ACT.Exp))
                dv("t3", c)
                done("front", nc.scalar.activation(b_a[p], b_a[p], ACT.Exp))

            def state(c):
                pw("wt", c)
                done("state", nc.scalar.activation(b_nw, heads(0), ACT.Copy, scale=-1.0))
                pw("vn", c)
                done("state", nc.scalar.activation(b_vn, heads(1), ACT.Copy))
                pw("o", c)
                done("state", nc.scalar.activation(H[:, 0:4, bass.ts(c, CH)], heads(2), ACT.Copy))

            def delta(c, p, before, after):
                if after:
                    front_stage(c + 1)
                if before:
                    state(c - 1)
                if after:
                    front_decays(c + 1, 1 - p)
            act.wait_ge(l_ok, 10)
            act.wait_ge(gt_dve, 13)
            act.wait_ge(w_split, SLOTS["dz"][0] + 2)
            nc.scalar.activation(s_ks, H[:, 4:8, TP:T], ACT.Copy).then_inc(sd_act, 1)
            front_stage(0)
            front_decays(0, 0)
            delta_blocks(act, delta)
            state(NBLK - 1)

            def sdone(i): i.then_inc(sd_act, 1)

            def z_gate(t):
                act.wait_ge(w_used, SLOTS["dz"][0] + t + 1)
                nc.scalar.activation(wide(z_sb[:, t, :]), acc(1), ACT.Silu).then_inc(acc_free, 1)
            r, tn = slice(0, TS), slice(TP, T)
            sb4 = lambda b: b[:, :, 0:TS]
            pw("su", NBLK - 1)
            act.wait_ge(gt_dve, 13)
            sdone(nc.scalar.activation(sb4(b_vs), DV[:, :, tn], ACT.Copy))
            act.wait_ge(sd_dve, at(SDVE_STEPS, "t1"))
            sdone(nc.scalar.activation(sb4(b_qd[0]), PS[:, 0, 0:P].rearrange("p (h n) -> p h n", h=NH), ACT.Exp))
            act.wait_ge(sd_dve, at(SDVE_STEPS, "t3"))
            sdone(nc.scalar.activation(b_qk[0][r, :, r], b_qk[0][r, :, r], ACT.Exp))
            sdone(nc.scalar.activation(b_a[0][r, :, r], b_a[0][r, :, r], ACT.Exp))
            act.wait_ge(sd_pe, at(SPE_STEPS, "wt"))
            sdone(nc.scalar.activation(sb4(b_ks), PS[:, 0, 0:P].rearrange("p (h n) -> p h n", h=NH), ACT.Copy, scale=-1.0))
            act.wait_ge(sd_pe, at(SPE_STEPS, "vnt"))
            sdone(nc.scalar.activation(sb4(b_vs), PS[:, 1, 0:P].rearrange("p (h n) -> p h n", h=NH), ACT.Copy))
            act.wait_ge(sd_pe, at(SPE_STEPS, "vtok"))
            z_gate(0)
            sdone(nc.scalar.activation(b_x[r, :, :], PS[r, 6, :].rearrange("p (h n) -> p h n", h=NH), ACT.Copy))
            act.wait_ge(sd_pe, at(SPE_STEPS, "o"))
            sdone(nc.scalar.activation(H[:, 0:4, tn], PS[:, 2, 0:P].rearrange("p (h n) -> p h n", h=NH), ACT.Copy))

            for t in range(1, 4):
                z_gate(t)
            act.wait_ge(out_done, n_attn + 32)
            rows_ln(9, range(4), o_rs, lambda t: 1.0 / P, lambda t: cst("eps"))
            rows_exp(9, range(4), o_rs)

            def gates(t0, n, dst):
                def gate(t, p):
                    act.wait_ge(w_used, SLOTS["gate"][0] + t0 + t + 1)
                    nc.scalar.activation(wide(dst(t)), acc(1 - p), ACT.Sigmoid).then_inc(acc_free, 1)
                pairs(act, n, gate)
            act.wait_ge(out_done, n_dn_state)
            gates(0, 4, lambda t: H[:, 4 + t, :])
            gates(4, 4, lambda t: DV[:, t, :])
            act.wait_ge(z_y, 4)
            gates(8, 8, lambda t: x_res[:, t, :])

            def split_heads(src, base):
                for k in range(KT):
                    nc.scalar.activation(XH[:, k, :], src(k), ACT.Copy).then_inc(y_hi, 1)
            split_heads(lambda k: YA[:, k, :] if k < 4 else H[:, k - 4, :], 0)
            act.wait_ge(w_used, SLOTS["branch"][0] + 8)
            act.wait_ge(br_s, 8)
            split_heads(ga, 8)

            act.wait_ge(y_lo, 16)
            act.wait_ge(mem_in, 16)
            for k in range(KT):
                norm_square(act, 1, k, m_x, NM)
            norm_root(act, 1, NM)
            norm_heads(act, 1, MH, NM)
            for k in range(KT):
                act.wait_ge(acc_free2, k + 1)
                norm_square(act, 2, k, H, T)
            def kv_out(n, m):
                act.wait_ge(w_used, SLOTS["xkv"][0] + 4 * n + 4)
                for i in range(2):
                    nc.scalar.activation(m[:, i, :], PS[:, 2 * n + i, :], ACT.Copy).then_inc(kv_sb, 1)
            kv_out(0, m_k)
            norm_root(act, 2, T)
            norm_heads(act, 2, XH, T)
            kv_out(1, m_v)
            act.wait_ge(mkt_ps, 1)
            for i in range(2):
                nc.scalar.activation(m_kT[:, :, CH * i:CH * i + CH], PS[:, 6 + i, :].rearrange("p (h n) -> p h n", h=NH),
                                     ACT.Copy).then_inc(mkt_ok, 1)
            act.wait_ge(mkt_ok, 2)
            for t in range(4):
                act.wait_ge(w_used, SLOTS["xq"][0] + t + 1)
                if t == 0:
                    act.wait_ge(nlo, 24)
                nc.scalar.activation(wide(HQ[:, t, :]), acc(t % 2), ACT.Copy).then_inc(hq_ok, 1)
            act.wait_ge(hq_ok, 4)
            xscale = float(P) ** -0.5

            def xattn_stage(c, p):
                nc.scalar.activation(x_q[:, p, :, :], HQ[:, :, bass.ts(c, CH)], ACT.Copy).then_inc(xa_st, 1)

            def xattn_out(c):
                act.wait_ge(xa_pv, c + 1)
                nc.scalar.activation(XH[:, 0:4, bass.ts(c, CH)], PS[:, 4, :].rearrange("p (h n) -> p h n", h=NH),
                                     ACT.Copy).then_inc(xa_hi, 1)

            def xattn_back(c, p, left):
                act.wait_ge(xa_mx, 4 * c + 4)
                wait(act, xa_tp, 2 * (c - 1))
                wait(act, xa_den, c - 1)
                for h in range(NH):
                    nc.scalar.activation(x_s[:, p, h, :], x_ps(h, p), ACT.Exp, scale=xscale,
                                         bias=x_nm[:, p, 1, h:h + 1], accum_out=x_den[:, p, 0, h:h + 1]).then_inc(xa_exp, 1)
                if not (isinstance(c, int) and c == 0):
                    xattn_out(c - 1)
                if left == 2:
                    xattn_stage(c + 2, p)
                for i in range(2):
                    act.wait_ge(xa_tp, 2 * c + i + 1)
                    nc.scalar.activation(x_pt[:, i, :, :], PS[:, 2 + i, :].rearrange("p (h n) -> p h n", h=NH), ACT.Copy).then_inc(xa_pt, 1)
            xattn_stage(0, 0)
            pipelined(act, NBLK, lambda c, p: xattn_stage(1, 1), xattn_back)
            xattn_out(NBLK - 1)
            act.wait_ge(xs_dv, 3)
            nc.scalar.activation(xs_s, xs_s, ACT.Exp, scale=xscale, bias=x_nm[:, 0, 1, 0:1],
                                 accum_out=x_den[:, 0, 0, 0:1]).then_inc(xs_exp, 1)
            for q in range(4):
                act.wait_ge(xs_tp, q + 1)
                if q == 0:
                    act.wait_ge(xs_sc, 4)
                nc.scalar.activation(xs_pt[:, 4 * q:4 * q + 4, :], PS[:, 4 + q % 2, :].rearrange("p (m n) -> p m n", m=4),
                                     ACT.Copy).then_inc(xs_ptok, 1)
            act.wait_ge(xs_pv, 1)
            nc.scalar.activation(XH[:, 0:4, TP:T], PS[:, 6, 0:P].rearrange("p (h n) -> p h n", h=NH), ACT.Copy).then_inc(xa_hi, 1)

            for k in range(KT):
                act.wait_ge(xo_free, k + 1)
                norm_square(act, 3, k, H, T)
            norm_root(act, 3, T)
            norm_heads(act, 3, XH, T)
            act.wait_ge(nlo, 32)
            act.wait_ge(f_z, 1)

            def mlp_u(f, i):
                t = 2 * f + i
                act.wait_ge(w_used, FFN0(f) + i + 1)
                wait(act, f_cv, 6 * t - 6)
                a = acc(i)
                k = TP - 2 * CW
                new = a[:, 2, k:CW].rearrange("p (b n) -> p b n", b=NB)
                nc.scalar.activation(f_tail[:, t, 0:2], a[:, 2, k - 2:k], ACT.Copy).then_inc(fp_ok, 1)
                nc.scalar.activation(f_tail[:, t, 2:18].rearrange("p (b n) -> p b n", b=NB), new[:, :, 2:4], ACT.Copy).then_inc(fp_ok, 1)
                nc.scalar.activation(f_pre[:, i, 2:2 + 2 * CW].rearrange("p (c n) -> p c n", c=2), a[:, 0:2, :], ACT.Copy).then_inc(fp_ok, 1)
                nc.scalar.activation(f_pre[:, i, 2 + 2 * CW:2 + TP], a[:, 2, 0:k], ACT.Copy).then_inc(fp_ok, 1)
                nc.scalar.activation(f_pre[:, i, 2 + TP:FPRE].rearrange("p (b n) -> p b n", b=NB)[:, :, 2:6], new,
                                     ACT.Copy).then_inc(fu_free, 1)

            def mlp_act(f):
                for i in range(2):
                    mlp_u(f, i)
                for i in range(2):
                    act.wait_ge(f_cv, 12 * f + 6 * i + 6)
                    nc.scalar.activation(f_act[:, i, :], f_act[:, i, :], ACT.Silu).then_inc(f_silu, 1)
                for i in range(2):
                    act.wait_ge(f_gate, 2 * f + i + 1)
                    if i == 0 and not (isinstance(f, int) and f == 0):
                        act.wait_ge(w_used, FFN0(f) + 6)
                    nc.scalar.activation(AH[:, i, :], f_act[:, i, :], ACT.Copy).then_inc(f_hi, 1)
            mlp_act(0)
            with act.Fori(1, FT // 2) as f:
                mlp_act(f)
            for k in range(KT):
                act.wait_ge(fd_free, 4 * (FT - 2) + k + 3)
                norm_square(act, 4, k, H, T)
            norm_root(act, 4, T)

        @block.tensor
        def _(pe):
            pe.wait_ge(const_in, 16)
            norm_sum(pe, 0)
            pe.wait_ge(nln, 1)

            def swap(t):
                pe.wait_ge(acc_free, t + 1)
                wait(pe, rot_t, t)
                for c in range(2):
                    mm = nc.tensor.matmul(PS[:, 6 + c, :], perm, H[:, t, bass.ts(c, 512)], start=True, stop=True)
                mm.then_inc(rot_ps, 1)

            for t in range(6):
                pe.wait_ge(w_split, t + 1)
                wait(pe, acc_free, t - 1)
                if t == 1:
                    pe.wait_ge(rope_in, 48)
                for k in range(KT):
                    if t == 0:
                        pe.wait_ge(nlo, k + 1)
                    mm = gemm_part(t % 2, t % 2, k, KT)
                    if k == 4 and t >= 1:
                        swap(t - 1)
                mm.then_inc(w_used, 1)
            pe.wait_ge(rot_t, 5)
            nc.tensor.matmul(PS[:, 6, 0:5 * TS], perm, H[:, 0:5, TP:T], start=True, stop=True).then_inc(rot_ps, 1)

            def swa_front(c, p):
                pe.wait_ge(at_stage, 3 * c + 3)
                if isinstance(c, int) and c == 0:
                    pe.wait_ge(acc_free, 6)
                    pe.wait_ge(rot_t, 6)
                for b in range(4):
                    wait(pe, at_msk, 4 * (c - 1) + b + 1)
                    for h in (2 * b, 2 * b + 1):
                        q = a_q[:, p, h // 4, (h % 4) * CH:(h % 4) * CH + CH]
                        o = (h % 2) * 2 * CH
                        if isinstance(c, int) and c == 0:
                            mm = nc.tensor.matmul(PS[:, b, o + CH:o + 2 * CH], q, H[:, 4, 0:CH], start=True, stop=True)
                        else:
                            mm = nc.tensor.matmul(PS[:, b, o:o + 2 * CH], q, H[:, 4, bass.ds((c - 1) * CH, 2 * CH)],
                                                  start=True, stop=True)
                    mm.then_inc(at_sc, 1)
                wait(pe, at_v, c)
                nc.tensor.transpose(PS[:, 7, 0:CH], a_vf[:, p, :], ident).then_inc(at_vt, 1)

            def swa_back(c, p, left):
                if left:
                    swa_front(c + 1, 1 - p)
                pe.wait_ge(at_p, c + 1)
                for b in range(4):
                    wait(pe, at_pt, 4 * c + b - 1)
                    for i in range(4):
                        s, h = (4 * b + i) // 8, (4 * b + i) % 8
                        mm = nc.tensor.transpose(PS[:, 4 + b % 2, i * CH:i * CH + CH], a_s[p][:, h, s * CH:s * CH + CH], ident)
                    mm.then_inc(at_tp, 1)
                pe.wait_ge(at_pt, 4 * c + 4)
                pe.wait_ge(at_v, c + 1)
                wait(pe, at_y, c)
                for g in range(2):
                    for s in range(2):
                        mm = nc.tensor.matmul(PS[HD * g:HD * g + HD, 6, :], a_v[:, (1 - p, p)[s], HD * g:HD * g + HD],
                                              a_pt[:, s, 4 * g:4 * g + 4, :], start=(s == 0), stop=(s == 1))
                mm.then_inc(at_pv, 1)
            pipelined(pe, NBLK, swa_front, swa_back)

            pe.wait_ge(at_y, NBLK)
            nc.tensor.transpose(PS[:, 6, 0:CH], H[:, 4, TP - CH:TP], ident)
            nc.tensor.transpose(PS[0:TS, 6, CH:2 * CH], H[:, 4, TP:T], ident)
            nc.tensor.transpose(PS[0:TS, 6, 2 * CH:3 * CH], H[:, 5, TP:T], ident).then_inc(ss_tr, 1)
            pe.wait_ge(kc_in, 32)
            pe.wait_ge(ss_q, 1)
            for g in range(2):
                rows = slice(HD * g, HD * g + HD)
                q = s_q[rows, :]
                nc.tensor.matmul(PS[:, 3 * g, :], q, s_kc[rows, 0:4, :], start=True, stop=True)
                nc.tensor.matmul(PS[:, 3 * g + 1, :], q, s_kc[rows, 4:8, :], start=True, stop=True)
                nc.tensor.matmul(PS[:, 3 * g + 2, 0:TS], q, H[rows, 4, TP:T], start=True, stop=True).then_inc(ss_sc, 1)
            def gate_products(c):
                for k in range(KT):
                    for n, (x_, w_) in enumerate(((XH, WABH), (XL, WABH), (XH, WABL))):
                        mm = nc.tensor.matmul(PS[:, (7, 6, 7)[c], 0:CW], w_[:, 8 * k:8 * k + P], x_[:, k, bass.ts(c, CW)],
                                              start=(k == 0 and n == 0), stop=(k == KT - 1 and n == 2))
                mm.then_inc(ab_mm, 1)
            pe.wait_ge(ab_w, 2)
            pe.wait_ge(at_v, NBLK)
            gate_products(0)
            pe.wait_ge(ss_tok, 3)
            gate_products(1)
            pe.wait_ge(ss_p, 1)
            for k in range(NB + 1):
                rows = CH if k < NB else TS
                for g in range(2):
                    i = 2 * k + g
                    mm = nc.tensor.transpose(PS[0:rows, i // 4, (i % 4) * CH:(i % 4) * CH + CH],
                                             s_s[:, g, k * CH:k * CH + rows], ident)
                if k % 2 or k == NB:
                    mm.then_inc(ss_tp, 1)
            pe.wait_ge(ab_row, 1)
            gate_products(2)
            pe.wait_ge(ss_pt, 5)
            for g in range(2):
                for k in range(NB):
                    nc.tensor.matmul(PS[HD * g:HD * g + HD, 5, 0:CH], s_vc[:, k, HD * g:HD * g + HD], s_pt[:, k, g, :],
                                     start=(k == 0), stop=False)
                mm = nc.tensor.matmul(PS[HD * g:HD * g + HD, 5, 0:CH], s_v[0:TS, HD * g:HD * g + HD],
                                      s_pt[0:TS, NB, g, :], start=False, stop=True)
            mm.then_inc(ss_pv, 1)

            pe.wait_ge(ab_row, 3)
            for c in range(NBLK):
                nc.tensor.transpose(PS[:, 6, 8 * c:8 * c + 8], g_rows[:, bass.ts(c, CH)], ident[0:8, 0:8])
            nc.tensor.transpose(PS[0:TS, 6, 64:72], g_rows[:, TP:T], ident[0:8, 0:8]).then_inc(gt_pe, 1)
            pe.wait_ge(ss_y, 1)
            pe.wait_ge(ss_pt, 5)
            def dn_tile(t, p, norm):
                pe.wait_ge(w_split, SLOTS["dn"][0] + t + 1)
                pe.wait_ge(acc_free, acc0["dn"] + (t - 1 if not (isinstance(t, int) and t < 2) else 0))
                for k in range(KT):
                    mm = gemm_part(p, p, k, KT)
                    if norm and k == KT // 2:
                        j = t - 4
                        pe.wait_ge(l_sq_ok, j + 1)
                        pe.wait_ge(gt_act, 12)
                        wait(pe, l_sd, j)
                        for c in range(2):
                            ms = nc.tensor.matmul(PS[:, 6 + c, :], ones, l_sq[p][:, bass.ts(c, 512)], start=True, stop=True)
                        ms.then_inc(l_ps, 1)
                mm.then_inc(w_used, 1)
            dn_tile(0, 0, False)
            dn_tile(1, 1, False)
            pe.wait_ge(dm_in, 32)
            pe.wait_ge(gt_dve, 10)
            gp = g_g[:, 0:NBLK, :].rearrange("p c h -> p (c h)")
            nc.tensor.matmul(PS[:, 6, 128:160], m_ut, gp, start=True, stop=True)
            nc.tensor.matmul(PS[0:TS, 6, 160:164], ms_ut[0:TS, :], g_g[0:TS, NBLK, :], start=True, stop=True)
            nc.tensor.matmul(PS[:, 6, 192:224], ones, gp, start=True, stop=True)
            nc.tensor.matmul(PS[0:TS, 6, 224:228], ms_blk[0:TS, :], g_g[0:TS, NBLK, :], start=True, stop=True)
            nc.tensor.matmul(PS[:, 6, 256:288], ones[0:TS, :], g_bm[0:TS, :, :].rearrange("p b h -> p (b h)"),
                             start=True, stop=True).then_inc(gt_pe, 1)
            dn_tile(2, 0, False)
            dn_tile(3, 1, False)
            dn_tile(4, 0, True)
            dn_tile(5, 1, True)
            with pe.Fori(3, 6) as i:
                dn_tile(2 * i, 0, True)
                dn_tile(2 * i + 1, 1, True)
            pe.wait_ge(l_sq_ok, 9)
            pe.wait_ge(l_sd, 8)
            nc.tensor.matmul(PS[:, 6, 0:KT * TS], ones, l_sqs.rearrange("p t n -> p (t n)"), start=True, stop=True).then_inc(l_ps, 1)

            def rows_norm(i0, n, groups, sq):
                for t in range(n):
                    pe.wait_ge(l_sq_ok, i0 + t + 1)
                    wait(pe, l_sd, i0 + t + 1 - groups if t + 1 > groups else 0)
                    for c in range(NCH):
                        mm = nc.tensor.matmul(PS[:, 3 * (t % groups) + c, 0:CW], ones, sq[t][:, bass.ts(c, CW)],
                                              start=True, stop=True)
                    mm.then_inc(l_ps, 1)
            pe.wait_ge(acc_free, acc0["dn"] + 12)

            def invert(levels, r, n, dv, done, p, side):
                def part(i, bank, lhs, rhs):
                    for j in range(2):
                        h = 2 * i + j
                        mm = nc.tensor.matmul(PS[r, bank, n * j:n * j + n], lhs(h), rhs(h), start=True, stop=True)
                    done(mm)
                A_, P_ = (lambda h: b_a[p][r, h, r]), (lambda h: b_p[r, h, r])
                X_, Y_ = (lambda h: b_x[r, h, r]), (lambda h: b_y[p][r, h, r])
                halves = [(i, "ab"[i], (HALF_BANKS if n == P else SHALF_BANKS)[i]) for i in range(2)]
                dv("a2")
                for i, nm, (b0, b1) in halves:
                    part(i, b0, A_, lambda h: ident[r, r])
                side(1)
                for l in range(2, levels + 1):
                    for i, nm, (b0, b1) in halves:
                        dv(f"y{l - 1}{nm}")
                        part(i, b0, A_, Y_)
                    side(l)
                    for i, nm, (b0, b1) in halves:
                        dv(f"p{l}{nm}")
                        part(i, b0, X_, P_)
                        if l < levels:
                            part(i, b1, P_, X_)
                dv(f"y{levels}b")

            def dv(name, c): delta_wait(pe, "dve", name, c)
            def aw(name, c): delta_wait(pe, "act", name, c)
            def done(stage, i): i.then_inc(delta_sem[stage, "pe"], 1)

            def each(stage, bank, lhs, rhs):
                for h in range(NH):
                    mm = nc.tensor.matmul(PS[:, bank, P * h:P * h + P], lhs(h), rhs(h), start=True, stop=True)
                done(stage, mm)

            def front(part, c, p):
                first = isinstance(c, int) and c == 0
                if part == "bc":
                    dv("gu", c)
                    if not first:
                        dv("vb", c - 1)
                    done("front", nc.tensor.matmul(PS[:, 0, :], ones, b_kbe[p].rearrange("p h n -> p (h n)"), start=True, stop=True))
                elif part == "kk":
                    aw("ks", c)
                    each("front", 1, lambda h: b_ks[:, h, :], lambda h: b_ks[:, h, :])
                elif part == "kq":
                    each("front", 2, lambda h: b_ks[:, h, :], lambda h: H[:, h, bass.ts(c, CH)])
                elif part == "kt":
                    for h in range(NH):
                        mm = nc.tensor.transpose(PS[:, 3, P * h:P * h + P], b_ks[:, h, :], ident)
                    done("front", mm)
                elif part == "vt":
                    aw("vs", c)
                    dv("t1", c)
                    aw("eg", c)
                    for h in range(NH):
                        mm = nc.tensor.transpose(PS[:, 0, P * h:P * h + P], b_vs[:, h, :], ident)
                    done("front", mm)

            def state(part, c, p):
                if part == "wt":
                    dv("y7b", c)
                    if not (isinstance(c, int) and c == NBLK - 1):
                        dv("vb", c + 1)
                    each("state", 0, lambda h: b_kbe[p][:, h, :], lambda h: b_y[p][:, h, :])
                elif part == "vn":
                    aw("nw", c)
                    if not (isinstance(c, int) and c == 0):
                        dv("s2", c - 1)
                    else:
                        pe.wait_ge(s_zero, 1)
                    for h in range(NH):
                        o = PS[:, 1, P * h:P * h + P]
                        nc.tensor.matmul(o, b_y[p][:, h, :], b_vb[p][:, h, :], start=True, stop=False)
                        mm = nc.tensor.matmul(o, b_nw[:, h, :], b_s[:, h, :], start=False, stop=True)
                    done("state", mm)
                elif part == "o":
                    aw("vn", c)
                    for h in range(NH):
                        o = PS[:, 2, P * h:P * h + P]
                        nc.tensor.matmul(o, b_s[:, h, :], b_qd[p][:, h, :], start=True, stop=False)
                        mm = nc.tensor.matmul(o, b_vn[:, h, :], b_qk[p][:, h, :], start=False, stop=True)
                    done("state", mm)
                elif part == "su":
                    each("state", 3, lambda h: b_kd[p][:, h, :], lambda h: b_vn[:, h, :])

            def delta(c, p, before, after):
                def side(l):
                    if before and l == 1:
                        state("wt", c - 1, 1 - p)
                    if before and l == 2:
                        state("vn", c - 1, 1 - p)
                    if after and l == 3:
                        front("bc", c + 1, 1 - p)
                    if before and l == 3:
                        state("o", c - 1, 1 - p)
                    if before and l == 4:
                        state("su", c - 1, 1 - p)
                    if after and l == 4:
                        front("kk", c + 1, 1 - p)
                    if after and l == 5:
                        if before:
                            aw("o", c - 1)
                        front("kq", c + 1, 1 - p)
                    if after and l == 6:
                        if before:
                            dv("s2", c - 1)
                        front("kt", c + 1, 1 - p)
                    if after and l == 7:
                        front("vt", c + 1, 1 - p)
                invert(LEVELS, slice(0, P), P, lambda name: dv(name, c), lambda mm: done("inverse", mm), p, side)
            pe.wait_ge(l_sd, 9)
            pe.wait_ge(gt_act, 14)
            for part in ("bc", "kk", "kq", "kt", "vt"):
                front(part, 0, 0)
            delta_blocks(pe, delta)
            for part in ("wt", "vn", "o", "su"):
                state(part, NBLK - 1, 1)

            r, tn = slice(0, TS), slice(TP, T)
            def sdv(name): pe.wait_ge(sd_dve, at(SDVE_STEPS, name))
            def saw(name): pe.wait_ge(sd_act, at(SACT_STEPS, name))
            def seach(bank, rows, width, lhs, rhs):
                for h in range(NH):
                    mm = nc.tensor.matmul(PS[rows, bank, width * h:width * h + width], lhs(h), rhs(h), start=True, stop=True)
                mm.then_inc(sd_pe, 1)

            def z_parts(a, b):
                for u in range(a, b):
                    t, k = u // KT, u % KT
                    if k == 0:
                        pe.wait_ge(w_split, SLOTS["dz"][0] + t + 1)
                        if t:
                            pe.wait_ge(acc_free, acc0["dz"] + t)
                    mm = gemm_part(1, t % 2, k, KT)
                    if k == KT - 1:
                        mm.then_inc(w_used, 1)
            sdv("gu")
            aw("o", NBLK - 1)
            dv("s2", NBLK - 1)
            nc.tensor.matmul(PS[:, 0, 0:P].rearrange("p (h n) -> p h n", h=NH), ones[r, :], b_kbe[0][r, :, r], start=True, stop=True).then_inc(sd_pe, 1)
            saw("ks")
            seach(1, r, TS, lambda h: s_ks[:, h, :], lambda h: s_ks[:, h, :])
            seach(2, r, TS, lambda h: s_ks[:, h, :], lambda h: H[:, h, tn])
            for h in range(NH):
                mm = nc.tensor.transpose(PS[r, 6, P * h:P * h + P], s_ks[:, h, :], ident)
            mm.then_inc(sd_pe, 1)
            z_parts(0, 2)
            saw("vs")
            sdv("t1")
            saw("eg")
            for h in range(NH):
                mm = nc.tensor.transpose(PS[r, 0, P * h:P * h + P], b_vs[:, h, r], ident)
            mm.then_inc(sd_pe, 1)
            z_parts(2, 3)
            invert(2, r, TS, sdv, lambda mm: mm.then_inc(sd_pe, 1), 0, lambda l: z_parts(2 + l, 3 + l))
            z_parts(5, 6)
            sdv("vb")
            seach(0, slice(0, P), TS, lambda h: b_kbe[0][r, h, :], lambda h: b_y[0][r, h, r])
            z_parts(6, 7)
            saw("nw")
            pe.wait_ge(s0_in, 16)
            for h in range(NH):
                nc.tensor.matmul(PS[:, 1, TS * h:TS * h + TS], b_vb[0][r, h, :], b_y[0][r, h, r], start=True, stop=False)
                for b in range(NB):
                    o = slice(LS * b, LS * b + LS)
                    mm = nc.tensor.matmul(PS[:, 1, TS * h + LS * b:TS * h + LS * b + LS], S0[:, b, h, :], b_ks[:, h, o],
                                          start=False, stop=(b == NB - 1))
            mm.then_inc(sd_pe, 1)
            z_parts(7, 8)
            saw("vnt")
            for h in range(NH):
                mm = nc.tensor.transpose(PS[r, 6, P * h:P * h + P], b_vs[:, h, r], ident)
            mm.then_inc(sd_pe, 1)
            z_parts(8, 10)
            saw("vn")
            for h in range(NH):
                nc.tensor.matmul(PS[:, 2, TS * h:TS * h + TS], b_x[r, h, :], b_qk[0][r, h, r], start=True, stop=False)
                for b in range(NB):
                    o = slice(LS * b, LS * b + LS)
                    mm = nc.tensor.matmul(PS[:, 2, TS * h + LS * b:TS * h + LS * b + LS], S0[:, b, h, :], b_qd[0][:, h, o],
                                          start=False, stop=(b == NB - 1))
            mm.then_inc(sd_pe, 1)
            for h in range(NH):
                z_parts(10 + 3 * h, 13 + 3 * h)
                sdv(f"vm{h}")
                vm = (s_vm0, s_vm1)[h % 2]
                if h >= 2:
                    sdv(f"sb{h - 2}")
                for q in range(2):
                    mm = nc.tensor.matmul(PS[:, 6 * (h % 2) + q, :], b_kd[0][r, h, :], vm[r, 512 * q:512 * q + 512],
                                          start=True, stop=True)
                mm.then_inc(sd_pe, 1)
            z_parts(22, 4 * KT)

            def gate_tile(t, p):
                pe.wait_ge(w_split, SLOTS["gate"][0] + t + 1)
                pe.wait_ge(acc_free, acc0["gate"] + (t - 1 if not (isinstance(t, int) and t < 2) else 0))
                gemm_tile(1 - p, p, 0, KT, 0).then_inc(w_used, 1)
            gate_tile(0, 0)
            rows_norm(9, 4, 1, o_sq)
            pe.wait_ge(l_sd, 13)
            gate_tile(1, 1)
            with pe.Fori(1, SLOTS["gate"][1] // 2) as i:
                gate_tile(2 * i, 0)
                gate_tile(2 * i + 1, 1)
            pe.wait_ge(acc_free, acc0["gate"] + 16)

            def branch(t, p):
                pe.wait_ge(w_split, SLOTS["branch"][0] + t + 1)
                wait(pe, br_m, 2 * t - 1)
                ready = (y_lo, 0) if isinstance(t, int) and t == 0 else None
                gemm_tile(0, p, 0, 4, 0, ready=ready).then_inc(br_a, 1)
                wait(pe, br_m, 2 * t)
                gemm_tile(1, p, 4, 4, 4 * P, 4, ready=ready).then_inc(w_used, 1)
            pairs(pe, 8, branch)
            pe.wait_ge(br_m, 16)

            def simple(name, free, ready):
                def body(t, p):
                    pe.wait_ge(w_split, SLOTS[name][0] + t + 1)
                    wait(pe, free, t - 1)
                    gemm_tile(p, p, 0, KT, 0, ready=ready if isinstance(t, int) and t == 0 else None).then_inc(w_used, 1)
                pairs(pe, SLOTS[name][1], body)
            def mix_tile(t, p):
                pe.wait_ge(w_split, SLOTS["mix"][0] + t + 1)
                wait(pe, acc_free2, t - 1)
                gemm_tile(p, p, 0, KT, 0, ready=(y_lo, 8) if isinstance(t, int) and t == 0 else None).then_inc(w_used, 1)
            mix_tile(0, 0)
            mix_tile(1, 1)
            norm_sum(pe, 1)
            with pe.Fori(1, SLOTS["mix"][1] // 2) as i:
                mix_tile(2 * i, 0)
                mix_tile(2 * i + 1, 1)

            pe.wait_ge(acc_free2, 7)
            pe.wait_ge(nlo, 16)
            for n in range(2):
                for s in range(4):
                    pe.wait_ge(w_split, SLOTS["xkv"][0] + 4 * n + s + 1)
                    p = s % 2
                    for kk in range(2):
                        k = 2 * s + kk
                        for m in range(2):
                            for j, (x_, w_) in enumerate(((MH, WH), (ML, WH), (MH, WL))):
                                mm = nc.tensor.matmul(PS[:, 2 * n + m, :], x_[:, k, CH * m:CH * m + CH],
                                                      w_[:, p, 512 * kk:512 * kk + 512],
                                                      start=(k == 0 and j == 0), stop=(k == KT - 1 and j == 2))
                    mm.then_inc(w_used, 1)
                if n == 0:
                    norm_sum(pe, 2)
                    pe.wait_ge(nln, 3)
            pe.wait_ge(kv_sb, 2)
            for m in range(2):
                for h in range(NH):
                    mm = nc.tensor.transpose(PS[:, 6 + m, P * h:P * h + P], m_k[:, m, P * h:P * h + P], ident)
            mm.then_inc(mkt_ps, 1)
            pe.wait_ge(kv_sb, 4)
            simple("xq", hq_ok, (nlo, 16))

            def xattn_front(c, p):
                pe.wait_ge(xa_st, c + 1)
                if isinstance(c, int) and c == 0:
                    pe.wait_ge(hq_ok, 4)
                wait(pe, xa_exp, 4 * (c - 1))
                for h in range(NH):
                    mm = nc.tensor.matmul(x_ps(h, p), x_q[:, p, h, :], m_kT[:, h, :], start=True, stop=True)
                    if h % 2:
                        mm.then_inc(xa_sc, 1)

            def xattn_back(c, p, left):
                if left:
                    xattn_front(c + 1, 1 - p)
                pe.wait_ge(xa_p, c + 1)
                wait(pe, xa_pt, 2 * c)
                for i in range(2):
                    for h in range(NH):
                        mm = nc.tensor.transpose(PS[:, 2 + i, CH * h:CH * h + CH], x_s[:, p, h, CH * i:CH * i + CH], ident)
                    mm.then_inc(xa_tp, 1)
                pe.wait_ge(xa_pt, 2 * c + 2)
                wait(pe, xa_lo, c)
                for h in range(NH):
                    for i in range(2):
                        mm = nc.tensor.matmul(PS[:, 4, CH * h:CH * h + CH], m_v[:, i, P * h:P * h + P], x_pt[:, i, h, :],
                                              start=(i == 0), stop=(i == 1))
                mm.then_inc(xa_pv, 1)
            pipelined(pe, NBLK, xattn_front, xattn_back)
            pe.wait_ge(xa_lo, NBLK)
            pe.wait_ge(xk_in, 64)
            for h in range(NH):
                for q in range(4):
                    mm = nc.tensor.matmul(PS[TS * h:TS * h + TS, q, :], HQ[:, h, TP:T], kc_buf[h][:, 512 * q:512 * q + 512],
                                          start=True, stop=True)
                mm.then_inc(xs_sc, 1)
            pe.wait_ge(xs_dv, 5)
            for q in range(4):
                wait(pe, xs_ptok, q - 1)
                for i in range(4):
                    k = 4 * q + i
                    mm = nc.tensor.transpose(PS[:, 4 + q % 2, CH * i:CH * i + CH], xs_s[:, CH * k:CH * k + CH], ident)
                mm.then_inc(xs_tp, 1)
            pe.wait_ge(xs_ptok, 4)
            pe.wait_ge(xv_in, 64)
            for h in range(NH):
                v = vc_buf[h].rearrange("p (m n) -> p m n", n=P)
                for k in range(2 * NB):
                    o = TS * h + LS * (k // 2)
                    mm = nc.tensor.matmul(PS[:, 6, o:o + LS], v[:, k, :], xs_pt[:, k, o:o + LS],
                                          start=(k % 2 == 0), stop=(k % 2 == 1))
            mm.then_inc(xs_pv, 1)

            pe.wait_ge(xa_lo, NBLK + 1)
            for s in range(4):
                pe.wait_ge(w_split, SLOTS["xo"][0] + s + 1)
                wait(pe, xo_free, 2 * s - 1)
                gemm_tile(0, s % 2, 0, 4, 0).then_inc(xo_a, 1)
                wait(pe, xo_free, 2 * s)
                gemm_tile(1, s % 2, 0, 4, 4 * P).then_inc(w_used, 1)

            norm_sum(pe, 3)

            def down(f, n0, last=False):
                pe.wait_ge(f_lo, 2 * f + 2)
                for m in range(KT):
                    if m % 4 == 0:
                        pe.wait_ge(w_split, n0 + m // 4 + 1)
                    if m < 2:
                        pe.wait_ge(f_gate, 2 * f + 2 if last else 2 * f + 3 + m)
                    pe.wait_ge(fd_free, 8 * f + (m + 1 if m >= 2 else 2))
                    p = m // 4
                    for k in range(2):
                        for w_, x_ in ((WH, AH), (WH, AL), (WL, AH)):
                            for c in range(NCH):
                                mm = nc.tensor.matmul(PS[:, 3 * (m % 2) + c, 0:CW],
                                                      w_[:, p, (m % 4) * 256 + k * P:(m % 4) * 256 + k * P + P],
                                                      x_[:, k, bass.ts(c, CW)], start=(k == 0 and w_ is WH and x_ is AH),
                                                      stop=(k == 1 and w_ is WL))
                    mm.then_inc(w_used if m % 4 == 3 else f_down, 1)

            def mlp_pe(f):
                first = isinstance(f, int) and f == 0
                for j in range(4):
                    pe.wait_ge(w_split, FFN0(f) + j + 1)
                    if j < 2:
                        if not first:
                            pe.wait_ge(fd_free, 8 * (f - 1) + 1 + j)
                            pe.wait_ge(f_gate, 2 * f - 1 + j)
                    else:
                        pe.wait_ge(fu_free, 2 * f + j - 1)
                    gemm_tile(j % 2, j % 2, 0, KT, 0, ready=(nlo, 24) if first and j == 0 else None).then_inc(w_used, 1)
                if not first:
                    down(f - 1, FFN0(f) + 4)
            mlp_pe(0)
            with pe.Fori(1, FT // 2) as f:
                mlp_pe(f)
            down(FT // 2 - 1, NSLOTS - 2, last=True)
            norm_sum(pe, 4)

        @block.vector
        def _(dve):
            dve.wait_ge(const_in, 16)
            w_ab = CST[:, CONST["w_ab"][0]:CONST["w_ab"][0] + NAB]
            nc.vector.tensor_copy(WABH, w_ab).then_inc(ab_w, 1)
            dve.wait_ge(ab_w, 1)
            nc.vector.tensor_tensor(WABL, w_ab, WABH.bitcast(F32), ALU.subtract).then_inc(ab_w, 1)
            for k in range(1, KT):
                norm_add(dve, 0, k, T)
            norm_dve(dve, 0, H, cst("g_mix"), XH, XL, T)
            dve.wait_ge(rope_in, 48)

            def rotate(n, x, sx, swapped, cos, sin):
                dve.wait_ge(rot_ps, n)
                wait(dve, rot_x, n - 1)
                nc.vector.tensor_tensor(sx, swapped, sin, ALU.mult).then_inc(rot_t, 1)
                nc.vector.tensor_tensor(x, x, cos, ALU.mult).then_inc(rot_c, 1)
                dve.wait_ge(rot_t, n)
                dve.wait_ge(rot_c, n)
                nc.vector.tensor_tensor(x, x, sx, ALU.add).then_inc(rot_x, 1)
            two = lambda ap: ap.rearrange("p (b n) -> p b n", b=2)
            for t in range(5):
                rotate(t + 1, two(H[:, t, 0:TP]), two(r_sin), PS[:, 6:8, :], two(rope[:, 0, 0:TP]), two(rope[:, 1, 0:TP]))
                if t == 0:
                    nc.vector.memset(a_q, 0.0).then_inc(at_zero, 1)
                    nc.vector.memset(a_v[:, 1, :], 0.0).then_inc(at_zero, 1)
                    nc.vector.memset(a_s[0][:, :, 0:CH], NEG).then_inc(at_zero, 1)
            five = lambda ap: ap.unsqueeze(1).to_broadcast([P, 5, TS])
            rotate(6, H[:, 0:5, TP:T], r_sins, PS[:, 6, 0:5 * TS].rearrange("p (t n) -> p t n", t=5), five(rope[:, 0, TP:T]),
                   five(rope[:, 1, TP:T]))
            dve.wait_ge(rot_x, 6)
            nc.vector.memset(a_s[1][:, :, 0:CH], NEG).then_inc(at_zero, 1)
            dve.wait_ge(at_zero, 4)
            scale = float(HD) ** -0.5

            def row_max(mx, nm, es, sinks, s, done, n0):
                nc.vector.reduce_max(mx, s, AX.X).then_inc(done, 1)
                dve.wait_ge(done, n0 + 1)
                nc.vector.tensor_tensor(nm, mx, sinks, ALU.max).then_inc(done, 1)
                dve.wait_ge(done, n0 + 2)
                nc.vector.tensor_tensor(es, sinks, nm, ALU.subtract).then_inc(done, 1)
                dve.wait_ge(done, n0 + 3)
                nc.vector.tensor_scalar(nm, nm, -1.0, None, ALU.mult).then_inc(done, 1)

            def row_divide(s, den_t, es, den, n0, probs):
                nc.vector.tensor_tensor(den_t, den_t, es, ALU.add).then_inc(den, 1)
                dve.wait_ge(den, n0 + 1)
                nc.vector.reciprocal(den_t, den_t).then_inc(den, 1)
                dve.wait_ge(den, n0 + 2)
                nc.vector.tensor_tensor(s, s, den_t.unsqueeze(2).to_broadcast(list(s.shape)), ALU.mult).then_inc(probs, 1)

            def swa_front(c, p):
                wait(dve, at_tp, 4 * (c - 1))
                for b in range(4):
                    dve.wait_ge(at_sc, 4 * c + b + 1)
                    ps = PS[:, b, :].rearrange("p (h n) -> p h n", h=2)
                    k0 = CH if isinstance(c, int) and c == 0 else 0
                    mask = a_mask[:, k0:2 * CH].unsqueeze(1).to_broadcast([P, 2, 2 * CH - k0])
                    nc.vector.scalar_tensor_tensor(a_s[p][:, 2 * b:2 * b + 2, k0:2 * CH], ps[:, :, k0:2 * CH], scale, mask,
                                                   ALU.mult, ALU.add).then_inc(at_msk, 1)
                dve.wait_ge(at_msk, 4 * c + 4)
                row_max(a_mx[:, p, :], a_nm[:, p, :], a_es[:, p, :], cst("sinks"), a_s[p], at_mx, 4 * c)

            def swa_back(c, p, left):
                dve.wait_ge(at_exp, 9 * c + 9)
                row_divide(a_s[p], a_den[:, p, :], a_es[:, p, :], at_den, 2 * c, at_p)
                if left:
                    swa_front(c + 1, 1 - p)
            pipelined(dve, NBLK, swa_front, swa_back)

            dve.wait_ge(smask_in, 16)
            dve.wait_ge(pwv_out, 1)
            for g in range(2):
                dve.wait_ge(ss_sc, g + 1)
                nc.vector.scalar_tensor_tensor(s_s[:, g, 0:TP].rearrange("p (b n) -> p b n", b=2), PS[:, 3 * g:3 * g + 2, :],
                                               scale, s_mask[:, 0:TP].rearrange("p (b n) -> p b n", b=2),
                                               ALU.mult, ALU.add).then_inc(ss_msk, 1)
                nc.vector.scalar_tensor_tensor(s_s[:, g, TP:T], PS[:, 3 * g + 2, 0:TS], scale, s_mask[:, TP:T],
                                               ALU.mult, ALU.add).then_inc(ss_msk, 1)
            dve.wait_ge(ss_msk, 4)
            row_max(s_mx, s_nm, s_es, cst("sinks_s"), s_s, ss_mx, 0)
            dve.wait_ge(ss_exp, 3)
            row_divide(s_s, s_den, s_es, ss_den, 0, ss_p)

            nc.vector.memset(SM, 0.0).then_inc(gt_dve, 1)
            n = [1]

            def g(i, after=None):
                i.then_inc(gt_dve, 1)
                n[0] += 1
                dve.wait_ge(gt_dve, n[0])
            bc4 = lambda ap: ap.unsqueeze(1).to_broadcast([P, 9, NH])
            dve.wait_ge(gt_act, 2)
            g(nc.vector.tensor_tensor(g_x, g_ab[:, :, 0:4], bc4(cst("dt_bias")), ALU.add))
            g(nc.vector.tensor_scalar(g_t, g_x, -1.0, None, ALU.mult))
            g(nc.vector.tensor_tensor(g_ax, g_x, g_t, ALU.max))
            g(nc.vector.tensor_scalar(g_x, g_x, 0.0, None, ALU.max))
            dve.wait_ge(gt_act, 6)
            g(nc.vector.tensor_tensor(g_x, g_x, g_l, ALU.add))
            g(nc.vector.tensor_tensor(g_g, g_x, bc4(g_ea), ALU.mult))
            g(nc.vector.tensor_scalar(g_g, g_g, -1.0, None, ALU.mult))
            g(nc.vector.tensor_scalar(g_eb, g_eb, 1.0, None, ALU.add))
            dve.wait_ge(dm_in, 32)
            g(nc.vector.tensor_tensor(g_bm[0:TS], g_g[0:TS, NBLK, :].unsqueeze(1).to_broadcast([TS, NB, NH]),
                                      ms_b[0:TS, :].unsqueeze(2).to_broadcast([TS, NB, NH]), ALU.mult))
            assert n[0] == 10

            nc.vector.memset(b_s, 0.0).then_inc(s_zero, 1)

            dve.wait_ge(ss_pv, 1)
            dve.wait_ge(out_done, n_attn)
            for p in range(2):
                nc.vector.memset(c_pre[:, p, 0:3], 0.0).then_inc(c_his, 1)
            dve.wait_ge(dn_in, 16)

            def conv(t, p):
                x = c_pre[:, p, :]
                xs = x[:, 3 + TP:PRE].rearrange("p (b n) -> p b n", b=NB)
                y = c_acc[:, p, :]
                ys = y[:, TP:T].rearrange("p (b n) -> p b n", b=NB)
                wait(dve, c_cv, 8 * (t - 1))
                nc.vector.tensor_copy(xs[:, :, 0:3], c_hist[:, t, :, :]).then_inc(c_his, 1)
                dve.wait_ge(c_pre_ok, 4 * t + 4)
                dve.wait_ge(acc_free, acc0["dn"] + t + 1)
                dve.wait_ge(c_his, t + 3)
                wait(dve, c_act, t - 1)
                for j in range(4):
                    w_ = CST[:, bass.ds(CONST["dn_w"][0] + 4 * t + j, 1)]
                    if j == 0:
                        nc.vector.tensor_scalar(y[:, 0:TP], x[:, 0:TP], w_, None, ALU.mult).then_inc(c_cv, 1)
                        nc.vector.tensor_scalar(ys, xs[:, :, 0:4], w_, None, ALU.mult).then_inc(c_cv, 1)
                    else:
                        dve.wait_ge(c_cv, 8 * t + 2 * j - 1)
                        nc.vector.scalar_tensor_tensor(y[:, 0:TP], x[:, j:j + TP], w_, y[:, 0:TP], ALU.mult, ALU.add).then_inc(c_cv, 1)
                        dve.wait_ge(c_cv, 8 * t + 2 * j)
                        nc.vector.scalar_tensor_tensor(ys, xs[:, :, j:j + 4], w_, ys, ALU.mult, ALU.add).then_inc(c_cv, 1)
            def square(t, sq, x):
                dve.wait_ge(c_act, t + 1 if not (isinstance(t, int) and t == 8) else 8)
                nc.vector.tensor_tensor(sq, x, x, ALU.mult).then_inc(l_sq_ok, 1)

            def tile_square(j, p):
                wait(dve, l_ok, j - 1)
                square(j, l_sq[p], H[:, j, 0:TP])

            def tile_scale(j, p):
                dve.wait_ge(l_iv, j + 1)
                nc.vector.scalar_tensor_tensor(H[:, j, 0:TP], H[:, j, 0:TP], CST[:, bass.ds(CONST["l2_gain"][0] + j, 1)],
                                               l_sq[p], ALU.mult, ALU.mult).then_inc(l_ok, 1)
            conv(0, 0)
            conv(1, 1)
            dve.wait_ge(gt_act, 12)
            for c0, c1, rows in ((0, NBLK, P), (NBLK, 9, TS)):
                i = nc.vector.tensor_tensor(g_kds[0:rows, c0:c1, :], g_gl[0:rows, c0:c1, :], g_c[0:rows, c0:c1, :], ALU.subtract)
                if c0 == 0:
                    i.then_inc(gt_dve2, 1)
            i.then_inc(gt_dve, 1)
            n[0] += 1
            nc.vector.reciprocal(g_beta, g_eb).then_inc(gt_dve, 1)
            n[0] += 1
            dve.wait_ge(gt_act, 14)
            dve.wait_ge(gt_dve, n[0])
            nc.vector.tensor_tensor(g_be, g_beta, g_ec, ALU.mult).then_inc(gt_dve, 1)
            n[0] += 1
            dve.wait_ge(gt_dve, n[0])
            conv(2, 0)
            tile_square(0, 0)
            conv(3, 1)

            def conv_pair(i):
                tile_square(2 * i - 3, 1)
                conv(2 * i, 0)
                tile_scale(2 * i - 4, 0)
                tile_square(2 * i - 2, 0)
                conv(2 * i + 1, 1)
                tile_scale(2 * i - 3, 1)
            conv_pair(2)
            with dve.Fori(3, 5) as i:
                conv_pair(i)
            tile_square(7, 1)
            conv(10, 0)
            tile_scale(6, 0)
            square(8, l_sqs, H[:, :, TP:T])
            conv(11, 1)
            tile_scale(7, 1)
            dve.wait_ge(l_iv, 9)
            for h0, gain in ((0, float(P) ** -0.5), (NH, 1.0)):
                x = H[:, h0:h0 + NH, TP:T]
                nc.vector.scalar_tensor_tensor(x, x, gain, l_sqs[:, h0:h0 + NH, :], ALU.mult, ALU.mult).then_inc(l_ok, 1)

            def rows_norm(i0, n, rs, gain):
                for t in range(n):
                    dve.wait_ge(l_iv, i0 + t + 1)
                    if gain is None:
                        i = nc.vector.tensor_tensor(H[:, t, :], H[:, t, :], rs[t], ALU.mult)
                    else:
                        i = nc.vector.scalar_tensor_tensor(H[:, t, :], H[:, t, :], gain, rs[t], ALU.mult, ALU.mult)
                    i.then_inc(l_ok, 1)
            def front(part, p, done, dv, pw, aw, rows, q, c, ut, mu, ml):
                r = slice(0, rows)
                hb = lambda ap: ap.unsqueeze(1).to_broadcast([rows, NH, rows])
                tb = lambda ap, w=rows: ap[r, c, :].unsqueeze(2).to_broadcast([rows, NH, w])
                ps = lambda bank, w=rows: PS[r, bank, 0:NH * w].rearrange("p (h n) -> p h n", h=NH)
                kt = 3 if rows == P else 6
                ba, bqk = b_a[p][r, :, r], b_qk[p][r, :, r]
                if part == "gu":
                    done(nc.vector.tensor_tensor(b_kbe[p][r, :, r], hb(ut), tb(g_g), ALU.mult))
                elif part == "t":
                    pw("bc")
                    done(nc.vector.tensor_tensor(ba, ps(0), tb(g_c), ALU.subtract))
                    dv("t1")
                    done(nc.vector.tensor_tensor(bqk, ba, hb(mu), ALU.add))
                    dv("t2")
                    done(nc.vector.tensor_tensor(ba, hb(ml), ba, ALU.subtract))
                elif part == "a":
                    pw("kk")
                    aw("dd")
                    done(nc.vector.tensor_tensor(ba, ps(1), ba, ALU.mult))
                    dv("a1")
                    done(nc.vector.tensor_tensor(ba, ba, tb(g_beta), ALU.mult))
                elif part == "q":
                    pw("kq")
                    done(nc.vector.tensor_tensor(bqk, ps(2), bqk, ALU.mult))
                    done(nc.vector.tensor_tensor(b_qd[p][:, :, r], q, b_qd[p][:, :, r], ALU.mult))
                elif part == "k":
                    pw("kt")
                    done(nc.vector.tensor_tensor(b_kbe[p][r, :, :], ps(kt, w=P), tb(g_be, P), ALU.mult))
                    done(nc.vector.tensor_tensor(b_kd[p][r, :, :], ps(kt, w=P), tb(g_kds, P), ALU.mult))
                elif part == "v":
                    pw("vt")
                    done(nc.vector.tensor_tensor(b_vb[p][r, :, :], ps(0, w=P), tb(g_beta, P), ALU.mult))

            def invert(levels, rows, p, done, dv, pw, side):
                r = slice(0, rows)
                hb = lambda ap: ap.unsqueeze(1).to_broadcast([rows, NH, rows])
                bp, ba, by, bx = (b[r, :, r] for b in (b_p, b_a[p], b_y[p], b_x))
                halves = [(n, slice(2 * i, 2 * i + 2), (HALF_BANKS if rows == P else SHALF_BANKS)[i]) for i, n in enumerate("ab")]
                h2 = lambda ap: ap.unsqueeze(1).to_broadcast([rows, 2, rows])
                p2 = lambda bank: PS[r, bank, 0:2 * rows].rearrange("p (h n) -> p h n", h=2)
                dv("a2")
                done(nc.vector.tensor_tensor(bx, ba, hb(m_1l[r, r]), ALU.mult))
                dv("x1a")
                done(nc.vector.tensor_tensor(bx, hb(ident[r, r]), bx, ALU.subtract))
                for n, hh, (b0, b1) in halves:
                    pw("u1" + n)
                    done(nc.vector.tensor_tensor(bp[:, hh, :], p2(b0), h2(m_lev[r, 0, r]), ALU.mult))
                for n, hh, (b0, b1) in halves:
                    dv("p1" + n)
                    done(nc.vector.tensor_tensor(by[:, hh, :], h2(ident[r, r]), bp[:, hh, :], ALU.subtract))
                for l in range(2, levels + 1):
                    for n, hh, (b0, b1) in halves:
                        pw(f"lp{l}{n}")
                        dv(f"y{l - 1}{n}")
                        done(nc.vector.tensor_tensor(bp[:, hh, :], p2(b0), h2(m_lev[r, l - 1, r]), ALU.mult))
                    side(l)
                    for n, hh, (b0, b1) in halves:
                        pw(f"lz{l}{n}")
                        done(nc.vector.tensor_tensor(by[:, hh, :], by[:, hh, :], p2(b0), ALU.subtract))
                        if l < levels:
                            pw(f"lx{l}{n}")
                            done(nc.vector.tensor_tensor(bx[:, hh, :], bx[:, hh, :], p2(b1), ALU.subtract))

            def dv(name, c): delta_wait(dve, "dve", name, c)
            def pw(name, c): delta_wait(dve, "pe", name, c)
            def aw(name, c): delta_wait(dve, "act", name, c)

            def prompt_front(part, c, p):
                front(part, p, lambda i: i.then_inc(delta_sem["front", "dve"], 1), lambda name: dv(name, c),
                      lambda name: pw(name, c), lambda name: aw(name, c), P, H[:, 0:4, bass.ts(c, CH)], c,
                      m_ut[:, :], m_u[:, :], m_l[:, :])

            def state(c):
                def done(i): i.then_inc(delta_sem["state", "dve"], 1)
                pw("su", c)
                done(nc.vector.tensor_tensor(b_s, b_s, g_egl[:, c, :].unsqueeze(2).to_broadcast([P, NH, P]), ALU.mult))
                dv("s1", c)
                done(nc.vector.tensor_tensor(b_s, b_s, PS[:, 3, :].rearrange("p (h n) -> p h n", h=NH), ALU.add))

            def delta(c, p, before, after):
                def side(l):
                    if after and l == 2:
                        if before:
                            pw("wt", c - 1)
                        prompt_front("gu", c + 1, 1 - p)
                    if after and l == 4:
                        if before:
                            pw("o", c - 1)
                        prompt_front("t", c + 1, 1 - p)
                    if before and l == 5:
                        state(c - 1)
                    if after and l == 6:
                        prompt_front("a", c + 1, 1 - p)
                        prompt_front("q", c + 1, 1 - p)
                    if after and l == 7:
                        prompt_front("k", c + 1, 1 - p)
                invert(LEVELS, P, p, lambda i: i.then_inc(delta_sem["inverse", "dve"], 1), lambda name: dv(name, c),
                       lambda name: pw(name, c), side)
                if after:
                    prompt_front("v", c + 1, 1 - p)
            dve.wait_ge(c_cv, 96)
            dve.wait_ge(c_act, 12)
            for part in ("gu", "t", "a", "q", "k", "v"):
                prompt_front(part, 0, 0)
            delta_blocks(dve, delta)
            state(NBLK - 1)

            def sdone(i): i.then_inc(sd_dve, 1)
            def sdv(name): dve.wait_ge(sd_dve, at(SDVE_STEPS, name))
            def spw(name): dve.wait_ge(sd_pe, at(SPE_STEPS, name))
            def saw(name): dve.wait_ge(sd_act, at(SACT_STEPS, name))
            for part in ("gu", "t", "a", "q", "k", "v"):
                front(part, 0, sdone, sdv, spw, saw, TS, H[:, 0:4, TP:T], NBLK, ms_ut[0:TS, :], ms_u[0:TS, :], ms_l[0:TS, :])
            invert(2, TS, 0, sdone, sdv, spw, lambda l: None)
            dve.wait_ge(s0_in, 16)
            spw("o")
            saw("vn")
            for h in range(NH):
                vm = (s_vm0, s_vm1)[h % 2]
                if h >= 2:
                    spw(f"su{h - 2}")
                sdone(nc.vector.tensor_tensor(vm[0:TS, :].rearrange("p (b n) -> p b n", b=NB),
                                              b_x[0:TS, h, :].unsqueeze(1).to_broadcast([TS, NB, P]),
                                              ms_b[0:TS, :].unsqueeze(2).to_broadcast([TS, NB, P]), ALU.mult))
                s0 = S0[:, :, h, :]
                sdone(nc.vector.tensor_tensor(s0, s0, g_egs[:, :, h].unsqueeze(2).to_broadcast([P, NB, P]), ALU.mult))
                sdv(f"sa{h}")
                spw(f"su{h}")
                k = 6 * (h % 2)
                sdone(nc.vector.tensor_tensor(s0, s0, PS[:, k:k + 2, :].rearrange("p a (b n) -> p (a b) n", n=P), ALU.add))

            dve.wait_ge(sd_act, at(SACT_STEPS, "o"))
            for t in range(4):
                wait(dve, l_ps, 9 + t - 1 if t >= 2 else 0)
                nc.vector.tensor_tensor(o_sq[t], H[:, t, :], H[:, t, :], ALU.mult).then_inc(l_sq_ok, 1)
            rows_norm(9, 4, o_rs, cst("g_dn"))
            for t in range(4):
                dve.wait_ge(l_ok, 11 + t)
                dve.wait_ge(acc_free, acc0["dz"] + t + 1)
                nc.vector.tensor_tensor(H[:, t, :], H[:, t, :], z_sb[:, t, :], ALU.mult).then_inc(z_y, 1)

            def split_rests(src, base):
                for k in range(KT):
                    dve.wait_ge(y_hi, base + k + 1)
                    nc.vector.tensor_tensor(XL[:, k, :], src(k), XH[:, k, :].bitcast(F32), ALU.subtract).then_inc(y_lo, 1)
            split_rests(lambda k: YA[:, k, :] if k < 4 else H[:, k - 4, :], 0)
            dve.wait_ge(acc_free, acc0["gate"] + 16)
            for t in range(8):
                dve.wait_ge(br_a, t + 1)
                nc.vector.tensor_tensor(wide(ga(t)), wide(ga(t)), acc(0), ALU.mult).then_inc(br_m, 1)
                dve.wait_ge(w_used, SLOTS["branch"][0] + t + 1)
                nc.vector.tensor_tensor(wide(gb(t)), wide(gb(t)), acc(1), ALU.mult).then_inc(br_m, 1)
                dve.wait_ge(br_m, 2 * t + 2)
                nc.vector.tensor_tensor(ga(t), ga(t), gb(t), ALU.add).then_inc(br_s, 1)
            split_rests(ga, 8)
            dve.wait_ge(y_lo, 16)
            dve.wait_ge(xres_in, 16)

            def residual(t, p):
                dve.wait_ge(w_used, SLOTS["mix"][0] + t + 1)
                nc.vector.tensor_tensor(wide(H[:, t, :]), wide(x_res[:, t, :]), acc(p), ALU.add).then_inc(acc_free2, 1)
            for k in range(1, KT):
                norm_add(dve, 1, k, NM)
            residual(0, 0)
            residual(1, 1)
            norm_dve(dve, 1, m_x, cst("g_mem"), MH, ML, NM)
            for t in range(2, 8):
                residual(t, t % 2)
                if t >= 3:
                    norm_add(dve, 2, t - 2, T)
            norm_add(dve, 2, 6, T)
            norm_add(dve, 2, 7, T)
            norm_dve(dve, 2, H, cst("g_x"), XH, XL, T)
            xscale = float(P) ** -0.5

            def xattn_front(c, p):
                for b in range(2):
                    dve.wait_ge(xa_sc, 2 * c + b + 1)
                    nc.vector.reduce_max(x_nm[:, p, 0, 2 * b:2 * b + 2],
                                         PS[:, X_BANKS[p] + b, :].rearrange("p (h n) -> p h n", h=2), AX.X).then_inc(xa_mx, 1)
                dve.wait_ge(xa_mx, 4 * c + 2)
                nc.vector.tensor_scalar(x_nm[:, p, 1, :], x_nm[:, p, 0, :], -xscale, None, ALU.mult).then_inc(xa_mx, 2)

            def xattn_rest(c):
                dve.wait_ge(xa_hi, c + 1)
                cs = bass.ts(c, CH)
                nc.vector.tensor_tensor(XL[:, 0:4, cs], PS[:, 4, :].rearrange("p (h n) -> p h n", h=NH),
                                        XH[:, 0:4, cs].bitcast(F32), ALU.subtract).then_inc(xa_lo, 1)

            def xattn_back(c, p, left):
                dve.wait_ge(xa_exp, 4 * c + 4)
                nc.vector.reciprocal(x_den[:, p, 1, :], x_den[:, p, 0, :]).then_inc(xa_den, 1)
                dve.wait_ge(xa_den, c + 1)
                nc.vector.tensor_tensor(x_s[:, p, :, :], x_s[:, p, :, :],
                                        x_den[:, p, 1, :].unsqueeze(2).to_broadcast([P, NH, NM]), ALU.mult).then_inc(xa_p, 1)
                if not (isinstance(c, int) and c == 0):
                    xattn_rest(c - 1)
                if left:
                    xattn_front(c + 1, 1 - p)
            pipelined(dve, NBLK, xattn_front, xattn_back)
            xattn_rest(NBLK - 1)
            dve.wait_ge(xs_in, 16)
            dve.wait_ge(xs_sc, 4)
            nc.vector.tensor_tensor(xs_s.rearrange("p (q b n) -> p q b n", q=4, b=2),
                                    PS[:, 0:4, :].rearrange("p q (b n) -> p q b n", b=2),
                                    x_sm.rearrange("p (q b) -> p q b", q=4).unsqueeze(3).to_broadcast([P, 4, 2, NM]),
                                    ALU.add).then_inc(xs_dv, 1)
            dve.wait_ge(xs_dv, 1)
            nc.vector.reduce_max(x_nm[:, 0, 0, 0:1], xs_s, AX.X).then_inc(xs_dv, 1)
            dve.wait_ge(xs_dv, 2)
            nc.vector.tensor_scalar(x_nm[:, 0, 1, 0:1], x_nm[:, 0, 0, 0:1], -xscale, None, ALU.mult).then_inc(xs_dv, 1)
            dve.wait_ge(xs_exp, 1)
            nc.vector.reciprocal(x_den[:, 0, 1, 0:1], x_den[:, 0, 0, 0:1]).then_inc(xs_dv, 1)
            dve.wait_ge(xs_dv, 4)
            nc.vector.tensor_scalar(xs_s, xs_s, x_den[:, 0, 1, 0:1], None, ALU.mult).then_inc(xs_dv, 1)
            dve.wait_ge(xa_hi, NBLK + 1)
            nc.vector.tensor_tensor(XL[:, 0:4, TP:T], PS[:, 6, 0:P].rearrange("p (h n) -> p h n", h=NH),
                                    XH[:, 0:4, TP:T].bitcast(F32), ALU.subtract).then_inc(xa_lo, 1)

            for t in range(8):
                if t % 2 == 0:
                    dve.wait_ge(xo_a, t // 2 + 1)
                else:
                    dve.wait_ge(w_used, SLOTS["xo"][0] + t // 2 + 1)
                nc.vector.tensor_tensor(wide(H[:, t, :]), wide(H[:, t, :]), acc(t % 2), ALU.add).then_inc(xo_free, 1)
                if t >= 2:
                    norm_add(dve, 3, t - 1, T)
            norm_add(dve, 3, 7, T)
            norm_dve(dve, 3, H, cst("g_ffn"), XH, XL, T)

            dve.wait_ge(nlo, 32)
            nc.vector.memset(f_pre[:, :, 0:2], 0.0).then_inc(f_z, 1)
            nc.vector.memset(f_one, 1.0).then_inc(fd_free, 2)
            dve.wait_ge(f_in, 16)

            def mlp_conv(f, i):
                t = 2 * f + i
                x, y = f_pre[:, i, :], f_act[:, i, :]
                xs = x[:, 2 + TP:FPRE].rearrange("p (b n) -> p b n", b=NB)
                ys = y[:, TP:T].rearrange("p (b n) -> p b n", b=NB)
                wait(dve, f_cv, 6 * t - 6)
                nc.vector.tensor_copy(xs[:, :, 0:2], f_hist[:, t, :, :]).then_inc(f_his, 1)
                dve.wait_ge(fp_ok, 4 * t + 4)
                dve.wait_ge(fu_free, t + 1)
                dve.wait_ge(f_his, t + 1)
                wait(dve, f_lo, t - 1)
                for j in range(3):
                    w_ = CST[:, bass.ds(CONST["ffn_w"][0] + 3 * t + j, 1)]
                    if j == 0:
                        nc.vector.tensor_scalar(y[:, 0:TP], x[:, 0:TP], w_, None, ALU.mult).then_inc(f_cv, 1)
                        nc.vector.tensor_scalar(ys, xs[:, :, 0:4], w_, None, ALU.mult).then_inc(f_cv, 1)
                    else:
                        dve.wait_ge(f_cv, 6 * t + 2 * j - 1)
                        nc.vector.scalar_tensor_tensor(y[:, 0:TP], x[:, j:j + TP], w_, y[:, 0:TP], ALU.mult, ALU.add).then_inc(f_cv, 1)
                        dve.wait_ge(f_cv, 6 * t + 2 * j)
                        nc.vector.scalar_tensor_tensor(ys, xs[:, :, j:j + 4], w_, ys, ALU.mult, ALU.add).then_inc(f_cv, 1)

            def mlp_down(f, n0, last=False):
                for m in range(KT):
                    if m % 4 == 3:
                        dve.wait_ge(w_used, n0 + m // 4 + 1)
                    else:
                        dve.wait_ge(f_down, 6 * f + m - m // 4 + 1)
                    dve.wait_ge(fd_free, 8 * f + 2)
                    nc.vector.tensor_tensor(wide(H[:, m, :]), wide(H[:, m, :]), acc(m % 2), ALU.add).then_inc(fd_free, 1)
                    if last and m >= 2:
                        norm_add(dve, 4, m - 1, T)

            def mlp_dve(f):
                for i in range(2):
                    mlp_conv(f, i)
                for i in range(2):
                    dve.wait_ge(w_used, FFN0(f) + 2 + i + 1)
                    dve.wait_ge(f_silu, 2 * f + i + 1)
                    nc.vector.tensor_tensor(wide(f_act[:, i, :]), wide(f_act[:, i, :]), acc(i), ALU.mult).then_inc(f_gate, 1)
                if not (isinstance(f, int) and f == 0):
                    mlp_down(f - 1, FFN0(f) + 4)
                for i in range(2):
                    dve.wait_ge(f_hi, 2 * f + i + 1)
                    nc.vector.tensor_tensor(AL[:, i, :], f_act[:, i, :], AH[:, i, :].bitcast(F32), ALU.subtract).then_inc(f_lo, 1)
            mlp_dve(0)
            with dve.Fori(1, FT // 2) as f:
                mlp_dve(f)
            mlp_down(FT // 2 - 1, NSLOTS - 2, last=True)
            norm_add(dve, 4, 7, T)
            dve.wait_ge(nrs, 5)
            for k in range(KT):
                nc.vector.scalar_tensor_tensor(H[:, k, :], H[:, k, :], cst("g_out")[:, k:k + 1], norm_space(4)[2],
                                               ALU.mult, ALU.mult).then_inc(y_fin, 1)


def layouts(inputs):
    import numpy as np
    f = {k: np.asarray(v) for k, v in inputs.items()}
    A = np.ascontiguousarray
    gk = lambda g: g.reshape(-1, P).T
    o = {}
    x = np.concatenate([f["x_prompt"][0], f["x_sample"].reshape(TS, D)], 0)
    o["xT"] = A(x.T.reshape(KT, P, T))
    w_in = f["w_in"][0]
    out_tile = lambda w: w.reshape(KT, P, -1, P).transpose(2, 1, 0, 3).reshape(-1, P, SLOT)
    qcols = np.concatenate([np.r_[64 * j:64 * j + 64, 64 * (j + 4):64 * (j + 4) + 64] for j in range(NJ)])
    st = [out_tile(w_in[:, qcols]), out_tile(w_in[:, 512:768]), out_tile(w_in[:, 768:768 + 1536]),
          out_tile(w_in[:, 2304:2816]), out_tile(w_in[:, 2824:4872])]
    bra = f["w_br_a"][0][qcols].reshape(4, P, 8, P)
    brb = f["w_br_b"][0].reshape(4, P, 8, P)
    st.append(np.concatenate([bra, brb], 0).transpose(2, 1, 0, 3).reshape(8, P, SLOT))
    st.append(out_tile(f["w_mix_out"][0]))
    st.append(f["w_xkv"][0].reshape(4, 2, P, 2, 512).transpose(3, 0, 2, 1, 4).reshape(8, P, SLOT))
    st.append(out_tile(f["w_xq"][0]))
    st.append(f["w_xo"][0].reshape(4, P, 4, 2, P).transpose(2, 1, 3, 0, 4).reshape(4, P, SLOT))
    up = out_tile(f["w_up"][0]).reshape(2, FT // 2, 2, P, SLOT).transpose(1, 0, 2, 3, 4).reshape(FT // 2, 4, P, SLOT)
    dn = f["w_down"][0].reshape(FT // 2, 2, P, 2, 4, P).transpose(0, 3, 2, 4, 1, 5).reshape(FT // 2, 2, P, SLOT)
    for g in range(FT // 2 + 1):
        st += [up[g]] if g < FT // 2 else []
        st += [dn[g - 1]] if g > 0 else []
    o["w"] = A(np.concatenate(st, 0))
    assert o["w"].shape[0] == NSLOTS
    rep = lambda v: np.broadcast_to(v, (P, v.shape[-1]))
    sk = f["attn_sinks"][0]
    parts = {"ident": np.eye(P), "ones": np.ones((P, P)), "g_mix": gk(f["norm_mix_g"][0]), "g_mem": gk(f["norm_mem_g"][0]),
             "g_x": gk(f["norm_x_g"][0]), "g_ffn": gk(f["norm_ffn_g"][0]), "g_out": gk(f["final_norm_g"]),
             "g_dn": f["dn_norm_g"][0][:, None], "sinks": rep(sk), "sinks_s": np.stack([np.repeat(sk[:4], 32), np.repeat(sk[4:], 32)], 1),
             "a_log": rep(f["dn_a_log"][0]), "dt_bias": rep(f["dn_dt_bias"][0]),
             "dn_w": f["dn_conv_w"][0].reshape(4, 12, P).transpose(2, 1, 0).reshape(P, 48),
             "ffn_w": f["ffn_conv_w"][0].reshape(3, FT, P).transpose(2, 1, 0).reshape(P, FT * 3),
             "eps": np.full((P, 1), EPS), "l2_gain": np.tile(np.repeat([float(P) ** -0.5, 1.0], NH), (P, 1)),
             "w_ab": w_in[:, 2816:2824].reshape(KT, P, 8).transpose(1, 0, 2).reshape(P, 64)}
    o["cst"] = A(np.concatenate([parts[k].astype(np.float32) for k in CONST], 1))
    assert o["cst"].shape[1] == NCONST
    pos = np.concatenate([np.arange(TP), np.tile(8192 + np.arange(LS), NB)]).astype(np.float32)
    inv = np.float32(500000.0) ** (np.float32(-2.0) * np.arange(8, dtype=np.float32) / np.float32(16))
    ang = pos[None, :] * inv.astype(np.float32)[:, None]
    cs, sn = np.ones((P, T), np.float32), np.zeros((P, T), np.float32)
    for g in range(2):
        for half in range(2):
            r = 64 * g + 8 * half
            cs[r:r + 8], sn[r:r + 8] = np.cos(ang), np.sin(ang)
    o["rope"] = A(np.stack([cs, sn], 1))
    pm = np.zeros((P, P), np.float32)
    for g in range(2):
        for i in range(8):
            pm[64 * g + 8 + i, 64 * g + i] = -1.0
            pm[64 * g + i, 64 * g + 8 + i] = 1.0
    o["perm"] = pm
    q, k = np.arange(CH)[:, None], np.arange(CH)[None]
    o["swa_mask"] = A(np.where(np.concatenate([k > q, k <= q], 1), 0.0, NEG).astype(np.float32))
    tok = np.tile(np.arange(TS), NJ)
    tb, tt = (tok // LS)[:, None], (tok % LS)[:, None]
    kb, ks = np.arange(TP)[None] // CH, np.arange(TP)[None] % CH
    nb_, nt = np.arange(TS)[None] // LS, np.arange(TS)[None] % LS
    o["swas_mask"] = A(np.where(np.concatenate([(kb == tb) & (ks > tt), (nb_ == tb) & (nt <= tt)], 1), 0.0, NEG).astype(np.float32))
    o["kcT"] = A(f["cache_win_k"][0].reshape(NB, CH, P).transpose(2, 0, 1))
    o["cwk"] = A(f["cache_win_k"][0].reshape(NB, CH, P))
    o["cwv"] = A(f["cache_win_v"][0].reshape(NB, CH, P))
    o["dn_hist"] = A(f["state_dn_conv"][0].reshape(NB, 3, 12, P).transpose(3, 2, 0, 1))
    o["ffn_hist"] = A(f["state_ffn_conv"][0].reshape(NB, 2, FT, P).transpose(3, 2, 0, 1))
    o["memT"] = A(f["mem_prompt"][0].T.reshape(KT, P, NM))
    o["mkT"] = A(f["cache_mem_k"][0].transpose(2, 3, 0, 1).reshape(NH, P, NB * NM))
    o["mv"] = A(f["cache_mem_v"][0].reshape(NB, 2, P, NH, P).transpose(3, 2, 0, 1, 4).reshape(NH, P, 2 * NB, P))
    rb = (np.arange(P) % TS) // LS
    o["xs_mask"] = np.where(rb[:, None] == np.arange(NB)[None], 0.0, NEG).astype(np.float32)
    o["s0"] = A(f["state_dn"][0])
    a_, b_ = np.arange(P)[:, None], np.arange(P)[None]
    lev = [((a_ >> l) == (b_ >> l)) & ((a_ >> (l - 1)) < (b_ >> (l - 1))) for l in range(1, LEVELS + 1)]
    o["d_mask"] = A(np.stack([(a_ <= b_) * 1.0, np.where(a_ <= b_, 0.0, NEG), np.where(b_ < a_, 0.0, NEG), lev[0].T * 1.0]
                             + [m * 1.0 for m in lev], 1).astype(np.float32))
    same = (a_ // LS) == (b_ // LS)
    sm = np.zeros((P, 6 * TS + NB), np.float32)
    for i, m in enumerate((same & (a_ <= b_), np.where(same & (a_ <= b_), 0.0, NEG), np.where(same & (b_ < a_), 0.0, NEG), same)):
        sm[:TS, TS * i:TS * i + TS] = m[:TS, :TS]
    sm[:TS, 6 * TS:] = (np.arange(TS)[:, None] // LS) == np.arange(NB)[None]
    o["ds_mask"] = sm
    return o


OUTS = {"yT": (KT, P, T), "p_mem_k": (NM, 512), "p_mem_v": (NM, 512), "ffn_tail": (P, FT, 18), "dn_tail": (P, 12, 27), "p_dn_state": (NH, P, P), "s_dn_state": (NB, NH, P, P), "p_win_k": (CH, P), "p_win_v": (CH, P), "s_win_k": (NB, CH, P), "s_win_v": (NB, CH, P)}


def kernel(**inputs):
    import numpy as np
    import concourse.bacc as bacc
    from concourse.bass_utils import run_bass_kernel_spmd

    nc = bacc.Bacc("TRN2", target_bir_lowering=False, num_devices=1)
    arrays, d = {}, {}
    for name, a in layouts(inputs).items():
        arrays["in_" + name] = a
        d[name] = nc.dram_tensor("in_" + name, a.shape, F32, kind="ExternalInput").ap()
    for name, shape in OUTS.items():
        d[name] = nc.dram_tensor("out_" + name, shape, F32, kind="ExternalOutput").ap()
    build(nc, d)
    r = run_bass_kernel_spmd(nc, [arrays], core_ids=[0]).results[0]
    o = {name: r["out_" + name] for name in OUTS}
    y = o["yT"].reshape(D, T).T
    dn, fn = o["dn_tail"], o["ffn_tail"]
    A = np.ascontiguousarray
    return (A(y[None, :TP]), A(y[TP:].reshape(NB, LS, D)),
            o["p_win_k"].reshape(1, 1, CH, 2, HD), o["p_win_v"].reshape(1, 1, CH, 2, HD),
            A(dn[:, :, 0:3].transpose(2, 1, 0).reshape(1, 1, 3, 12 * P)), o["p_dn_state"].reshape(1, 1, NH, P, P),
            o["p_mem_k"].reshape(1, 1, NM, NH, P), o["p_mem_v"].reshape(1, 1, NM, NH, P),
            A(fn[:, :, 0:2].transpose(2, 1, 0).reshape(1, 1, 2, FT * P)),
            o["s_win_k"].reshape(1, NB, CH, 2, HD), o["s_win_v"].reshape(1, NB, CH, 2, HD),
            A(dn[:, :, 3:].reshape(P, 12, NB, 3).transpose(2, 3, 1, 0).reshape(1, NB, 3, 12 * P)),
            o["s_dn_state"].reshape(1, NB, NH, P, P),
            A(fn[:, :, 2:].reshape(P, FT, NB, 2).transpose(2, 3, 1, 0).reshape(1, NB, 2, FT * P)))
```
